# Optimizing a Trainium2 kernel written in Bass

```python
import jax
import jax.numpy as jnp
from jax import lax
import numpy as np
import math
import jax, jax.numpy as jnp

D_MODEL = 1024
BATCH = 1
SEQ = 256
DEPTH = 2

POOL_WINDOWS = (2, 4, 8, 16)
N_POOL_GROUPS = len(POOL_WINDOWS)
POOL_WIDTH = D_MODEL // 2
POOL_GROUP = POOL_WIDTH // N_POOL_GROUPS
RET_HEADS = 4
RET_QK_DIM = 64
RET_V_DIM = 128
RET_WIDTH = RET_HEADS * RET_V_DIM
RET_CHUNK = 128
ROPE_BASE = 10000.0
AB_SPLITS = (POOL_WIDTH,
             POOL_WIDTH + RET_HEADS * RET_QK_DIM,
             POOL_WIDTH + 2 * RET_HEADS * RET_QK_DIM,
             POOL_WIDTH + 2 * RET_HEADS * RET_QK_DIM + RET_WIDTH)
AB_IN = POOL_WIDTH + 2 * RET_HEADS * RET_QK_DIM + 2 * RET_WIDTH
AB_OUT_IN = POOL_WIDTH + RET_WIDTH
HGRN_HEADS = 8
HGRN_EXPAND = 128
HGRN_FDIM = HGRN_HEADS * HGRN_EXPAND
HGRN_V_DIM = D_MODEL // HGRN_HEADS
HGRN_CHUNK = 32
C_SPLITS = (HGRN_FDIM, 2 * HGRN_FDIM, 2 * HGRN_FDIM + D_MODEL)
C_IN = 2 * HGRN_FDIM + 2 * D_MODEL
PEER_HEADS = 8
PEER_NKEYS = 128
PEER_EXPERTS = PEER_NKEYS * PEER_NKEYS
PEER_KEY_DIM = 256
PEER_HALF = PEER_KEY_DIM // 2
PEER_TOPK = 16
PEER_BLOCK = 128
DN_ALPHA = (2 * DEPTH) ** 0.25
DN_BETA = (8 * DEPTH) ** -0.25
LN_EPS = 1e-5
N_EVEN = (DEPTH + 1) // 2
N_ODD = DEPTH // 2


def layer_norm(x, g, b):
    xf = x.astype(jnp.float32)
    mu = xf.mean(-1, keepdims=True)
    var = jnp.square(xf - mu).mean(-1, keepdims=True)
    return ((xf - mu) * lax.rsqrt(var + LN_EPS) * g + b).astype(x.dtype)

def head_layernorm(o, g):
    B_, S_, H, d = o.shape
    mu = o.mean(-1, keepdims=True)
    var = jnp.square(o - mu).mean(-1, keepdims=True)
    return ((o - mu) * lax.rsqrt(var + LN_EPS)).reshape(B_, S_, H * d) * g

def head_rmsnorm(o, g):
    B_, S_, H, d = o.shape
    y = o * lax.rsqrt(jnp.square(o).mean(-1, keepdims=True) + LN_EPS)
    return y.reshape(B_, S_, H * d) * g

def to_chunks(t, chunk, heads):
    B_, S_ = t.shape[0], t.shape[1]
    t = t.astype(jnp.float32).reshape(B_, S_ // chunk, chunk, heads, -1)
    return t.transpose(1, 0, 3, 2, 4)

def from_chunks(t):
    N, B_, H, C, d = t.shape
    return t.transpose(1, 0, 3, 2, 4).reshape(B_, N * C, H, d)

def pool_mixer(u, pool_w, pool_scale):
    B_, S_, _ = u.shape
    ug = u.astype(jnp.float32).reshape(B_, S_, N_POOL_GROUPS, POOL_GROUP)
    count = jnp.arange(1, S_ + 1, dtype=jnp.float32)
    outs = []
    for gi, w in enumerate(POOL_WINDOWS):
        xg = ug[:, :, gi]
        cs = jnp.cumsum(xg, axis=1)
        lagged = jnp.pad(cs, ((0, 0), (w, 0), (0, 0)))[:, :S_]
        mean = (cs - lagged) / jnp.minimum(count, float(w))[None, :, None]
        outs.append(mean - xg)
    p = jnp.stack(outs, axis=2).astype(u.dtype)
    y = jnp.einsum('bsgc,gcd->bsgd', p, pool_w).reshape(B_, S_, POOL_WIDTH)
    return y * pool_scale

def rotary(x, pos):
    half = x.shape[-1] // 2
    inv = 1.0 / (ROPE_BASE ** jnp.linspace(0.0, 1.0, half, dtype=jnp.float32))
    ang = pos[:, None] * inv[None, :]
    cos = jnp.cos(ang)[None, :, None, :]
    sin = jnp.sin(ang)[None, :, None, :]
    xf = x.astype(jnp.float32)
    x1, x2 = xf[..., :half], xf[..., half:]
    return jnp.concatenate([x1 * cos - x2 * sin, x2 * cos + x1 * sin], axis=-1)

def retention(q, k, v):
    C = RET_CHUNK
    H = q.shape[2]
    log_gamma = jnp.log1p(-jnp.exp2(-5.0 - jnp.arange(H, dtype=jnp.float32)))
    idx = jnp.arange(C, dtype=jnp.float32)
    diff = idx[:, None] - idx[None, :]
    dmask = jnp.where(diff >= 0, jnp.exp(log_gamma[:, None, None] * jnp.maximum(diff, 0.0)), 0.0)
    q_decay = jnp.exp(log_gamma[:, None] * (idx[None, :] + 1.0))[None, :, :, None]
    k_decay = jnp.exp(log_gamma[:, None] * (C - 1.0 - idx[None, :]))[None, :, :, None]
    chunk_decay = jnp.exp(log_gamma * C)[None, :, None, None]
    qc, kc, vc = to_chunks(q, C, H), to_chunks(k, C, H), to_chunks(v, C, H)
    scores = jnp.einsum('nbhcd,nbhsd->nbhcs', qc, kc) * dmask
    intra = jnp.einsum('nbhcs,nbhse->nbhce', scores, vc)

    def step(state, inp):
        q_n, k_n, v_n = inp
        cross = jnp.einsum('bhcd,bhde->bhce', q_n, state) * q_decay
        state = state * chunk_decay + jnp.einsum('bhsd,bhse->bhde', k_n * k_decay, v_n)
        return state, cross

    state0 = jnp.zeros((q.shape[0], H, q.shape[3], v.shape[3]), jnp.float32)
    _, cross = lax.scan(step, state0, (qc, kc, vc))
    return from_chunks(intra + cross)

def hgrn2_chunkwise(q, k, v, logf):
    C, H = HGRN_CHUNK, HGRN_HEADS
    qc, kc, vc, lc = (to_chunks(t, C, H) for t in (q, k, v, logf))
    b = jnp.cumsum(lc, axis=3)
    b_last = b[:, :, :, -1:, :]
    q_in = qc * jnp.exp(b)
    k_in = kc * jnp.exp(-b)
    k_out = kc * jnp.exp(b_last - b)
    causal = jnp.tril(jnp.ones((C, C), dtype=bool))
    scores = jnp.where(causal, jnp.einsum('nbhcd,nbhsd->nbhcs', q_in, k_in), 0.0)
    intra = jnp.einsum('nbhcs,nbhse->nbhce', scores, vc)
    chunk_decay = jnp.exp(b_last[:, :, :, 0, :])

    def step(state, inp):
        q_n, k_n, v_n, d_n = inp
        cross = jnp.einsum('bhcd,bhde->bhce', q_n, state)
        state = state * d_n[..., None] + jnp.einsum('bhsd,bhse->bhde', k_n, v_n)
        return state, cross

    state0 = jnp.zeros((q.shape[0], H, HGRN_EXPAND, HGRN_V_DIM), jnp.float32)
    _, cross = lax.scan(step, state0, (q_in, k_out, vc, chunk_decay))
    return from_chunks(intra + cross)

def mixer_ab(x, w_in, pool_w, pool_scale, ret_norm_g, w_out):
    B_, S_, _ = x.shape
    h = x @ w_in
    u, q, k, v, g = jnp.split(h, AB_SPLITS, axis=-1)
    y_a = pool_mixer(u, pool_w, pool_scale)
    pos = jnp.arange(S_, dtype=jnp.float32)
    q = rotary(q.reshape(B_, S_, RET_HEADS, RET_QK_DIM), pos)
    k = rotary(k.reshape(B_, S_, RET_HEADS, RET_QK_DIM), pos) * (RET_QK_DIM ** -0.5)
    o = retention(q, k, v.reshape(B_, S_, RET_HEADS, RET_V_DIM))
    y_b = head_layernorm(o, ret_norm_g) * jax.nn.silu(g.astype(jnp.float32))
    y = jnp.concatenate([y_a.astype(x.dtype), y_b.astype(x.dtype)], axis=-1)
    return y @ w_out

def mixer_c(x, w_in, lower_bound, norm_g, w_out):
    h = x @ w_in
    q, fz, i, g = jnp.split(h, C_SPLITS, axis=-1)
    f = lower_bound + (1.0 - lower_bound) * jax.nn.sigmoid(fz.astype(jnp.float32))
    o = hgrn2_chunkwise(q, 1.0 - f, i, jnp.log(f))
    y = head_rmsnorm(o, norm_g) * jax.nn.silu(g.astype(jnp.float32))
    return y.astype(x.dtype) @ w_out

def peer(x, w_q, sub_keys, u_tab, v_tab):
    B_, S_, D = x.shape
    xb = x.reshape((B_ * S_) // PEER_BLOCK, PEER_BLOCK, D)
    kk = PEER_TOPK * PEER_TOPK

    def block(xt):
        T = xt.shape[0]
        q = (xt @ w_q).reshape(T, PEER_HEADS, 2, PEER_HALF)
        s = jnp.einsum('thpd,hpkd->thpk', q, sub_keys).astype(jnp.float32)
        s_top, i_top = lax.top_k(s, PEER_TOPK)
        cand = (s_top[:, :, 0, :, None] + s_top[:, :, 1, None, :]).reshape(T, PEER_HEADS, kk)
        cand_id = (i_top[:, :, 0, :, None] * PEER_NKEYS + i_top[:, :, 1, None, :]).reshape(T, PEER_HEADS, kk)
        best, pos = lax.top_k(cand, PEER_TOPK)
        eid = jnp.take_along_axis(cand_id, pos, axis=-1)
        gate = jax.nn.softmax(best, axis=-1)
        u_sel = jnp.take(u_tab, eid, axis=0)
        v_sel = jnp.take(v_tab, eid, axis=0)
        act = jax.nn.gelu(jnp.einsum('td,thkd->thk', xt, u_sel).astype(jnp.float32), approximate=False)
        coef = (gate * act).astype(xt.dtype)
        return jnp.einsum('thk,thkd->td', coef, v_sel)

    return lax.map(block, xb).reshape(B_, S_, D)

def first_inputs(seed: int = 0) -> dict:
    key = jax.random.key(seed)
    ks = jax.random.split(key, 16)

    def nrm(k, shape, scale):
        return jax.random.normal(k, shape, jnp.float32) * scale

    return {
        "x": nrm(ks[0], (BATCH, SEQ, D_MODEL), 1.0),
        "ab_w_in": nrm(ks[1], (N_EVEN, D_MODEL, AB_IN), D_MODEL ** -0.5),
        "pool_w": nrm(ks[2], (N_EVEN, N_POOL_GROUPS, POOL_GROUP, POOL_GROUP), POOL_GROUP ** -0.5),
        "pool_scale": 1.0 + nrm(ks[3], (N_EVEN, POOL_WIDTH), 0.02),
        "ret_norm_g": 1.0 + nrm(ks[4], (N_EVEN, RET_WIDTH), 0.02),
        "ab_w_out": nrm(ks[5], (N_EVEN, AB_OUT_IN, D_MODEL), AB_OUT_IN ** -0.5 * DN_BETA),
        "c_w_in": nrm(ks[6], (N_ODD, D_MODEL, C_IN), D_MODEL ** -0.5),
        "hgrn_lb": nrm(ks[7], (DEPTH, HGRN_FDIM), 0.1),
        "hgrn_norm_g": 1.0 + nrm(ks[8], (N_ODD, HGRN_HEADS * HGRN_V_DIM), 0.02),
        "c_w_out": nrm(ks[9], (N_ODD, D_MODEL, D_MODEL), D_MODEL ** -0.5 * DN_BETA),
        "peer_w_q": nrm(ks[10], (DEPTH, D_MODEL, PEER_HEADS * PEER_KEY_DIM), D_MODEL ** -0.5),
        "peer_sub_keys": nrm(ks[11], (DEPTH, PEER_HEADS, 2, PEER_NKEYS, PEER_HALF), PEER_HALF ** -0.5),
        "peer_u": nrm(ks[12], (DEPTH, PEER_EXPERTS, D_MODEL), D_MODEL ** -0.5),
        "peer_v": nrm(ks[13], (DEPTH, PEER_EXPERTS, D_MODEL), PEER_HEADS ** -0.5 * DN_BETA),
        "ln_g": 1.0 + nrm(ks[14], (DEPTH, 2, D_MODEL), 0.02),
        "ln_b": nrm(ks[15], (DEPTH, 2, D_MODEL), 0.02),
    }

def first_block(x, ab_w_in, pool_w, pool_scale, ret_norm_g, ab_w_out, c_w_in, hgrn_lb,
              hgrn_norm_g, c_w_out, peer_w_q, peer_sub_keys, peer_u, peer_v, ln_g, ln_b):
    lb_p = jax.nn.softmax(hgrn_lb.astype(jnp.float32), axis=0)
    lower_bounds = jnp.cumsum(lb_p, axis=0) - lb_p[0]
    h = x
    for layer in range(DEPTH):
        j = layer // 2
        if layer % 2 == 0:
            mix = mixer_ab(h, ab_w_in[j], pool_w[j], pool_scale[j], ret_norm_g[j], ab_w_out[j])
        else:
            mix = mixer_c(h, c_w_in[j], lower_bounds[layer], hgrn_norm_g[j], c_w_out[j])
        h = layer_norm(DN_ALPHA * h + mix.astype(h.dtype), ln_g[layer, 0], ln_b[layer, 0])
        ffn = peer(h, peer_w_q[layer], peer_sub_keys[layer], peer_u[layer], peer_v[layer])
        h = layer_norm(DN_ALPHA * h + ffn.astype(h.dtype), ln_g[layer, 1], ln_b[layer, 1])
    return h


DEPTH_2 = 1

N_META = 16
D_MIX = 2 * D_MODEL
SSD_HEAD_DIM = 64
SSD_HEADS = 24
D_SSD = SSD_HEADS * SSD_HEAD_DIM
SSD_GROUPS = 4
SSD_STATE = 128
SSD_CONV = 4
SSD_CHUNK = 128
D_XBC = D_SSD + 2 * SSD_GROUPS * SSD_STATE
D_SC = D_MIX - D_SSD
SC_CONV = 3
D_IN = D_SSD + D_XBC + SSD_HEADS + 3 * D_SC
PEER_KEYS = 128
PEER_EXPERTS_2 = PEER_KEYS * PEER_KEYS
PEER_QDIM = 256
PEER_HALF_2 = PEER_QDIM // 2
PEER_BLOCK_2 = 512
EPS = 1e-6


def rmsnorm(x, g):
    xf = x.astype(jnp.float32)
    xf = xf * lax.rsqrt(jnp.mean(xf * xf, axis=-1, keepdims=True) + EPS)
    return (xf * g.astype(jnp.float32)).astype(x.dtype)

def causal_dwconv(x, w):
    width, ch = w.shape
    return lax.conv_general_dilated(
        x, w[:, None, :].astype(x.dtype), window_strides=(1,), padding=[(width - 1, 0)],
        dimension_numbers=('NWC', 'WIO', 'NWC'), feature_group_count=ch)

def segsum(a):
    t = a.shape[-1]
    ar = jnp.broadcast_to(a[..., None], a.shape + (t,))
    ar = jnp.where(jnp.tril(jnp.ones((t, t), bool), -1), ar, 0.0)
    cs = jnp.cumsum(ar, axis=-2)
    return jnp.where(jnp.tril(jnp.ones((t, t), bool), 0), cs, -jnp.inf)

def ssd_scan(x, dt, A, Bm, Cm):
    b, l, h, p = x.shape
    g, n = Bm.shape[2], Bm.shape[3]
    r, q = h // g, SSD_CHUNK
    c = l // q
    xc = x.reshape(b, c, q, g, r, p)
    Bc = Bm.reshape(b, c, q, g, n)
    Cc = Cm.reshape(b, c, q, g, n)
    dtc = dt.reshape(b, c, q, g, r)
    a = (dtc * A.reshape(g, r)).transpose(0, 3, 4, 1, 2)
    x_dt = xc * dtc[..., None]
    a_cs = jnp.cumsum(a, axis=-1)
    decay_in = jnp.exp(segsum(a))
    cb = jnp.einsum('bclgn,bcsgn->bgcls', Cc, Bc)
    y_diag = jnp.einsum('bgcls,bgrcls,bcsgrp->bclgrp', cb, decay_in, x_dt)
    decay_states = jnp.exp(a_cs[..., -1:] - a_cs)
    states = jnp.einsum('bcsgn,bgrcs,bcsgrp->bcgrpn', Bc, decay_states, x_dt)
    states = jnp.concatenate([jnp.zeros_like(states[:, :1]), states], axis=1)
    chunk_a = jnp.pad(a_cs[..., -1], ((0, 0), (0, 0), (0, 0), (1, 0)))
    decay_chunk = jnp.exp(segsum(chunk_a))
    new_states = jnp.einsum('bgrzc,bcgrpn->bzgrpn', decay_chunk, states)
    prev_states = new_states[:, :-1]
    y_off = jnp.einsum('bclgn,bcgrpn,bgrcl->bclgrp', Cc, prev_states, jnp.exp(a_cs))
    return (y_diag + y_off).reshape(b, l, h, p)

def hybrid_mixer(n, w_in, conv_ssd_w, conv_ssd_b, dt_bias, a_log, d_skip, ssd_norm_w,
                 conv_sc_w, w_out):
    bsz, L, _ = n.shape
    proj = n @ w_in.astype(n.dtype)
    s1 = D_SSD
    s2 = s1 + D_XBC
    s3 = s2 + SSD_HEADS
    s4 = s3 + D_SC
    s5 = s4 + D_SC
    z, xbc, dt_raw, sc_b, sc_c, sc_x = jnp.split(proj, [s1, s2, s3, s4, s5], axis=-1)

    xbc = jax.nn.silu(causal_dwconv(xbc, conv_ssd_w) + conv_ssd_b.astype(n.dtype))
    xs, Bm, Cm = jnp.split(xbc, [D_SSD, D_SSD + SSD_GROUPS * SSD_STATE], axis=-1)
    xs_h = xs.reshape(bsz, L, SSD_HEADS, SSD_HEAD_DIM)
    dt = jax.nn.softplus(dt_raw.astype(jnp.float32) + dt_bias.astype(jnp.float32))
    A = -jnp.exp(a_log.astype(jnp.float32))
    pad_len = SSD_CHUNK - N_META

    def lpad(t):
        return jnp.pad(t, ((0, 0), (pad_len, 0)) + ((0, 0),) * (t.ndim - 2))

    y = ssd_scan(lpad(xs_h.astype(jnp.float32)), lpad(dt), A,
                 lpad(Bm.reshape(bsz, L, SSD_GROUPS, SSD_STATE).astype(jnp.float32)),
                 lpad(Cm.reshape(bsz, L, SSD_GROUPS, SSD_STATE).astype(jnp.float32)))
    y = y[:, pad_len:] + d_skip.astype(jnp.float32)[:, None] * xs_h.astype(jnp.float32)
    y = y.reshape(bsz, L, D_SSD) * jax.nn.silu(z.astype(jnp.float32))
    y_ssd = rmsnorm(y.reshape(bsz, L, SSD_GROUPS, D_SSD // SSD_GROUPS),
                    ssd_norm_w.reshape(SSD_GROUPS, D_SSD // SSD_GROUPS))
    y_ssd = y_ssd.reshape(bsz, L, D_SSD).astype(n.dtype)

    y_sc = sc_b * causal_dwconv(sc_c * sc_x, conv_sc_w)

    return jnp.concatenate([y_ssd, y_sc], axis=-1) @ w_out.astype(n.dtype)

def peer_ffn(n, w_q, sub_keys, expert_u, expert_v):
    bsz, L, d = n.shape
    t = n.reshape(-1, d)
    T = t.shape[0]
    q = (t @ w_q.astype(n.dtype)).reshape(T, PEER_HEADS, 2, PEER_HALF_2)
    s = jnp.einsum('thsd,hskd->thsk', q, sub_keys.astype(n.dtype)).astype(jnp.float32)
    v_half, i_half = lax.top_k(s, PEER_TOPK)
    cand = (v_half[:, :, 0, :, None] + v_half[:, :, 1, None, :]).reshape(T, PEER_HEADS, PEER_TOPK * PEER_TOPK)
    best, pos = lax.top_k(cand, PEER_TOPK)
    i1 = jnp.take_along_axis(i_half[:, :, 0], pos // PEER_TOPK, axis=-1)
    i2 = jnp.take_along_axis(i_half[:, :, 1], pos % PEER_TOPK, axis=-1)
    experts = (i1 * PEER_KEYS + i2).reshape(T, PEER_HEADS * PEER_TOPK)
    gates = jax.nn.softmax(best, axis=-1).reshape(T, PEER_HEADS * PEER_TOPK).astype(n.dtype)

    nb = -(-T // PEER_BLOCK_2)
    padT = nb * PEER_BLOCK_2 - T
    tp = jnp.pad(t, ((0, padT), (0, 0))).reshape(nb, PEER_BLOCK_2, d)
    ep = jnp.pad(experts, ((0, padT), (0, 0))).reshape(nb, PEER_BLOCK_2, -1)
    gp = jnp.pad(gates, ((0, padT), (0, 0))).reshape(nb, PEER_BLOCK_2, -1)

    def block(args):
        xb, eb, gb = args
        u = expert_u[eb].astype(xb.dtype)
        act = jax.nn.gelu(jnp.einsum('td,tkd->tk', xb, u), approximate=False) * gb
        return jnp.einsum('tk,tkd->td', act, expert_v[eb].astype(xb.dtype))

    out = lax.map(block, (tp, ep, gp))
    return out.reshape(-1, d)[:T].reshape(bsz, L, d)

def second_inputs(seed: int = 0) -> dict:
    key = jax.random.key(seed)
    ks = jax.random.split(key, 20)

    def nrm(k, shape, scale):
        return jax.random.normal(k, shape, jnp.float32) * scale

    x = nrm(ks[0], (BATCH, SEQ, D_MODEL), 1.0)
    meta_tokens = nrm(ks[1], (N_META, D_MODEL), 1.0)
    g_mix = 1.0 + nrm(ks[2], (DEPTH_2, D_MODEL), 0.05)
    w_in = nrm(ks[3], (DEPTH_2, D_MODEL, D_IN), D_MODEL ** -0.5)
    conv_ssd_w = nrm(ks[4], (DEPTH_2, SSD_CONV, D_XBC), SSD_CONV ** -0.5)
    conv_ssd_b = nrm(ks[5], (DEPTH_2, D_XBC), 0.02)
    dt0 = jnp.exp(jax.random.uniform(ks[6], (DEPTH_2, SSD_HEADS), jnp.float32,
                                     minval=math.log(1e-3), maxval=math.log(1e-1)))
    dt_bias = dt0 + jnp.log(-jnp.expm1(-dt0))
    a_log = jnp.log(jax.random.uniform(ks[7], (DEPTH_2, SSD_HEADS), jnp.float32, minval=1.0, maxval=16.0))
    d_skip = 1.0 + nrm(ks[8], (DEPTH_2, SSD_HEADS), 0.05)
    ssd_norm_w = 1.0 + nrm(ks[9], (DEPTH_2, D_SSD), 0.05)
    conv_sc_w = nrm(ks[10], (DEPTH_2, SC_CONV, D_SC), SC_CONV ** -0.5)
    w_out = nrm(ks[11], (DEPTH_2, D_MIX, D_MODEL), D_MIX ** -0.5)
    g_ffn = 1.0 + nrm(ks[12], (DEPTH_2, D_MODEL), 0.05)
    w_q = nrm(ks[13], (DEPTH_2, D_MODEL, PEER_HEADS * PEER_QDIM), D_MODEL ** -0.5)
    sub_keys = nrm(ks[14], (DEPTH_2, PEER_HEADS, 2, PEER_KEYS, PEER_HALF_2), PEER_HALF_2 ** -0.5)
    expert_u = nrm(ks[15], (DEPTH_2, PEER_EXPERTS_2, D_MODEL), D_MODEL ** -0.5)
    expert_v = nrm(ks[16], (DEPTH_2, PEER_EXPERTS_2, D_MODEL), PEER_HEADS ** -0.5)
    g_final = 1.0 + nrm(ks[17], (D_MODEL,), 0.05)
    return {"x": x, "meta_tokens": meta_tokens, "g_mix": g_mix, "w_in": w_in,
            "conv_ssd_w": conv_ssd_w, "conv_ssd_b": conv_ssd_b, "dt_bias": dt_bias,
            "a_log": a_log, "d_skip": d_skip, "ssd_norm_w": ssd_norm_w,
            "conv_sc_w": conv_sc_w, "w_out": w_out, "g_ffn": g_ffn, "w_q": w_q,
            "sub_keys": sub_keys, "expert_u": expert_u, "expert_v": expert_v,
            "g_final": g_final}

def second_block(x, meta_tokens, g_mix, w_in, conv_ssd_w, conv_ssd_b, dt_bias, a_log, d_skip,
              ssd_norm_w, conv_sc_w, w_out, g_ffn, w_q, sub_keys, expert_u, expert_v, g_final):
    bsz = x.shape[0]
    meta = jnp.broadcast_to(meta_tokens[None].astype(x.dtype), (bsz, N_META, D_MODEL))
    h = jnp.concatenate([meta, x], axis=1)
    for l in range(DEPTH_2):
        h = h + hybrid_mixer(rmsnorm(h, g_mix[l]), w_in[l], conv_ssd_w[l], conv_ssd_b[l],
                             dt_bias[l], a_log[l], d_skip[l], ssd_norm_w[l], conv_sc_w[l], w_out[l])
        h = h + peer_ffn(rmsnorm(h, g_ffn[l]), w_q[l], sub_keys[l], expert_u[l], expert_v[l])
    h = rmsnorm(h, g_final)
    return h[:, N_META:]


def setup_inputs(seed=0):
    out = dict(first_inputs(seed))
    for name, value in second_inputs(seed + 1).items():
        if name != "x":
            out[name + "_2"] = value
    return out


def reference(
    x, ab_w_in, pool_w, pool_scale, ret_norm_g, ab_w_out, c_w_in, hgrn_lb, hgrn_norm_g, c_w_out,
    peer_w_q, peer_sub_keys, peer_u, peer_v, ln_g, ln_b, meta_tokens_2, g_mix_2, w_in_2,
    conv_ssd_w_2, conv_ssd_b_2, dt_bias_2, a_log_2, d_skip_2, ssd_norm_w_2, conv_sc_w_2,
    w_out_2, g_ffn_2, w_q_2, sub_keys_2, expert_u_2, expert_v_2, g_final_2,
):
    x = first_block(
        x, ab_w_in, pool_w, pool_scale, ret_norm_g, ab_w_out, c_w_in, hgrn_lb, hgrn_norm_g,
        c_w_out, peer_w_q, peer_sub_keys, peer_u, peer_v, ln_g, ln_b,
    )
    return second_block(
        x, meta_tokens_2, g_mix_2, w_in_2, conv_ssd_w_2, conv_ssd_b_2, dt_bias_2, a_log_2,
        d_skip_2, ssd_norm_w_2, conv_sc_w_2, w_out_2, g_ffn_2, w_q_2, sub_keys_2, expert_u_2,
        expert_v_2, g_final_2,
    )


_drawn_inputs = setup_inputs


def setup_inputs(seed=0):
    import zlib

    import numpy as np

    out = dict(_drawn_inputs(seed))
    spreads = {}
    factors = {'pool_scale': 3.306, 'ret_norm_g': 3.698, 'hgrn_norm_g': 4.118}
    for name, (base, spread) in spreads.items():
        noise = np.random.default_rng([zlib.crc32(name.encode()), seed]).standard_normal(out[name].shape)
        drawn = base * np.exp(spread * noise) if base else spread * noise
        out[name] = jnp.asarray(drawn.astype(out[name].dtype))
    for name, factor in factors.items():
        out[name] = (out[name] * factor).astype(out[name].dtype)
    return out
```

```python
from contextlib import ExitStack

import numpy as np

import concourse.bass as bass
from concourse import mybir

F32 = mybir.dt.float32
F32R = mybir.dt.float32r
BF16 = mybir.dt.bfloat16
U32 = mybir.dt.uint32
ALU = mybir.AluOpType
ACT = mybir.ActivationFunctionType
AX = mybir.AxisListType.X

P = 128
D = 1024
DC = D // P
T = 256
NT = T // P
META = 16
TM = T + META
SLOTS = 3
NEG = -3.0e38

HEADS = 8
HP = 2 * HEADS
KEYS = 128
TOPK = 16
EARLY = KEYS // 2
EXP_AT = 54
SELS = HEADS * TOPK
UNROLL = 2 * SLOTS
PARTS = 3
GB = 4
BATCHES = T // GB
HEAD = BATCHES % UNROLL
TURNS = BATCHES // UNROLL
VREST = KEYS - BATCHES
assert BATCHES == KEYS - EARLY and HEAD > SLOTS and EXP_AT % UNROLL == 0 and VREST % SLOTS == 1

POOLG = 4
RH = 4
CH = 8
CCH = 32
SG, SR, SP_ = 4, 6, 64
SH = SG * SR
SW = SH * SP_
DN_ALPHA = 4.0 ** 0.25
LN_EPS = 1e-5
RMS_EPS = 1e-6

STREAM = [("ab_in", 16, "col"), ("ab_out", 8, "row"),
          ("wq0", HP, "col"), ("u0", KEYS, "col"), ("v0", KEYS, "row"),
          ("c_in", 32, "col"), ("c_out", 8, "row"),
          ("wq1", HP, "col"), ("u1", KEYS, "col"), ("v1", KEYS, "row"),
          ("s_in", 44, "col"), ("s_out", 16, "row"),
          ("wq2", HP, "col"), ("u2", KEYS, "col"), ("v2", KEYS, "row")]


STAGES = ("ab", "peer0", "c", "peer1", "s", "peer2")
STAGE_OF = {"ab_in": "ab", "ab_out": "ab", "c_in": "c", "c_out": "c", "s_in": "s", "s_out": "s"} | {
    f"{x}{n}": f"peer{n}" for x in ("wq", "u", "v") for n in range(3)}


class Slab:

    def __init__(self, base, turn=None):
        self.base, self.turn = base, turn

    def __add__(self, n):
        return Slab(self.base + n, self.turn)

    def __sub__(self, n):
        return Slab(self.base - n, self.turn)

    @property
    def slot(self):
        return self.base % SLOTS

    def index(self, less=0):
        n = self.base - less
        return n if self.turn is None else self.turn * SLOTS + n

    def half(self):
        return self.base // 2 if self.turn is None else self.turn // 2 * SLOTS + self.base // 2

    def round(self, times=1, more=0):
        n = (self.base // SLOTS) * times + more
        return n if self.turn is None else self.turn * times + n


class Steps:

    def __init__(self, eng, sem):
        self.eng, self.sem, self.n = eng, sem, 0

    def do(self, ins):
        ins.then_inc(self.sem, 1)
        self.n += 1

    def join(self):
        self.eng.wait_ge(self.sem, self.n)


class Kernel:

    def __init__(self, nc, ctx, dram, out, stages):
        self.nc, self.d, self.out = nc, dram, out
        self.stages = stages
        self.first, self.kind, self.cols_before = {}, [], [0]
        self.count = {}
        for name, n, kind in STREAM:
            if STAGE_OF[name] not in stages:
                continue
            self.count[name] = n
            self.first[name] = len(self.kind)
            for _ in range(n):
                self.kind.append(kind)
                self.cols_before.append(self.cols_before[-1] + (kind == "col"))
        self.total = len(self.kind)

        def sb(name, shape, dt=F32):
            return ctx.enter_context(nc.sbuf_tensor(name, shape, dt))

        def ps(name, shape):
            return ctx.enter_context(nc.psum_tensor(name, shape, F32))

        self.sem_names = []

        def sem(name):
            self.sem_names.append(name)
            return ctx.enter_context(nc.semaphore(name))

        self.ring = [sb(f"ring{i}", [P, D]) for i in range(SLOTS)]
        self.w_hi = [sb(f"w_hi{i}", [P, D], F32R) for i in range(SLOTS)]
        self.w_lo = [sb(f"w_lo{i}", [P, D], F32R) for i in range(SLOTS)]
        self.x_hi = sb("x_hi", [P, DC, TM], F32R)
        self.x_lo = sb("x_lo", [P, DC, TM], F32R)
        self.h = sb("h_tok", [P, NT, D])
        self.big = sb("work", [P, KEYS * T])
        self.c_hi = [sb(f"c_hi{i}", [P, T], F32R) for i in range(SLOTS)]
        self.c_lo = [sb(f"c_lo{i}", [P, T], F32R) for i in range(SLOTS)]
        self.oh1_room = sb("onehot_i1", [P, 2, GB, P])
        self.oh2_room = sb("gated_onehot_i2", [P, 2, GB, P])
        room = self.oh1_room[:, :, :, :].rearrange("p j t i -> p (j t i)")
        self.oh1 = room[:, 0:GB * P].bitcast(BF16).rearrange("p (j t i) -> p j t i", j=2, t=GB)
        self.gate = room[:, GB * P:GB * P + PARTS * T // 2].bitcast(BF16).rearrange("p (n t) -> p n t", n=PARTS)
        room = self.oh2_room[:, :, :, :].rearrange("p j t i -> p (j t i)")
        self.oh2 = room[:, 0:GB * PARTS * EARLY].bitcast(BF16)\
            .rearrange("p (j t n i) -> p j t n i", j=2, t=GB, n=PARTS)
        self.rest = room[:, 0:T]
        self.i1 = sb("i1", [P, T], BF16)
        self.neg_i1 = sb("neg_i1", [P, T])
        self.i2 = sb("i2", [P, T])
        self.ident = sb("ident", [P, P])
        self.iota = sb("iota", [P, P])
        self.iota_b = sb("iota_bf16", [P, P], BF16)
        self.small = sb("small", [P, 128])
        self.col = [ps(f"col{i}", [P, 512]) for i in range(SLOTS)]
        self.misc = ps("misc", [P, 512])
        self.acc = [ps(f"acc{i}", [P, 512]) for i in range(4)]

        self.load = [sem(f"slab_loaded{i}") for i in range(SLOTS)]
        self.hi = [sem(f"hi_ready{i}") for i in range(SLOTS)]
        self.lo = [sem(f"lo_ready{i}") for i in range(SLOTS)]
        self.used = sem("slab_used")
        self.evac = sem("column_evacuated")
        self.const = sem("const_loaded")
        self.xload = sem("x_loaded")
        self.param = [sem(f"norm_param{i}_loaded") for i in range(3)]
        self.dve_step = sem("dve_step")
        self.act_step = sem("act_step")
        self.h_ready = sem("h_ready")
        self.xt = sem("x_transposed")
        self.xhi = sem("x_hi_ready")
        self.x_ready = sem("x_ready")
        self.rms_in = sem("rms_input_ready")
        self.summed = sem("residual_added")
        self.norms = self.norms_before(None)
        self.var = sem("variance_ready")
        self.sq = sem("squares_ready")
        self.std = sem("std_ready")
        self.stored = sem("output_stored")
        self.keys = sem("keys_loaded")
        self.s_full = sem("scores_full")
        self.s_evac = sem("scores_evacuated")
        self.m_ready = sem("gate_max_subtracted")
        self.e_ready = sem("gate_exp_ready")
        self.routed = sem("routed")
        self.rt = sem("routing_transposed")
        self.i1_ready = sem("neg_i1_ready")
        self.oh_ready = sem("vector_onehots_ready")
        self.oh1_abs = sem("onehot_distance")
        self.oh1_ready = sem("scalar_onehot_ready")
        self.g_full = sem("gate_matrix_full")
        self.g_used = sem("gate_matrix_used")
        self.coef = [sem(f"coef_ready{i}") for i in range(SLOTS)]
        self.coef_h = sem("coef_hi_ready")
        self.mload = [sem(f"mixer_const{i}_loaded") for i in range(3)]
        self.m = {name: sem(name) for name in (
            "pool_ready", "pool_mixed", "rope_ready", "ret_scores", "ret_probs", "ret_out", "ret_y", "ret_yT",
            "y_ready",
            "c_lb", "c_lbe", "c_f", "c_logf", "c_b", "c_exps", "c_diff", "c_expdiff", "c_kout", "c_koutT", "c_ktok", "c_qk", "c_scores", "c_probs",
            "c_state_psum", "c_state", "c_out", "c_msq", "c_y", "c_yT",
            "s_conv", "s_silu", "s_xsT", "s_xtok", "s_dt", "s_dtb", "s_exps", "s_w", "s_ln", "s_a", "s_cs", "s_diff", "s_exp2", "s_xdt", "s_btokT", "s_btok", "s_cb", "s_cbm",
            "s_st", "s_state", "s_yoff", "s_yoffd", "s_am", "s_seg", "s_E", "s_P", "s_ydiag", "s_ysum", "s_gated", "s_msq", "s_y", "s_yT")}

    def cols(self, s):
        n = self.cols_before[s.base]
        return n if s.turn is None else s.turn * SLOTS + n

    def after_s(self, name):
        return "s" in self.stages and self.stages.index("s") < self.stages.index(name)

    def rows_in_slot(self, s, more=0):
        n = sum(self.kind[m] == "row" for m in range(s.slot, s.base, SLOTS)) + more
        return n if s.turn is None else s.turn + n

    def rows(self, s, more=0):
        n = s.base - self.cols_before[s.base] + more
        return n if s.turn is None else s.turn * SLOTS + n

    def norms_before(self, stage):
        n = 0
        for name in self.stages:
            if name == stage:
                return n
            n += 2 if name == "s" else 1
        return n

    def gates_before(self, layer, late):
        peers = sum(name[:4] == "peer" for name in self.stages[:self.stages.index(f"peer{layer}")])
        return (2 * peers + late) * BATCHES

    def scalar_onehots(self, layer):
        return self.gates_before(layer, 0) // 4

    def gate_pass(self, layer, late):
        if late:
            return self.col, EARLY, self.gates_before(layer, 1)
        return self.acc, 0, self.gates_before(layer, 0)


class Waits:

    def __init__(self, eng):
        self.eng, self.seen = eng, {}

    def next(self, sem, n=1):
        self.skip(sem, n)
        self.eng.wait_ge(sem, self.seen[sem.name])

    def skip(self, sem, n):
        self.seen[sem.name] = self.seen.get(sem.name, 0) + n

    def count(self, sem):
        return self.seen.get(sem.name, 0)


G_AT = (0, 2 * D, 4 * D)
NORMED = 6 * D
JUNK = 9 * D
MIX = 10 * D
QT = EARLY * T
SCORES = QT + HP * T
KEYT = SCORES + NT * HP * KEYS
ROUTE = KEYT
CAND = QT
PICK = CAND + 2048
assert KEYT + HP * KEYS <= KEYS * T


def view(t, at, *shape, p=P):
    n = int(np.prod(shape))
    v = t[0:p, at:at + n]
    if len(shape) == 1:
        return v
    names = "abcd"[:len(shape)]
    sizes = dict(zip(names[1:], shape[1:], strict=True))
    return v.rearrange(f"p ({' '.join(names)}) -> p {' '.join(names)}", **sizes)


class Lay:

    def __init__(self, k, at, end=KEYS * T):
        self.k, self.at, self.end = k, at, end

    def __call__(self, *shape, p=P):
        v = view(self.k.big, self.at, *shape, p=p)
        self.at += int(np.prod(shape))
        assert self.at <= self.end, (self.at, self.end)
        return v


def slab_view(k, s):
    return (k.w_hi[s.slot][:, :].rearrange("p (c n) -> p c n", c=DC),
            k.w_lo[s.slot][:, :].rearrange("p (c n) -> p c n", c=DC))


def sync_program(k, sp):
    w = Waits(sp)
    sp.dma_start(k.ident[:, :], k.d["ident"]).then_inc(k.const, 16)
    sp.dma_start(k.iota[:, :], k.d["iota"]).then_inc(k.const, 16)
    for t in range(NT):
        sp.dma_start(k.h[:, t, :], k.d["x"][t * P:(t + 1) * P, :]).then_inc(k.xload, 16)

    def put(name, s, n):
        if s.turn is not None or s.base >= SLOTS:
            sp.wait_ge(k.lo[s.slot], s.round())
        src = k.d[name][:, n, :] if name[0] == "v" else k.d[name][n, :, :]
        sp.dma_start(k.ring[s.slot][:, :], src).then_inc(k.load[s.slot], 16)

    def stream(name):
        first, count = k.first[name], k.count[name]
        head = SLOTS if first == 0 else 0
        for n in range(head):
            put(name, Slab(first + n), n)
        rounds = (count - head) // SLOTS
        with sp.Fori(0, rounds) as i:
            for p in range(SLOTS):
                put(name, Slab(first + head + p, i), i * SLOTS + (head + p))
        for n in range(head + rounds * SLOTS, count):
            put(name, Slab(first + n), n)

    def row(name, dst, i, sem):
        src = k.d[name][i:i + 1, :]
        sp.dma_start(dst, src.to_broadcast([P, src.shape[1]])).then_inc(sem, 16)

    def norm_param(slot, gain, bias=None):
        row(gain[0], view(k.big, G_AT[slot], D), gain[1], k.param[slot])
        if bias:
            row(bias[0], view(k.big, G_AT[slot] + D, D), bias[1], k.param[slot])

    def load(dst, name, i):
        sp.dma_start(dst, k.d[name]).then_inc(k.mload[i], 16)

    def keys(layer):
        if k.norms_before(f"peer{layer}"):
            sp.wait_ge(k.h_ready, k.norms_before(f"peer{layer}"))
        sp.dma_start(view(k.big, KEYT, HP, KEYS), k.d["keys"][layer]).then_inc(k.keys, 16)

    def peer(layer):
        stream(f"wq{layer}")
        keys(layer)
        stream(f"u{layer}")
        stream(f"v{layer}")
        last = Slab(k.first[f"v{layer}"] + KEYS - 1)
        sp.wait_ge(k.coef[last.slot], k.rows_in_slot(last, 1))

    for stage in k.stages:
        if stage == "ab":
            ab = MixAB(k)
            for dst, name in ((ab.cos, "cos"), (ab.sin, "sin"), (ab.count, "pool_count"), (ab.pool_w, "pool_w"),
                              (ab.pool_scale, "pool_scale"), (ab.decay, "ret_decay")):
                load(dst, name, 0)
            row("ret_g", ab.gain, 0, k.mload[0])
            norm_param(0, ("ln_g", 0), ("ln_b", 0))
            stream("ab_in")
            stream("ab_out")
        elif stage == "peer0":
            peer(0)
            norm_param(1, ("ln_g", 1), ("ln_b", 1))
        elif stage == "c":
            norm_param(2, ("ln_g", 2), ("ln_b", 2))
            c = MixC(k)
            load(c.bound, "hgrn_lb", 1)
            load(c.restart, "restart", 1)
            load(c.causal.bitcast(F32), "chunk_causal", 1)
            row("hgrn_g", c.gain, 0, k.mload[1])
            stream("c_in")
            stream("c_out")
        elif stage == "peer1":
            peer(1)
            norm_param(1, ("ln_g", 3), ("ln_b", 3))
        elif stage == "s":
            norm_param(2, ("g_mix", 0))
            norm_param(0, ("g_ffn", 0))
            s = MixS(k)
            for dst, name in s.loads():
                load(dst, name, 2)
            for dst, name in s.rows():
                row(name, dst, 0, k.mload[2])
            stream("s_in")
            stream("s_out")
        else:
            peer(2)
            norm_param(1, ("g_final", 0))
    sp.wait_ge(k.h_ready, k.norms)
    for t in range(NT):
        src = view(k.big, NORMED + t * D, D) if k.stages[-1] in ("s", "peer2") else k.h[:, t, :]
        sp.dma_start(k.out[t * P:(t + 1) * P, :], src).then_inc(k.stored, 16)
    sp.wait_ge(k.stored, 16 * NT)


def split_rest(k, eng, s):
    eng.wait_ge(k.hi[s.slot], s.round(1, 1))
    eng.tensor_tensor(k.w_lo[s.slot][:, :], k.ring[s.slot][:, :], k.w_hi[s.slot][:, :].bitcast(F32),
                      ALU.subtract).then_inc(k.lo[s.slot], 1)


def gpsimd_program(k, pool):
    def run(name, at, rounds):
        with pool.Fori(0, rounds) as i:
            for p in range(SLOTS):
                split_rest(k, pool, Slab(k.first[name] + at + p, i))

    def run_third(name, at, rounds):
        with pool.Fori(0, rounds) as i:
            split_rest(k, pool, Slab(k.first[name] + at + 2, i))

    def some(name, at, to):
        for n in range(at, to):
            split_rest(k, pool, Slab(k.first[name] + n))

    def stage(name, count):
        run(name, 0, count // SLOTS)
        some(name, count - count % SLOTS, count)

    def peer(layer):
        stage(f"wq{layer}", HP)
        u, v = f"u{layer}", f"v{layer}"
        stage(u, KEYS)
        run(v, 0, BATCHES // SLOTS)
        some(v, BATCHES - BATCHES % SLOTS, BATCHES + 1)
        run_third(v, BATCHES + 1, VREST // SLOTS)

    for name in k.stages:
        if name[:4] == "peer":
            peer(int(name[4]))
        else:
            stage(f"{name}_in", k.count[f"{name}_in"])
            stage(f"{name}_out", k.count[f"{name}_out"])


class Tensor:
    def __init__(self, k, pe):
        self.k, self.pe, self.w = k, pe, Waits(pe)

    def split_matmuls(self, out, a, b, start, stop, **kw):
        pe = self.pe
        pe.matmul(out, a[0], b[0], start=start, stop=False, **kw)
        pe.matmul(out, a[0], b[1], start=False, stop=False, **kw)
        return pe.matmul(out, a[1], b[0], start=False, stop=stop, **kw)

    def slab_ready(self, s):
        self.pe.wait_ge(self.k.lo[s.slot], s.round(1, 1))

    def bank_free(self, s):
        k = self.k
        if s.base >= SLOTS and k.cols_before[s.base - SLOTS + 1]:
            self.pe.wait_ge(k.evac, k.cols(s - (SLOTS - 1)))

    def features(self, s, n=T):
        k = self.k
        self.bank_free(s)
        self.slab_ready(s)
        hi, lo = slab_view(k, s)
        for c in range(DC):
            ins = self.split_matmuls(k.col[s.slot][:, 0:n], (hi[:, c, :], lo[:, c, :]),
                                     (k.x_hi[:, c, 0:n], k.x_lo[:, c, 0:n]), c == 0, c == DC - 1)
        ins.then_inc(k.used, 1)

    def tokens(self, s, at=0):
        k = self.k
        self.bank_free(s)
        self.slab_ready(s)
        hi, lo = slab_view(k, s)
        for t in range(NT):
            for c in range(DC):
                cut = slice(at + t * P, at + (t + 1) * P)
                ins = self.split_matmuls(k.col[s.slot][:, t * P:(t + 1) * P],
                                         (k.x_hi[:, c, cut], k.x_lo[:, c, cut]), (hi[:, c, :], lo[:, c, :]),
                                         c == 0, c == DC - 1)
        ins.then_inc(k.used, 1)

    def rows(self, s, y_hi, y_lo, start, stop):
        k = self.k
        self.slab_ready(s)
        for t in range(NT):
            for half in range(2):
                cut, n = slice(t * P, (t + 1) * P), slice(half * 512, (half + 1) * 512)
                ins = self.split_matmuls(k.acc[t * 2 + half][:, :], (y_hi[:, cut], y_lo[:, cut]),
                                         (k.w_hi[s.slot][:, n], k.w_lo[s.slot][:, n]), start, stop,
                                         skip_group_check=True)
        ins.then_inc(k.used, 1)

    def transpose_x(self, src, meta):
        k, pe = self.k, self.pe
        for b in range(4):
            for c in range(2):
                for t in range(NT):
                    ins = pe.transpose(k.acc[b][:, c * T + t * P:c * T + (t + 1) * P],
                                       src[t][:, (2 * b + c) * P:(2 * b + c + 1) * P], k.ident[:, :])
            ins.then_inc(k.xt, 1)
        if meta is not None:
            for c in range(DC):
                ins = pe.transpose(k.misc[:, c * META:(c + 1) * META], meta[:, c * P:(c + 1) * P],
                                   k.ident[0:META, 0:META])
            ins.then_inc(k.xt, 1)

    def peer(self, layer):
        k, pe, w = self.k, self.pe, self.w
        first = k.first[f"wq{layer}"]
        for n in range(HP):
            self.features(Slab(first + n))
        q = view(k.big, QT, HP, T)
        keys = view(k.big, KEYT, HP, KEYS)
        w.next(k.keys, 16)
        pe.wait_ge(k.evac, k.cols_before[first + HP])
        for t in range(NT):
            for quad in range(4):
                if t:
                    w.next(k.s_evac)
                for j in range(4):
                    hp = quad * 4 + j
                    ins = pe.matmul(k.acc[quad][:, j * KEYS:(j + 1) * KEYS], q[:, hp, t * P:(t + 1) * P],
                                    keys[:, hp, :], start=True, stop=True)
                ins.then_inc(k.s_full, 1)
        w.next(k.s_evac, 4)

        first = k.first[f"u{layer}"]
        with pe.Fori(0, EARLY // SLOTS) as i:
            for p in range(SLOTS):
                self.features(Slab(first + p, i))
        for n in range(EARLY - EARLY % SLOTS, EARLY):
            self.features(Slab(first + n))
        w.next(k.routed, NT)
        r = Route(k)
        for t in range(NT):
            pe.transpose(k.misc[:, t * P:(t + 1) * P], r.i1[t], k.ident[:, :])
            pe.transpose(k.acc[0][:, t * P:(t + 1) * P], r.gate[t], k.ident[:, :])
            ins = pe.transpose(k.acc[0][:, T + t * P:T + (t + 1) * P], r.i2[t], k.ident[:, :])
        ins.then_inc(k.rt, 1)

        def gates(b, late, wait=True):
            banks, _, g0 = k.gate_pass(layer, late)
            pe.wait_ge(k.oh_ready, b.index() + (g0 + 1))
            if late and b.base % 2:
                pe.wait_ge(k.oh1_ready, b.half() + (k.scalar_onehots(layer) + 1))
            if wait:
                pe.wait_ge(k.g_used, b.index() + (g0 + 1 - SLOTS))
            for t in range(GB):
                for n in range(PARTS):
                    ins = pe.matmul(banks[b.slot][:, t * EARLY:(t + 1) * EARLY], k.oh1[:, b.base % 2, t, :],
                                    k.oh2[:, b.base % 2, t, n, :], start=n == 0, stop=n == PARTS - 1)
            ins.then_inc(k.g_full, 1)

        for n in range(HEAD):
            self.features(Slab(first + EARLY + n))
            gates(Slab(n), False, wait=n >= SLOTS)
        with pe.Fori(0, TURNS) as i:
            for n in range(HEAD, HEAD + UNROLL):
                self.features(Slab(first + EARLY + n, i * 2))
                gates(Slab(n, i * 2), False)

        first = k.first[f"v{layer}"]
        pe.wait_ge(k.evac, k.cols_before[first])
        pe.wait_ge(k.g_used, k.gates_before(layer, 1))
        for n in range(HEAD):
            self.row_slab(Slab(first + n), start=n == 0)
            gates(Slab(n), True, wait=n >= SLOTS)
        with pe.Fori(0, TURNS) as i:
            for n in range(HEAD, HEAD + UNROLL):
                self.row_slab(Slab(first + n, i * 2))
                gates(Slab(n, i * 2), True)
        self.row_slab(Slab(first + BATCHES))
        with pe.Fori(0, VREST // SLOTS) as i:
            for p in range(SLOTS):
                self.row_slab(Slab(first + BATCHES + 1 + p, i))

    def row_slab(self, s, start=False, stop=False):
        k = self.k
        self.pe.wait_ge(k.coef[s.slot], k.rows_in_slot(s, 1))
        self.rows(s, k.c_hi[s.slot], k.c_lo[s.slot], start, stop)

    def row_stage(self, name, count):
        for n in range(count):
            self.row_slab(Slab(self.k.first[name] + n), n == 0, n == count - 1)


def tensor_program(k, pe):
    e = Tensor(k, pe)
    pe.wait_ge(k.const, 32)
    pe.wait_ge(k.xload, 16 * NT)
    for name in k.stages:
        if name == "s" or k.after_s(name):
            src = [view(k.big, NORMED + t * D, D) for t in range(NT)]
        else:
            src = [k.h[:, t, :] for t in range(NT)]
        meta = view(k.big, NORMED + 2 * D, D, p=META) if name == "s" else None
        norms = k.norms_before(name) + (name == "s")
        if norms:
            pe.wait_ge(k.h_ready, norms)
        e.transpose_x(src, meta)
        e.w.next(k.x_ready, 5 if name == "s" else 4)
        if name[:4] == "peer":
            e.peer(int(name[4]))
        else:
            MIXERS[name](k).tensor(e)


class Scalar:
    AHEAD = SLOTS

    def __init__(self, k, act):
        self.k, self.act, self.w = k, act, Waits(act)
        self.own = Steps(act, k.act_step)

    def split_lead(self, s):
        k, act = self.k, self.act
        if s.turn is None and s.base >= k.total:
            return
        if s.turn is not None or s.base >= SLOTS:
            act.wait_ge(k.used, s.index(SLOTS - 1))
        act.wait_ge(k.load[s.slot], s.round(16, 16))
        act.activation(k.w_hi[s.slot][:, :], k.ring[s.slot][:, :], ACT.Copy).then_inc(k.hi[s.slot], 1)

    def column(self, s, dst, func=ACT.Copy, n=T, src=None):
        k, act = self.k, self.act
        act.wait_ge(k.used, s.index(-1))
        src = k.col[s.slot][:, 0:n] if src is None else src(k.col[s.slot])
        act.activation(dst, src, func).then_inc(k.evac, 1)
        self.split_lead(s + self.AHEAD)

    def row_slabs(self, name, count):
        for n in range(count):
            self.split_lead(Slab(self.k.first[name] + n + self.AHEAD))

    def lead_x(self, meta=False):
        k, act, w = self.k, self.act, self.w
        at = META if meta else 0
        for b in range(4):
            w.next(k.xt)
            act.activation(k.x_hi[:, 2 * b:2 * b + 2, at:at + T],
                           k.acc[b][:, :].rearrange("p (c t) -> p c t", c=2), ACT.Copy).then_inc(k.xhi, 1)
        if meta:
            w.next(k.xt)
            act.activation(k.x_hi[:, :, 0:META], k.misc[:, 0:DC * META].rearrange("p (c t) -> p c t", c=DC),
                           ACT.Copy).then_inc(k.xhi, 1)

    def std(self, src=None, dst=None):
        k, act = self.k, self.act
        self.w.next(k.var)
        act.activation(k.small[:, 8:10] if dst is None else dst, k.small[:, 4:6] if src is None else src,
                       ACT.Sqrt).then_inc(k.std, 1)

    def rms(self, srcs, ready=None):
        k, act, w = self.k, self.act, self.w
        if ready is None:
            w.next(k.rms_in)
        for n, src in enumerate(srcs):
            rows = src.shape[0]
            ins = act.activation(view(k.big, JUNK, D, p=rows), src, ACT.Square,
                                 accum_out=k.small[0:rows, 40 + n:41 + n])
            if n + 1 < len(srcs):
                self.own.do(ins)
                self.own.join()
        ins.then_inc(k.sq, 1)
        w.next(k.var)
        act.activation(k.small[:, 8:8 + len(srcs)], k.small[:, 4:4 + len(srcs)], ACT.Sqrt).then_inc(k.std, 1)

    def peer(self, layer):
        k, act, w = self.k, self.act, self.w
        first = k.first[f"wq{layer}"]
        q = view(k.big, QT, HP, T)
        for n in range(HP):
            self.column(Slab(first + n), q[:, n, :])
        scores = view(k.big, SCORES, NT, HP * KEYS)
        for t in range(NT):
            for quad in range(4):
                w.next(k.s_full)
                act.activation(scores[:, t, quad * 512:(quad + 1) * 512], k.acc[quad][:, :], ACT.Copy)\
                   .then_inc(k.s_evac, 1)

        first = k.first[f"u{layer}"]
        act_of = view(k.big, 0, KEYS, T)

        def expert(n, s):
            self.column(s, act_of[:, n, :], ACT.Gelu)

        with act.Fori(0, EXP_AT // UNROLL) as i:
            for p in range(UNROLL):
                expert(i * UNROLL + p, Slab(first + p, i * 2))
        r = Route(k)
        for t in range(NT):
            w.next(k.m_ready)
            act.activation(r.gate[t], r.gate[t], ACT.Exp).then_inc(k.e_ready, 1)
        for n in range(EXP_AT, EARLY):
            expert(n, Slab(first + n))
        w.next(k.rt)
        act.activation(k.neg_i1[:, :], k.misc[:, 0:T], ACT.Copy, scale=-1.0).then_inc(k.i1_ready, 1)
        w.next(k.i1_ready)
        for n in range(EARLY, EARLY + HEAD):
            expert(n, Slab(first + n))

        with act.Fori(0, (KEYS - EARLY - HEAD) // UNROLL) as i:
            for p in range(UNROLL):
                expert(i * UNROLL + (EARLY + HEAD + p), Slab(first + EARLY + HEAD + p, i * 2))

        def onehots(b):
            act.wait_ge(k.g_full, b.index() + (k.gates_before(layer, 1) - 1))
            for t in range(GB):
                at = bass.ds(b.index() * GB + t, 1)
                act.activation(k.oh1[:, 1, t, :], k.iota_b[:, :], ACT.Abs, bias=k.neg_i1[:, at])\
                   .then_inc(k.oh1_abs, 1)
            act.wait_ge(k.oh1_abs, b.half() * GB + (k.scalar_onehots(layer) + 1) * GB)
            act.activation(k.oh1[:, 1, :, :], k.oh1[:, 1, :, :], ACT.Relu, bias=1.0, scale=-1.0)\
               .then_inc(k.oh1_ready, 1)

        first = k.first[f"v{layer}"]

        def late(n, i=None):
            self.split_lead(Slab(first + n + self.AHEAD, i))
            if n % 2 and n + 2 < BATCHES:
                onehots(Slab(n + 2, i))

        onehots(Slab(1))
        for n in range(HEAD):
            late(n)
        with act.Fori(0, TURNS - 1) as i:
            for n in range(HEAD, HEAD + UNROLL):
                late(n, i * 2)
        for n in range(BATCHES - UNROLL, BATCHES):
            late(n)
        at = first + BATCHES + self.AHEAD
        self.split_lead(Slab(at))
        with act.Fori(0, VREST // SLOTS - 1) as i:
            for p in range(SLOTS):
                self.split_lead(Slab(at + 1 + p, i))
        for n in range(KEYS - SLOTS, KEYS):
            self.split_lead(Slab(first + n + self.AHEAD))


class Route:

    def __init__(self, k):
        lay = Lay(k, ROUTE)
        self.gate = [lay(SELS) for _ in range(NT)]
        self.i1 = [lay(SELS) for _ in range(NT)]
        self.i2 = [lay(SELS) for _ in range(NT)]
        self.top = lay(HP, TOPK)
        self.itop = lay(HP, TOPK).bitcast(U32)
        self.itop_f = lay(HP, TOPK)
        self.pos = lay(HEADS, TOPK).bitcast(U32)
        self.half = lay(HEADS, TOPK).bitcast(U32)
        self.half_f = lay(SELS)
        self.sums = [lay(HEADS) for _ in range(NT)]


class Vector:
    def __init__(self, k, dve):
        self.k, self.dve, self.w = k, dve, Waits(dve)
        self.own = Steps(dve, k.dve_step)

    def rest_x(self, meta=False):
        k, dve, w = self.k, self.dve, self.w
        at = META if meta else 0
        for b in range(4):
            w.next(k.xhi)
            cut = (slice(None), slice(2 * b, 2 * b + 2), slice(at, at + T))
            dve.tensor_tensor(k.x_lo[cut], k.acc[b][:, :].rearrange("p (c t) -> p c t", c=2),
                              k.x_hi[cut].bitcast(F32), ALU.subtract).then_inc(k.x_ready, 1)
        if meta:
            w.next(k.xhi)
            dve.tensor_tensor(k.x_lo[:, :, 0:META], k.misc[:, 0:DC * META].rearrange("p (c t) -> p c t", c=DC),
                              k.x_hi[:, :, 0:META].bitcast(F32), ALU.subtract).then_inc(k.x_ready, 1)

    def add_residual(self, last, alpha, ready=None):
        k, dve = self.k, self.dve
        ready = k.summed if ready is None else ready
        dve.wait_ge(k.used, last + 1)
        for t in range(NT):
            for half in range(2):
                part = k.h[:, t, half * 512:(half + 1) * 512]
                ins = dve.scalar_tensor_tensor(part, part, alpha, k.acc[t * 2 + half][:, :], ALU.mult, ALU.add)
        ins.then_inc(ready, 1)
        self.w.next(ready)

    def inverse_std(self, n):
        k, dve = self.k, self.dve
        self.w.next(k.std)
        self.own.do(dve.reciprocal(k.small[:, 12:12 + n], k.small[:, 8:8 + n]))
        self.own.join()

    def layer_norm(self, slot):
        k, dve, own = self.k, self.dve, self.own
        stats = k.small[:, 16:40].rearrange("p (t h s) -> p t h s", t=NT, h=2)
        mean_var = k.small[:, 0:4].rearrange("p (t s) -> p t s", t=NT)
        for t in range(NT):
            for half in range(2):
                own.do(dve.bn_stats(stats[:, t, half, :], k.h[:, t, half * 512:(half + 1) * 512]))
        own.join()
        for t in range(NT):
            own.do(dve.bn_aggr(mean_var[:, t, :], stats[:, t, :, :].rearrange("p h s -> p (h s)")))
        own.join()
        dve.tensor_scalar(k.small[:, 4:6], mean_var[:, :, 1], LN_EPS, None, ALU.add).then_inc(k.var, 1)
        self.inverse_std(NT)
        for t in range(NT):
            own.do(dve.tensor_scalar(k.h[:, t, :], k.h[:, t, :], mean_var[:, t, 0:1], k.small[:, 12 + t:13 + t],
                                     ALU.subtract, ALU.mult))
        own.join()
        self.w.next(k.param[slot], 32)
        gain, bias = view(k.big, G_AT[slot], D), view(k.big, G_AT[slot] + D, D)
        for t in range(NT):
            own.do(dve.tensor_tensor(k.h[:, t, :], k.h[:, t, :], gain, ALU.mult))
        own.join()
        for t in range(NT):
            ins = dve.tensor_tensor(k.h[:, t, :], k.h[:, t, :], bias, ALU.add)
        ins.then_inc(k.h_ready, 1)
        self.w.next(k.h_ready)

    def rms_norm(self, slot, meta=None):
        k, dve, own = self.k, self.dve, self.own
        n = 3 if meta is not None else 2
        self.w.next(k.sq)
        dve.tensor_scalar(k.small[:, 4:4 + n], k.small[:, 40:40 + n], 1.0 / D, RMS_EPS, ALU.mult, ALU.add)\
           .then_inc(k.var, 1)
        self.inverse_std(n)
        self.w.next(k.param[slot], 16)
        gain = view(k.big, G_AT[slot], D)
        for t in range(NT):
            ins = dve.scalar_tensor_tensor(view(k.big, NORMED + t * D, D), k.h[:, t, :], k.small[:, 12 + t:13 + t],
                                           gain, ALU.mult, ALU.mult)
        if meta is not None:
            ins = dve.scalar_tensor_tensor(view(k.big, NORMED + 2 * D, D, p=META), meta, k.small[0:META, 14:15],
                                           gain[0:META, :], ALU.mult, ALU.mult)
        ins.then_inc(k.h_ready, 1)
        self.w.next(k.h_ready)

    def coef(self, src, s):
        k, dve = self.k, self.dve
        dve.wait_ge(k.used, s.index(SLOTS - 1))
        dve.tensor_copy(k.c_hi[s.slot][:, :], src).then_inc(k.coef_h, 1)
        dve.wait_ge(k.coef_h, k.rows(s, 1))
        dve.tensor_tensor(k.c_lo[s.slot][:, :], src, k.c_hi[s.slot][:, :].bitcast(F32),
                          ALU.subtract).then_inc(k.coef[s.slot], 1)

    def top16(self, rows, top, index):
        dve, own = self.dve, self.own
        for n in range(len(rows)):
            own.do(dve.max(top(n)[:, 0:8], rows[n]))
        own.join()
        for n in range(len(rows)):
            own.do(dve.max_index(index(n)[:, 0:8], top(n)[:, 0:8], rows[n]))
        own.join()
        for n in range(len(rows)):
            own.do(dve.match_replace(rows[n], top(n)[:, 0:8], rows[n], NEG))
        own.join()
        for n in range(len(rows)):
            own.do(dve.max(top(n)[:, 8:16], rows[n]))
        own.join()
        for n in range(len(rows)):
            own.do(dve.max_index(index(n)[:, 8:16], top(n)[:, 8:16], rows[n]))
        own.join()

    def route(self, t):
        k, dve, own = self.k, self.dve, self.own
        r = Route(k)
        scores = view(k.big, SCORES, NT, HP, KEYS)
        cand = view(k.big, CAND, HEADS, TOPK * TOPK)
        self.top16([scores[:, t, n, :] for n in range(HP)], lambda n: r.top[:, n, :], lambda n: r.itop[:, n, :])
        own.do(dve.tensor_copy(r.itop_f, r.itop))
        halves = r.top.rearrange("p (h two) k -> p h two k", two=2)
        shape = [P, HEADS, TOPK, TOPK]
        own.do(dve.tensor_tensor(cand.rearrange("p h (a b) -> p h a b", a=TOPK),
                                 halves[:, :, 0, :].unsqueeze(3).to_broadcast(shape),
                                 halves[:, :, 1, :].unsqueeze(2).to_broadcast(shape), ALU.add))
        own.join()
        best = r.gate[t].rearrange("p (h k) -> p h k", h=HEADS)
        self.top16([cand[:, n, :] for n in range(HEADS)], lambda n: best[:, n, :], lambda n: r.pos[:, n, :])
        own.do(dve.tensor_copy(r.sums[t], best[:, :, 0]))
        own.join()
        dve.tensor_tensor(best, best, r.sums[t].unsqueeze(2).to_broadcast([P, HEADS, TOPK]), ALU.subtract)\
           .then_inc(k.m_ready, 1)
        pick = view(k.big, PICK, HEADS, TOPK, TOPK)
        places = r.itop_f.rearrange("p (h two) k -> p h two k", two=2)
        for half, dst in enumerate((r.i1[t], r.i2[t])):
            if half == 0:
                own.do(dve.tensor_scalar(r.half, r.pos, 4, None, ALU.logical_shift_right))
            else:
                own.do(dve.tensor_scalar(r.half, r.pos, TOPK - 1, None, ALU.bitwise_and))
            own.join()
            own.do(dve.tensor_copy(r.half_f, r.half.rearrange("p h k -> p (h k)")))
            own.join()
            own.do(dve.tensor_tensor(pick.rearrange("p h k a -> p (h k) a"),
                                     r.half_f.unsqueeze(2).to_broadcast([P, SELS, TOPK]),
                                     k.iota[:, 0:TOPK].unsqueeze(1).to_broadcast([P, SELS, TOPK]), ALU.is_equal))
            own.join()
            own.do(dve.tensor_tensor(pick, pick, places[:, :, half, :].unsqueeze(2).to_broadcast(shape), ALU.mult))
            own.join()
            own.do(dve.tensor_reduce(dst, pick.rearrange("p h k a -> p (h k) a"), AX, ALU.add))
            own.join()

    def peer(self, layer):
        k, dve, w, own = self.k, self.dve, self.w, self.own
        r = Route(k)
        w.next(k.s_evac, 8)
        for t in range(NT):
            self.route(t)
        for t in range(NT):
            w.next(k.e_ready)
            gate = r.gate[t].rearrange("p (h k) -> p h k", h=HEADS)
            own.do(dve.tensor_reduce(r.sums[t], gate, AX, ALU.add))
            own.join()
            own.do(dve.reciprocal(r.sums[t], r.sums[t]))
            own.join()
            dve.tensor_tensor(gate, gate, r.sums[t].unsqueeze(2).to_broadcast([P, HEADS, TOPK]), ALU.mult)\
               .then_inc(k.routed, 1)
        w.next(k.rt)
        w.next(k.i1_ready)
        own.do(dve.tensor_scalar(k.i1[:, :], k.neg_i1[:, :], -1.0, None, ALU.mult))
        own.do(dve.tensor_copy(k.i2[:, :], k.acc[0][:, T:2 * T]))
        rest = k.acc[0][:, 0:T]
        for n in range(PARTS):
            own.do(dve.tensor_copy(k.gate[:, n, :], rest))
            own.join()
            if n + 1 < PARTS:
                own.do(dve.tensor_tensor(k.rest, rest, k.gate[:, n, :], ALU.subtract))
                own.join()
                rest = k.rest

        experts = view(k.big, 0, KEYS, T)

        def onehots(b, late, wait=True):
            _, at, g0 = k.gate_pass(layer, late)
            if wait:
                dve.wait_ge(k.g_full, b.index() + (g0 - 1))
            slot, token = b.base % 2, b.index() * GB
            if slot == 0 or not late:
                shape = [P, GB, P]
                dve.tensor_tensor(k.oh1[:, slot, :, :], k.iota_b[:, :].unsqueeze(1).to_broadcast(shape),
                                  k.i1[:, bass.ds(token, GB)].unsqueeze(2).to_broadcast(shape), ALU.is_equal)
            shape = [P, PARTS, EARLY]
            for t in range(GB):
                sel = bass.ds(token + t, 1)
                ins = dve.scalar_tensor_tensor(k.oh2[:, slot, t, :, :],
                                               k.iota_b[:, at:at + EARLY].unsqueeze(1).to_broadcast(shape),
                                               k.i2[:, sel], k.gate[:, :, sel].to_broadcast(shape),
                                               ALU.is_equal, ALU.mult)
            ins.then_inc(k.oh_ready, 1)

        def weigh(b, late):
            banks, at, g0 = k.gate_pass(layer, late)
            dve.wait_ge(k.g_full, b.index() + (g0 + 1))
            part = experts[:, at:at + EARLY, bass.ds(b.index() * GB, GB)]
            dve.tensor_tensor(part, part, banks[b.slot][:, 0:GB * EARLY].rearrange("p (t i) -> p i t", t=GB),
                              ALU.mult).then_inc(k.g_used, 1)

        def gate_pass(step):
            for n in range(HEAD):
                step(n)
            with dve.Fori(0, TURNS - 1) as i:
                for n in range(HEAD, HEAD + UNROLL):
                    step(n, i * 2)
            for n in range(BATCHES - UNROLL, BATCHES):
                step(n)

        for n in range(2):
            onehots(Slab(n), 0, wait=k.gates_before(layer, 0) > 0)
        dve.wait_ge(k.evac, k.cols_before[k.first[f"u{layer}"] + EARLY])

        def early(n, i=None):
            weigh(Slab(n, i), 0)
            if n + 2 < BATCHES:
                onehots(Slab(n + 2, i), 0)
            else:
                onehots(Slab(n + 2 - BATCHES), 1)

        gate_pass(early)
        dve.wait_ge(k.g_used, k.gates_before(layer, 1))
        first = k.first[f"v{layer}"]
        for n in range(2):
            self.coef(experts[:, n, :], Slab(first + n))
        dve.wait_ge(k.evac, k.cols_before[first])

        def late(n, i=None):
            weigh(Slab(n, i), 1)
            if n + 2 < BATCHES:
                s = Slab(first + n + 2, i)
                self.coef(experts[:, s.index(first), :], s)
                onehots(Slab(n + 2, i), 1)

        gate_pass(late)
        dve.wait_ge(k.g_used, k.gates_before(layer, 1) + BATCHES)
        self.coef(experts[:, BATCHES, :], Slab(first + BATCHES))
        with dve.Fori(0, VREST // SLOTS) as i:
            for p in range(SLOTS):
                s = Slab(first + BATCHES + 1 + p, i)
                if p < 2:
                    split_rest(k, dve, s)
                self.coef(experts[:, s.index(first), :], s)
        if layer < 2:
            self.add_residual(k.first[f"v{layer}"] + KEYS - 1, DN_ALPHA)
        else:
            self.add_residual(k.first[f"v{layer}"] + KEYS - 1, 1.0, k.rms_in)


def vector_program(k, dve):
    e = Vector(k, dve)
    e.own.do(dve.memset(k.small[:, :], 1.0))
    e.own.join()
    dve.wait_ge(k.const, 32)
    e.own.do(dve.tensor_copy(k.iota_b[:, :], k.iota[:, :]))
    dve.wait_ge(k.xload, 16 * NT)
    for name in k.stages:
        if name == "s":
            e.w.next(k.mload[2], 16 * MixS.LOADS)
            e.rms_norm(2, MixS(k).meta)
        e.rest_x(meta=name == "s")
        if name[:4] == "peer":
            e.peer(int(name[4]))
        else:
            MIXERS[name](k).vector(e)
            e.add_residual(k.first[f"{name}_out"] + k.count[f"{name}_out"] - 1, *((1.0, k.rms_in) if name == "s"
                                                                                  else (DN_ALPHA,)))
        if name in ("ab", "c", "peer0", "peer1"):
            e.layer_norm({"ab": 0, "c": 2}.get(name, 1))
        else:
            e.rms_norm({"s": 0}.get(name, 1))


def scalar_program(k, act):
    e = Scalar(k, act)
    tiles = [k.h[:, t, :] for t in range(NT)]
    for s in range(Scalar.AHEAD):
        e.split_lead(Slab(s))
    act.wait_ge(k.dve_step, 1)
    for name in k.stages:
        if name == "s":
            e.w.next(k.mload[2], 16 * MixS.LOADS)
            act.wait_ge(k.xload, 16 * NT)
            if k.norms_before("s"):
                act.wait_ge(k.h_ready, k.norms_before("s"))
            e.rms([*tiles, MixS(k).meta], True)
        e.lead_x(meta=name == "s")
        if name[:4] == "peer":
            e.peer(int(name[4]))
        else:
            MIXERS[name](k).scalar(e)
            e.row_slabs(f"{name}_out", k.count[f"{name}_out"])
        if name in ("s", "peer2"):
            e.rms(tiles)
        else:
            e.std()


class MixAB:
    HALF = 32
    PAD = 16
    CONSTS = 7

    def __init__(self, k):
        self.k = k
        lay = Lay(k, MIX)
        self.cos, self.sin = lay(T), lay(T)
        self.count = lay(POOLG, T)
        self.pool_w = lay(POOLG, P)
        self.pool_scale = lay(POOLG)
        self.decay = lay(RH, 3 * P)
        self.gain = lay(RH * P)
        self.u = lay(POOLG, self.PAD + T)
        self.win = [lay(POOLG, self.PAD + T) for _ in range(2)]
        self.pooled = lay(POOLG, T)
        self.x = [lay(2, T) for _ in range(2)]
        self.prod = [lay(2, T) for _ in range(4)]
        self.rot = [lay(2, T) for _ in range(2)]
        self.v = lay(NT, RH * P)
        self.g = lay(NT, RH * P)
        self.probs = lay(RH, 3 * P)
        self.o = lay(NT, RH * P)
        self.stats = lay(NT, RH, 6)
        self.mean_var = lay(NT * RH, 2)
        self.var, self.std, self.inv = lay(NT * RH), lay(NT * RH), lay(NT * RH)
        self.y = lay(8, T)

    def tensor(self, e):
        k, pe, w = self.k, e.pe, e.w
        m = k.m
        first = k.first["ab_in"]
        for n in range(8):
            e.features(Slab(first + n))
        for n in range(8, 16):
            e.tokens(Slab(first + n))
        pe.wait_ge(k.evac, first + 16)
        w.next(k.mload[0], 16 * self.CONSTS)
        w.next(m["pool_ready"])
        for g in range(POOLG):
            ins = pe.matmul((k.misc, k.col[2])[g // 2][:, g % 2 * T:(g % 2 + 1) * T], self.pool_w[:, g, :],
                            self.pooled[:, g, :], start=True, stop=True)
        ins.then_inc(m["pool_mixed"], 1)
        w.next(m["rope_ready"])
        for h in range(RH):
            rows = slice(h * self.HALF, (h + 1) * self.HALF)
            for src, to, out in ((0, slice(0, T), slice(0, T)), (1, slice(P, T), slice(T, T + P))):
                for half in range(2):
                    r = self.rot[half]
                    ins = pe.matmul(k.acc[h][:, out], r[rows, 1, src * P:(src + 1) * P], r[rows, 0, to],
                                    start=half == 0, stop=half == 1)
            ins.then_inc(m["ret_scores"], 1)
        for h in range(RH):
            w.next(m["ret_probs"])
            cut = slice(h * P, (h + 1) * P)
            pe.matmul(k.col[0][:, cut], self.probs[:, h, 0:P], self.v[:, 0, cut], start=True, stop=True)
            pe.matmul(k.col[1][:, cut], self.probs[:, h, P:2 * P], self.v[:, 0, cut], start=True, stop=False)
            ins = pe.matmul(k.col[1][:, cut], self.probs[:, h, 2 * P:], self.v[:, 1, cut], start=False, stop=True)
        ins.then_inc(m["ret_out"], 1)
        w.next(m["ret_y"])
        for j in range(4):
            for t in range(NT):
                ins = pe.transpose((k.misc, k.col[2])[j // 2][:, j % 2 * T + t * P:j % 2 * T + (t + 1) * P],
                                   self.o[:, t, j * P:(j + 1) * P], k.ident[:, :])
            if j % 2:
                ins.then_inc(m["ret_yT"], 1)
        e.row_stage("ab_out", 8)

    def scalar(self, e):
        k, act, w = self.k, e.act, e.w
        first = k.first["ab_in"]
        dst = [self.u[:, g, self.PAD:] for g in range(POOLG)]
        dst += [self.x[half][:, j, :] for half in range(2) for j in range(2)]
        for n in range(8):
            e.column(Slab(first + n), dst[n])
        for n in range(4):
            e.column(Slab(first + 8 + n), self.v[:, :, n * P:(n + 1) * P],
                     src=lambda b: b[:, 0:T].rearrange("p (t c) -> p t c", t=NT))
        for n in range(4):
            e.column(Slab(first + 12 + n), self.g[:, :, n * P:(n + 1) * P], ACT.Silu,
                     src=lambda b: b[:, 0:T].rearrange("p (t c) -> p t c", t=NT))
        e.std(self.var, self.std)
        for b in range(2):
            w.next(k.m["ret_yT"])
            act.activation(self.y[:, 4 + 2 * b:6 + 2 * b, :],
                           (k.misc, k.col[2])[b][:, :].rearrange("p (c t) -> p c t", c=2), ACT.Copy)\
               .then_inc(k.m["y_ready"], 1)

    def vector(self, e):
        k, dve, w, own = self.k, e.dve, e.w, e.own
        m = k.m
        first = k.first["ab_in"]
        w.next(k.mload[0], 16 * self.CONSTS)
        own.do(dve.memset(self.u[:, :, 0:self.PAD], 0.0))
        own.join()
        dve.wait_ge(k.evac, first + POOLG)
        end = self.PAD + T
        for j in range(POOLG):
            for g in range(j, POOLG):
                at = self.PAD - (2 ** (g + 1) - 2 ** (j + 1))
                src = self.u if j == 0 else self.win[(j - 1) % 2]
                own.do(dve.tensor_tensor(self.win[j % 2][:, g, at:end], src[:, g, at:end],
                                         src[:, g, at - 2 ** j:end - 2 ** j], ALU.add))
            own.join()
            own.do(dve.tensor_tensor(self.pooled[:, j, :], self.win[j % 2][:, j, self.PAD:], self.count[:, j, :],
                                     ALU.mult))
        own.join()
        dve.tensor_tensor(self.pooled, self.pooled, self.u[:, :, self.PAD:], ALU.subtract)\
           .then_inc(m["pool_ready"], 1)
        dve.wait_ge(k.evac, first + 8)
        for n, (half, table) in enumerate(((0, self.cos), (1, self.sin), (1, self.cos), (0, self.sin))):
            own.do(dve.tensor_tensor(self.prod[n], self.x[half], table.unsqueeze(1).to_broadcast([P, 2, T]),
                                     ALU.mult))
        own.join()
        own.do(dve.tensor_tensor(self.rot[0], self.prod[0], self.prod[1], ALU.subtract))
        dve.tensor_tensor(self.rot[1], self.prod[2], self.prod[3], ALU.add).then_inc(m["rope_ready"], 1)
        w.next(m["pool_mixed"])
        for g in range(POOLG):
            own.do(dve.tensor_scalar(self.y[:, g, :], (k.misc, k.col[2])[g // 2][:, g % 2 * T:(g % 2 + 1) * T],
                                     self.pool_scale[:, g:g + 1], None, ALU.mult))
        for h in range(RH):
            w.next(m["ret_scores"])
            dve.tensor_tensor(self.probs[:, h, :], k.acc[h][:, 0:3 * P], self.decay[:, h, :], ALU.mult)\
               .then_inc(m["ret_probs"], 1)
        dve.wait_ge(k.evac, first + 16)
        own.do(dve.tensor_tensor(self.g, self.g, self.gain.unsqueeze(1).to_broadcast([P, NT, RH * P]), ALU.mult))
        w.next(m["ret_out"])
        for t in range(NT):
            for h in range(RH):
                own.do(dve.bn_stats(self.stats[:, t, h, :], k.col[t][:, h * P:(h + 1) * P]))
        own.join()
        for t in range(NT):
            for h in range(RH):
                own.do(dve.bn_aggr(self.mean_var[:, t * RH + h, :], self.stats[:, t, h, :]))
        own.join()
        dve.tensor_scalar(self.var, self.mean_var[:, :, 1], LN_EPS, None, ALU.add).then_inc(k.var, 1)
        w.next(k.std)
        own.do(dve.reciprocal(self.inv, self.std))
        own.join()
        for t in range(NT):
            for h in range(RH):
                n = t * RH + h
                own.do(dve.tensor_scalar(self.o[:, t, h * P:(h + 1) * P], k.col[t][:, h * P:(h + 1) * P],
                                         self.mean_var[:, n, 0:1], self.inv[:, n:n + 1], ALU.subtract, ALU.mult))
        own.join()
        dve.tensor_tensor(self.o, self.o, self.g, ALU.mult).then_inc(m["ret_y"], 1)
        first = k.first["ab_out"]
        for n in range(8):
            if n >= 4 and n % 2 == 0:
                w.next(m["y_ready"])
            e.coef(self.y[:, n, :], Slab(first + n))


class MixC:
    CONSTS = 4

    def __init__(self, k):
        self.k = k
        self.banks = [*k.col, k.misc]
        lay = Lay(k, MIX)
        self.bound = lay(2, CH)
        self.restart = lay(T)
        self.causal = lay(P).bitcast(U32)
        self.gain = lay(D)
        self.f = lay(CH, T)
        self.q = lay(CH, T)
        self.key = lay(CH, T)
        self.log = lay(CH, T)
        self.b = lay(CH, T)
        self.v = lay(NT, D)
        self.g = lay(NT, D)
        self.probs = lay(NT, CH, P)
        self.ktok = lay(NT, CH, P)
        self.state = [lay(CH, P) for _ in range(2)]
        self.max = lay(CH)
        self.exps = lay(2, CH)
        self.low, self.span = lay(CH), lay(CH)
        self.b_last = lay(CH, T // CCH)
        self.msq, self.var, self.std, self.inv = (lay(NT * CH) for _ in range(4))
        self.yT = self.f
        self.y = self.key.rearrange("p h t -> p (h t)").rearrange("p (t c) -> p t c", t=NT)

    def block(self, banks, t, h):
        n = t * CH + h
        return banks[n // 4][:, n % 4 * P:(n % 4 + 1) * P]

    def tensor(self, e):
        k, pe, w = self.k, e.pe, e.w
        m = k.m
        first = k.first["c_in"]
        for n in range(16):
            e.features(Slab(first + n))
        for n in range(16, 32):
            e.tokens(Slab(first + n))
        pe.wait_ge(k.evac, k.cols_before[first + 32])
        w.next(m["c_qk"])
        for t in range(NT):
            for h in range(CH):
                cut = slice(t * P, (t + 1) * P)
                ins = pe.matmul(self.block(self.banks, t, h), self.f[:, h, cut], self.q[:, h, cut],
                                start=True, stop=True)
                if h % 4 == 3:
                    ins.then_inc(m["c_scores"], 1)
        w.next(m["c_kout"])
        for t in range(NT):
            for h in range(CH):
                ins = pe.transpose(self.block(k.acc, t, h), self.b[:, h, t * P:(t + 1) * P], k.ident[:, :])
                if h % 4 == 3:
                    ins.then_inc(m["c_koutT"], 1)
        w.next(m["c_ktok"], 4)
        w.next(m["c_probs"], 4)
        for t in range(NT):
            for h in range(CH):
                pe.matmul(self.block(k.acc, t, h), self.probs[:, t, h, :], self.v[:, t, h * P:(h + 1) * P],
                          start=h % 4 == 0, stop=False, skip_group_check=True)
        chunks = T // CCH
        for n in range(chunks):
            t, j = divmod(n, P // CCH)
            rows = slice(j * CCH, (j + 1) * CCH)
            if n:
                w.next(m["c_state"])
                for h in range(CH):
                    ins = pe.matmul(self.block(k.acc, t, h)[rows, :], self.q[:, h, n * CCH:(n + 1) * CCH],
                                    self.state[n % 2][:, h, :], start=False, stop=n % 4 == 3, skip_group_check=True)
            if n < chunks - 1:
                for h in range(CH):
                    ins = pe.matmul(self.banks[n % 2 * 2 + h // 4][:, h % 4 * P:(h % 4 + 1) * P],
                                    self.ktok[rows, t, h, :], self.v[rows, t, h * P:(h + 1) * P],
                                    start=True, stop=True)
                ins.then_inc(m["c_state_psum"], 1)
        ins.then_inc(m["c_out"], 1)
        w.next(m["c_y"])
        for b in range(4):
            for c in range(2):
                for t in range(NT):
                    ins = pe.transpose(self.banks[b][:, c * T + t * P:c * T + (t + 1) * P],
                                       self.y[:, t, (2 * b + c) * P:(2 * b + c + 1) * P], k.ident[:, :])
            ins.then_inc(m["c_yT"], 1)
        e.row_stage("c_out", 8)

    def scalar(self, e):
        k, act, w = self.k, e.act, e.w
        m = k.m
        first = k.first["c_in"]
        w.next(m["c_lb"])
        act.activation(self.exps, self.exps, ACT.Exp).then_inc(m["c_lbe"], 1)
        for n in range(8):
            e.column(Slab(first + n), self.f[:, n, :], ACT.Sigmoid)
        for n in range(8):
            e.column(Slab(first + 8 + n), self.q[:, n, :])
        w.next(m["c_f"])
        act.activation(self.log, self.f, ACT.Ln).then_inc(m["c_logf"], 1)
        for n in range(8):
            e.column(Slab(first + 16 + n), self.v[:, :, n * P:(n + 1) * P],
                     src=lambda b: b[:, 0:T].rearrange("p (t c) -> p t c", t=NT))
        w.next(m["c_b"])
        act.activation(self.f, self.b, ACT.Exp, scale=-1.0).then_inc(m["c_exps"], 1)
        act.activation(self.log, self.b, ACT.Exp).then_inc(m["c_exps"], 1)
        w.next(m["c_diff"])
        act.activation(self.b, self.b, ACT.Exp).then_inc(m["c_expdiff"], 1)
        for n in range(8):
            e.column(Slab(first + 24 + n), self.g[:, :, n * P:(n + 1) * P], ACT.Silu,
                     src=lambda b: b[:, 0:T].rearrange("p (t c) -> p t c", t=NT))
        for b in range(4):
            w.next(m["c_koutT"])
            t, h = divmod(4 * b, CH)
            act.activation(self.ktok[:, t, h:h + 4, :], k.acc[b][:, :].rearrange("p (h d) -> p h d", h=4), ACT.Copy)\
               .then_inc(m["c_ktok"], 1)
        w.next(m["c_out"])
        for t in range(NT):
            for h in range(CH):
                n = t * CH + h
                ins = act.activation(self.y[:, t, h * P:(h + 1) * P], self.block(k.acc, t, h), ACT.Square,
                                     accum_out=self.msq[:, n:n + 1])
        ins.then_inc(m["c_msq"], 1)
        e.std(self.var, self.std)
        for b in range(4):
            w.next(m["c_yT"])
            act.activation(self.yT[:, 2 * b:2 * b + 2, :], self.banks[b][:, :].rearrange("p (c t) -> p c t", c=2),
                           ACT.Copy).then_inc(m["y_ready"], 1)

    def vector(self, e):
        k, dve, w, own = self.k, e.dve, e.w, e.own
        m = k.m
        before = k.cols_before[k.first["c_in"]]
        w.next(k.mload[1], 16 * self.CONSTS)
        own.do(dve.tensor_tensor(self.max, self.bound[:, 0, :], self.bound[:, 1, :], ALU.max))
        own.do(dve.memset(self.probs, 0.0))
        own.join()
        dve.tensor_tensor(self.exps, self.bound, self.max.unsqueeze(1).to_broadcast([P, 2, CH]), ALU.subtract)\
           .then_inc(m["c_lb"], 1)
        w.next(m["c_lbe"])
        own.do(dve.tensor_tensor(self.max, self.exps[:, 0, :], self.exps[:, 1, :], ALU.add))
        own.join()
        own.do(dve.reciprocal(self.max, self.max))
        own.join()
        own.do(dve.tensor_tensor(self.low, self.exps[:, 1, :], self.max, ALU.mult))
        own.join()
        own.do(dve.tensor_scalar(self.span, self.low, -1.0, 1.0, ALU.mult, ALU.add))
        own.join()
        dve.wait_ge(k.evac, before + 8)
        for h in range(CH):
            ins = dve.tensor_scalar(self.f[:, h, :], self.f[:, h, :], self.span[:, h:h + 1], self.low[:, h:h + 1],
                                    ALU.mult, ALU.add)
        ins.then_inc(m["c_f"], 1)
        w.next(m["c_f"])
        own.do(dve.tensor_scalar(self.key, self.f, -1.0, 1.0, ALU.mult, ALU.add))
        w.next(m["c_logf"])
        for h in range(CH):
            ins = dve.tensor_tensor_scan(self.b[:, h, :], self.restart, self.log[:, h, :], 0.0, ALU.mult, ALU.add)
        ins.then_inc(m["c_b"], 1)
        w.next(m["c_b"])
        by_chunk = self.b.rearrange("p h t -> p (h t)").rearrange("p (n c) -> p n c", c=CCH)
        last = self.b_last.rearrange("p h n -> p (h n)")
        own.do(dve.tensor_copy(last, by_chunk[:, :, CCH - 1]))
        w.next(m["c_exps"], 2)
        own.join()
        dve.tensor_tensor(by_chunk, last.unsqueeze(2).to_broadcast([P, CH * T // CCH, CCH]), by_chunk, ALU.subtract)\
           .then_inc(m["c_diff"], 1)
        dve.wait_ge(k.evac, before + 16)
        own.do(dve.tensor_tensor(self.f, self.f, self.key, ALU.mult))
        dve.tensor_tensor(self.q, self.q, self.log, ALU.mult).then_inc(m["c_qk"], 1)
        w.next(m["c_expdiff"])
        dve.tensor_tensor(self.b, self.b, self.key, ALU.mult).then_inc(m["c_kout"], 1)
        for b in range(4):
            w.next(m["c_scores"])
            t, h = divmod(4 * b, CH)
            dve.copy_predicated(self.probs[:, t, h:h + 4, :], self.causal.unsqueeze(1).to_broadcast([P, 4, P]),
                                self.banks[b][:, :].rearrange("p (h c) -> p h c", h=4)).then_inc(m["c_probs"], 1)
        decay = self.log.rearrange("p h (n c) -> p h n c", c=CCH)[:, :, :, CCH - 1]
        for n in range(T // CCH - 1):
            w.next(m["c_state_psum"])
            for h in range(CH):
                new = self.banks[n % 2 * 2 + h // 4][:, h % 4 * P:(h % 4 + 1) * P]
                if n:
                    ins = dve.scalar_tensor_tensor(self.state[(n + 1) % 2][:, h, :], self.state[n % 2][:, h, :],
                                                   decay[:, h, n:n + 1], new, ALU.mult, ALU.add)
                else:
                    ins = dve.tensor_copy(self.state[1][:, h, :], new)
            ins.then_inc(m["c_state"], 1)
            w.next(m["c_state"])
        dve.wait_ge(k.evac, before + 32)
        own.do(dve.tensor_tensor(self.g, self.g, self.gain.unsqueeze(1).to_broadcast([P, NT, D]), ALU.mult))
        w.next(m["c_msq"])
        dve.tensor_scalar(self.var, self.msq, 1.0 / P, LN_EPS, ALU.mult, ALU.add).then_inc(k.var, 1)
        w.next(k.std)
        own.do(dve.reciprocal(self.inv, self.std))
        own.join()
        for t in range(NT):
            for h in range(CH):
                n = t * CH + h
                cut = slice(h * P, (h + 1) * P)
                ins = dve.scalar_tensor_tensor(self.y[:, t, cut], self.block(k.acc, t, h), self.inv[:, n:n + 1],
                                               self.g[:, t, cut], ALU.mult, ALU.mult)
        ins.then_inc(m["c_y"], 1)
        first = k.first["c_out"]
        for n in range(8):
            if n % 2 == 0:
                w.next(m["y_ready"])
            e.coef(self.yT[:, n, :], Slab(first + n))


class MixS:
    XS = SW // P
    CONVS = XS + 2 * SG
    TAPS, SC_TAPS = 4, 3
    SC = 4
    UNIT = 3
    GW = SR * SP_
    LOADS = 11
    M = 2

    def __init__(self, k):
        self.k = k
        self.banks = [*k.col, k.misc]
        lay = Lay(k, MIX)
        self.meta = lay(D, p=META)
        self.conv_w, self.conv_b = lay(self.CONVS, self.TAPS), lay(self.CONVS)
        self.sc_w = lay(self.SC, self.SC_TAPS)
        self.dt_w = lay(DC, SH)
        self.tri = lay(P)
        self.after = lay(P)
        self.dt_bias, self.a_log, self.d_skip = lay(SH), lay(SH), lay(SH)
        self.gain = lay(SW)
        self.x = lay(NT + 1, SW)
        self.xdecay = lay(2, SW)
        self.y = lay(NT, SW)
        self.z = lay(NT, SW)
        self.state = lay(SW)
        self.bc = lay(2 * SG, TM)
        self.btok = lay(2, SG * P)
        self.dt = lay(NT + 1, SH)
        self.a = lay(NT + 1, SH)
        self.sums = lay(3, NT + 1, SH)
        self.t = [lay(NT + 1, SH) for _ in range(5)]
        self.msq, self.var, self.std, self.inv = (lay(NT * SG) for _ in range(4))
        low = Lay(k, 2 * D, MIX)
        self.raw = [low(self.TAPS - 1 + TM) for _ in range(SLOTS)]
        at = low.at
        self.conv = [low(TM) for _ in range(SLOTS)]
        self.silu = [low(TM) for _ in range(SLOTS)]
        self.tmp = view(k.big, at, SW)
        self.weighted = [view(k.big, 2 * D + j * self.UNIT * P, self.UNIT, P) for j in range(2)]
        self.m = low(self.SC, self.SC_TAPS - 1 + TM)
        self.sc_x = low(self.SC, TM)
        self.sc_b = low(self.SC, TM)
        self.sc_y = low(self.SC, T)
        self.cb = low(NT, SG, P)
        self.am = [k.oh1_room[:, j, 0:self.UNIT, :] for j in range(2)]
        self.e = [k.oh2_room[:, j, 0:self.UNIT, :] for j in range(2)]
        self.ones = k.oh1_room[:, 0, 3, :]
        self.yT = self.xdecay.rearrange("p t c -> p (t c)").rearrange("p (n t) -> p n t", t=T)

    def loads(self):
        return ((self.meta, "meta"), (self.conv_w, "conv_w"), (self.conv_b, "conv_b"), (self.sc_w, "sc_w"),
                (self.dt_w, "dt_w"), (self.tri, "tri"), (self.after, "after"))

    def rows(self):
        return ((self.dt_bias, "dt_bias"), (self.a_log, "a_log"), (self.d_skip, "d_skip"), (self.gain, "ssd_norm"))

    def tile(self, t):
        return (slice(0, META), META) if t == self.M else (slice(META + t * P, META + (t + 1) * P), P)

    def tensor(self, e):
        k, pe, w = self.k, e.pe, e.w
        m = k.m
        first = k.first["s_in"]
        w.next(k.mload[2], 16 * self.LOADS)
        for t in (0, 1, self.M):
            cut, n = self.tile(t)
            for c in range(DC):
                for part in (k.x_hi, k.x_lo):
                    ins = pe.matmul(k.misc[0:n, t * SH:(t + 1) * SH], part[:, c, cut].bitcast(F32),
                                    self.dt_w[:, c, :], start=c == 0 and part is k.x_hi,
                                    stop=c == DC - 1 and part is k.x_lo)
        ins.then_inc(m["s_dt"], 1)

        def x_tokens(n):
            w.next(m["s_silu"])
            if n >= 2:
                w.next(m["s_xtok"])
            for t in (0, 1, self.M):
                cut, rows = self.tile(t)
                ins = pe.transpose(k.acc[n % 2][0:rows, t * P:(t + 1) * P], self.silu[n % SLOTS][:, cut],
                                   k.ident[:, :])
            ins.then_inc(m["s_xsT"], 1)

        for n in range(self.CONVS):
            e.features(Slab(first + n), TM)
            if 2 <= n < self.XS + 2:
                x_tokens(n - 2)
            if n == 4:
                w.next(m["s_a"])
                for t in (0, 1, self.M):
                    _, rows = self.tile(t)
                    at = t * SH
                    pe.matmul(k.acc[3][0:rows, at:at + SH], self.tri[0:rows, 0:rows], self.a[0:rows, t, :],
                              start=True, stop=True)
                    at += 96
                    ins = pe.matmul(k.acc[3][:, at:at + SH], self.ones[0:rows, :], self.a[0:rows, t, :],
                                    start=True, stop=True)
                ins.then_inc(m["s_cs"], 1)
        for n in range(self.CONVS, self.CONVS + 3 * self.SC):
            e.features(Slab(first + n), TM)
        for n in range(self.CONVS + 3 * self.SC, k.count["s_in"]):
            e.tokens(Slab(first + n), META)
        pe.wait_ge(k.evac, k.cols_before[first + k.count["s_in"]])
        w.next(m["s_silu"], self.CONVS - self.XS)
        w.next(m["s_xtok"], 2)

        for b, t in enumerate((0, self.M)):
            cut, rows = self.tile(t)
            for g in range(SG):
                ins = pe.transpose(k.acc[b][0:rows, g * P:(g + 1) * P], self.bc[:, g, cut], k.ident[:, :])
            ins.then_inc(m["s_btokT"], 1)
        for t in range(NT):
            cut, _ = self.tile(t)
            for g in range(SG):
                ins = pe.matmul(k.acc[2 + t][:, g * P:(g + 1) * P], self.bc[:, g, cut], self.bc[:, SG + g, cut],
                                start=True, stop=True)
            ins.then_inc(m["s_cb"], 1)
        w.next(m["s_btok"], 2)
        w.next(m["s_cbm"], 2)
        for t, source in ((0, self.M), (1, 0)):
            _, rows = self.tile(source)
            b = 1 if source == self.M else 0
            w.next(m["s_xdt"])
            for g in range(SG):
                ins = pe.matmul(self.banks[g][:, 0:self.GW], self.btok[0:rows, b, g * P:(g + 1) * P],
                                self.xdecay[0:rows, b, g * self.GW:(g + 1) * self.GW], start=True, stop=True)
            ins.then_inc(m["s_st"], 1)
            w.next(m["s_state"])
            if t:
                w.next(m["s_yoffd"])
            cut, _ = self.tile(t)
            for g in range(SG):
                ins = pe.matmul(k.acc[g][:, 0:self.GW], self.bc[:, SG + g, cut],
                                self.state[:, g * self.GW:(g + 1) * self.GW], start=True, stop=True)
            ins.then_inc(m["s_yoff"], 1)
        w.next(m["s_yoffd"])

        units = SH // self.UNIT

        def decays(n):
            w.next(m["s_am"])
            if n >= 4:
                w.next(m["s_E"])
            for r in range(self.UNIT):
                ins = pe.matmul(self.banks[n % 4][:, r * P:(r + 1) * P], self.am[n % 2][:, r, :], self.tri,
                                start=True, stop=True)
            ins.then_inc(m["s_seg"], 1)

        def products(n):
            t, u = divmod(n, units)
            w.next(m["s_P"])
            if u == 0 and t:
                w.next(m["s_ysum"])
            for r in range(self.UNIT):
                h = u * self.UNIT + r
                g, at = h // SR, h % SR * SP_
                ins = pe.matmul(k.acc[g][:, at:at + SP_], self.weighted[n % 2][:, r, :],
                                self.x[:, t, h * SP_:(h + 1) * SP_], start=True, stop=True)
            ins.then_inc(m["s_ydiag"], 1)

        decays(0)
        for n in range(NT * units):
            if n + 1 < NT * units:
                decays(n + 1)
            products(n)
        w.next(m["s_y"])
        w.next(m["s_E"], 4)
        banks = [*self.banks, k.acc[0], k.acc[1]]
        for b in range(6):
            for c in range(2):
                for t in range(NT):
                    ins = pe.transpose(banks[b][:, c * T + t * P:c * T + (t + 1) * P],
                                       self.y[:, t, (2 * b + c) * P:(2 * b + c + 1) * P], k.ident[:, :])
            ins.then_inc(m["s_yT"], 1)
        w.next(m["y_ready"], 6)
        e.row_stage("s_out", 16)

    def scalar(self, e):
        k, act, w = self.k, e.act, e.w
        m = k.m
        first = k.first["s_in"]

        def silu(n):
            w.next(m["s_conv"])
            if n < self.XS:
                if n >= SLOTS:
                    w.next(m["s_xsT"])
                dst = self.silu[n % SLOTS]
            else:
                dst = self.bc[:, n - self.XS, :]
            act.activation(dst, self.conv[n % SLOTS], ACT.Silu, bias=self.conv_b[:, n:n + 1])\
               .then_inc(m["s_silu"], 1)

        for n in range(self.CONVS):
            if n >= SLOTS:
                act.wait_ge(m["s_conv"], n - 2)
            e.column(Slab(first + n), self.raw[n % SLOTS][:, self.TAPS - 1:], n=TM)
            if n:
                silu(n - 1)
            if n == 1:
                w.next(m["s_dtb"])
                act.activation(self.a_log, self.a_log, ACT.Exp).then_inc(m["s_exps"], 1)
                act.activation(self.t[1], self.t[0], ACT.Exp, scale=-1.0).then_inc(m["s_exps"], 1)
            if n == 2:
                w.next(m["s_w"])
                act.activation(self.t[3], self.t[2], ACT.Ln).then_inc(m["s_ln"], 1)
            if n == 6:
                w.next(m["s_diff"])
                act.activation(self.sums, self.sums, ACT.Exp).then_inc(m["s_exp2"], 1)
        silu(self.CONVS - 1)
        dst = [self.m[:, g, self.SC_TAPS - 1:] for g in range(self.SC)]
        dst += [self.sc_x[:, g, :] for g in range(self.SC)] + [self.sc_b[:, g, :] for g in range(self.SC)]
        for n in range(3 * self.SC):
            e.column(Slab(first + self.CONVS + n), dst[n], n=TM)
        base = first + self.CONVS + 3 * self.SC
        for n in range(self.XS):
            e.column(Slab(base + n), self.z[:, :, n * P:(n + 1) * P], ACT.Silu,
                     src=lambda b: b[:, 0:T].rearrange("p (t c) -> p t c", t=NT))
        for b, t in enumerate((0, self.M)):
            w.next(m["s_btokT"])
            _, rows = self.tile(t)
            act.activation(self.btok[0:rows, b, :], k.acc[b][0:rows, :], ACT.Copy).then_inc(m["s_btok"], 1)
        units = SH // self.UNIT
        for n in range(NT * units):
            w.next(m["s_seg"])
            if n >= 2:
                w.next(m["s_P"])
            act.activation(self.e[n % 2], self.banks[n % 4][:, 0:self.UNIT * P].rearrange("p (r l) -> p r l", l=P),
                           ACT.Exp).then_inc(m["s_E"], 1)
        w.next(m["s_gated"])
        for t in range(NT):
            for g in range(SG):
                cut = slice(g * self.GW, (g + 1) * self.GW)
                ins = act.activation(self.x[:, t, cut], self.y[:, t, cut], ACT.Square,
                                     accum_out=self.msq[:, t * SG + g:t * SG + g + 1])
        ins.then_inc(m["s_msq"], 1)
        e.std(self.var, self.std)
        banks = [*self.banks, k.acc[0], k.acc[1]]
        for b in range(6):
            w.next(m["s_yT"])
            act.activation(self.yT[:, 2 * b:2 * b + 2, :], banks[b][:, :].rearrange("p (c t) -> p c t", c=2),
                           ACT.Copy).then_inc(m["y_ready"], 1)

    def heads(self, x):
        return x.rearrange("p (h c) -> p h c", c=SP_)

    def per_head(self, s, rows=P):
        return s.unsqueeze(2).to_broadcast([rows, s.shape[1], SP_])

    def vector(self, e):
        k, dve, w, own = self.k, e.dve, e.w, e.own
        m = k.m
        before = k.cols_before[k.first["s_in"]]
        own.do(dve.memset(self.ones, 1.0))
        own.do(dve.memset(self.m[:, :, 0:self.SC_TAPS - 1], 0.0))
        own.do(dve.memset(self.sums, 0.0))
        own.do(dve.memset(self.t[4], 0.0))
        for r in self.raw:
            own.do(dve.memset(r[:, 0:self.TAPS - 1], 0.0))
        own.join()

        def part(out, t):
            return out[0:self.tile(t)[1], t, :]

        w.next(m["s_dt"])
        x = self.t[4]
        for t in (0, 1, self.M):
            rows = self.tile(t)[1]
            own.do(dve.tensor_tensor(part(x, t), k.misc[0:rows, t * SH:(t + 1) * SH], self.dt_bias[0:rows, :], ALU.add))
        own.join()
        own.do(dve.tensor_scalar(self.t[2], x, -1.0, None, ALU.mult))
        own.join()
        dve.tensor_tensor(self.t[0], x, self.t[2], ALU.max).then_inc(m["s_dtb"], 1)

        def conv(n):
            dve.wait_ge(k.evac, before + n + 1)
            if n >= SLOTS:
                w.next(m["s_silu"])
            out, raw = self.conv[n % SLOTS], self.raw[n % SLOTS]
            last = self.TAPS - 1
            own.do(dve.tensor_scalar(out, raw[:, last:last + TM], self.conv_w[:, n, last:last + 1], None, ALU.mult))
            for tap in range(last - 1, -1, -1):
                own.join()
                ins = dve.scalar_tensor_tensor(out, raw[:, tap:tap + TM], self.conv_w[:, n, tap:tap + 1], out,
                                               ALU.mult, ALU.add)
                if tap:
                    own.do(ins)
            ins.then_inc(m["s_conv"], 1)

        def x_tokens(n):
            w.next(m["s_xsT"])
            cut = slice(n * P, (n + 1) * P)
            own.do(dve.tensor_copy(self.x[:, 0:NT, cut], k.acc[n % 2][:, 0:NT * P].rearrange("p (t c) -> p t c", t=NT)))
            dve.tensor_copy(self.x[0:META, self.M, cut], k.acc[n % 2][0:META, NT * P:(NT + 1) * P])\
               .then_inc(m["s_xtok"], 1)

        for n in range(self.CONVS):
            conv(n)
            if 2 <= n < self.XS + 2:
                x_tokens(n - 2)
            if n == 1:
                w.next(m["s_exps"], 2)
                z = self.t[1]
                own.do(dve.tensor_scalar(self.a_log, self.a_log, -1.0, None, ALU.mult))
                dve.tensor_scalar(self.t[2], z, 1.0, None, ALU.add).then_inc(m["s_w"], 1)
                w.next(m["s_w"])
                own.do(dve.tensor_scalar(self.t[0], self.t[2], 1.0, None, ALU.subtract))
                own.join()
                own.do(dve.tensor_scalar(self.dt, self.t[0], 0.0, None, ALU.is_equal))
                own.join()
                own.do(dve.tensor_tensor(self.t[0], self.t[0], self.dt, ALU.add))
                own.join()
                own.do(dve.reciprocal(self.t[0], self.t[0]))
                own.do(dve.tensor_tensor(self.dt, self.dt, z, ALU.mult))
                own.join()
                own.do(dve.tensor_tensor(self.t[0], self.t[0], z, ALU.mult))
                own.do(dve.scalar_tensor_tensor(self.dt, self.t[4], 0.0, self.dt, ALU.max, ALU.add))
            if n == 3:
                w.next(m["s_ln"])
                own.join()
                own.do(dve.tensor_tensor(self.t[0], self.t[0], self.t[3], ALU.mult))
                own.join()
                own.do(dve.tensor_tensor(self.dt, self.dt, self.t[0], ALU.add))
                own.join()
                dve.tensor_tensor(self.a, self.dt, self.a_log.unsqueeze(1).to_broadcast([P, NT + 1, SH]), ALU.mult)\
                   .then_inc(m["s_a"], 1)
            if n == 5:
                w.next(m["s_cs"])
                for t in (0, 1, self.M):
                    rows = self.tile(t)[1]
                    own.do(dve.tensor_copy(self.sums[0:rows, 0, t, :], k.acc[3][0:rows, t * SH:(t + 1) * SH]))
                    own.do(dve.tensor_copy(self.sums[:, 1, t, :], k.acc[3][:, 96 + t * SH:96 + (t + 1) * SH]))
                own.join()
                dve.tensor_tensor(self.sums[:, 2, :, :], self.sums[:, 1, :, :], self.sums[:, 0, :, :], ALU.subtract)\
                   .then_inc(m["s_diff"], 1)
        own.join()
        w.next(m["s_xtok"], self.XS)
        w.next(m["s_exp2"])
        w.next(m["s_silu"], SLOTS)
        for t in range(NT):
            own.do(dve.tensor_tensor(self.heads(self.y[:, t, :]), self.heads(self.x[:, t, :]),
                                     self.per_head(self.d_skip), ALU.mult))
        own.join()
        for t in (0, 1, self.M):
            rows = self.tile(t)[1]
            xt = self.heads(self.x[0:rows, t, :])
            own.do(dve.tensor_tensor(xt, xt, self.per_head(self.dt[0:rows, t, :], rows), ALU.mult))
        own.join()
        for b, t in ((1, self.M), (0, 0)):
            rows = self.tile(t)[1]
            dve.tensor_tensor(self.heads(self.xdecay[0:rows, b, :]), self.heads(self.x[0:rows, t, :]),
                              self.per_head(self.sums[0:rows, 2, t, :], rows), ALU.mult).then_inc(m["s_xdt"], 1)
        dve.wait_ge(k.evac, before + self.CONVS + 3 * self.SC)
        taps = self.SC_TAPS
        for g in range(self.SC):
            own.do(dve.tensor_tensor(self.m[:, g, taps - 1:], self.m[:, g, taps - 1:], self.sc_x[:, g, :], ALU.mult))
        own.join()
        for g in range(self.SC):
            own.do(dve.tensor_scalar(self.sc_y[:, g, :], self.m[:, g, META:META + T], self.sc_w[:, g, 0:1], None,
                                     ALU.mult))
        for tap in range(1, taps):
            own.join()
            for g in range(self.SC):
                own.do(dve.scalar_tensor_tensor(self.sc_y[:, g, :], self.m[:, g, META + tap:META + tap + T],
                                                self.sc_w[:, g, tap:tap + 1], self.sc_y[:, g, :], ALU.mult, ALU.add))
        own.join()
        own.do(dve.tensor_tensor(self.sc_y, self.sc_y, self.sc_b[:, :, META:], ALU.mult))
        for t in range(NT):
            w.next(m["s_cb"])
            dve.tensor_tensor(self.cb[:, t, :, :], k.acc[2 + t][:, :].rearrange("p (g l) -> p g l", g=SG),
                              self.tri.unsqueeze(1).to_broadcast([P, SG, P]), ALU.mult).then_inc(m["s_cbm"], 1)
        for t in range(NT):
            w.next(m["s_st"])
            if t:
                own.do(dve.tensor_tensor(self.heads(self.state), self.heads(self.state),
                                         self.per_head(self.sums[:, 1, 0, :]), ALU.mult))
                own.join()
            for g in range(SG):
                cut = slice(g * self.GW, (g + 1) * self.GW)
                src = self.banks[g][:, 0:self.GW]
                if t:
                    ins = dve.tensor_tensor(self.state[:, cut], self.state[:, cut], src, ALU.add)
                else:
                    ins = dve.tensor_copy(self.state[:, cut], src)
            ins.then_inc(m["s_state"], 1)
            w.next(m["s_state"])
            w.next(m["s_yoff"])
            for g in range(SG):
                cut = slice(g * self.GW, (g + 1) * self.GW)
                ins = dve.tensor_tensor(self.heads(self.tmp[:, cut]), self.heads(k.acc[g][:, 0:self.GW]),
                                        self.per_head(self.sums[:, 0, t, g * SR:(g + 1) * SR]), ALU.mult)
            ins.then_inc(m["s_yoffd"], 1)
            w.next(m["s_yoffd"])
            own.do(dve.tensor_tensor(self.y[:, t, :], self.y[:, t, :], self.tmp, ALU.add))
            own.join()
        units = SH // self.UNIT

        def decays(n):
            t, u = divmod(n, units)
            if n >= 2:
                w.next(m["s_seg"])
            for r in range(self.UNIT):
                h = u * self.UNIT + r
                ins = dve.tensor_scalar(self.am[n % 2][:, r, :], self.after, self.a[:, t, h:h + 1], None, ALU.mult)
            ins.then_inc(m["s_am"], 1)

        decays(0)
        for n in range(NT * units):
            t, u = divmod(n, units)
            if n + 1 < NT * units:
                decays(n + 1)
            w.next(m["s_E"])
            if n >= 2:
                w.next(m["s_ydiag"])
            g = u * self.UNIT // SR
            dve.tensor_tensor(self.weighted[n % 2], self.e[n % 2],
                              self.cb[:, t, g, :].unsqueeze(1).to_broadcast([P, self.UNIT, P]), ALU.mult)\
               .then_inc(m["s_P"], 1)
            if u == units - 1:
                dve.wait_ge(m["s_ydiag"], n + 1)
                for g in range(SG):
                    cut = slice(g * self.GW, (g + 1) * self.GW)
                    ins = dve.tensor_tensor(self.y[:, t, cut], self.y[:, t, cut], k.acc[g][:, 0:self.GW], ALU.add)
                ins.then_inc(m["s_ysum"], 1)
        w.next(m["s_ysum"], 2)
        dve.wait_ge(k.evac, before + k.count["s_in"])
        dve.tensor_tensor(self.y, self.y, self.z, ALU.mult).then_inc(m["s_gated"], 1)
        w.next(m["s_msq"])
        dve.tensor_scalar(self.var, self.msq, 1.0 / self.GW, RMS_EPS, ALU.mult, ALU.add).then_inc(k.var, 1)
        w.next(k.std)
        own.do(dve.reciprocal(self.inv, self.std))
        own.join()
        for t in range(NT):
            for g in range(SG):
                cut = slice(g * self.GW, (g + 1) * self.GW)
                n = t * SG + g
                ins = dve.scalar_tensor_tensor(self.y[:, t, cut], self.y[:, t, cut], self.inv[:, n:n + 1],
                                               self.gain[:, cut], ALU.mult, ALU.mult)
        ins.then_inc(m["s_y"], 1)
        first = k.first["s_out"]
        w.next(m["y_ready"], 6)
        for n in range(k.count["s_out"]):
            src = self.yT[:, n, :] if n < self.XS else self.sc_y[:, n - self.XS, :]
            e.coef(src, Slab(first + n))


MIXERS = {"ab": MixAB, "c": MixC, "s": MixS}


def build(nc, dram, out, stages):
    with ExitStack() as ctx:
        k = Kernel(nc, ctx, dram, out, stages)
        block = ctx.enter_context(nc.Block())

        @block.sync
        def _(sp):
            sync_program(k, sp)

        @block.gpsimd
        def _(pool):
            gpsimd_program(k, pool)

        @block.scalar
        def _(act):
            scalar_program(k, act)

        @block.tensor
        def _(pe):
            tensor_program(k, pe)

        @block.vector
        def _(dve):
            vector_program(k, dve)


def columns(w):
    n = w.shape[1] // P
    return np.ascontiguousarray(w.reshape(DC, P, n, P).transpose(2, 1, 0, 3)).reshape(n, P, D)


def arrange(inputs):
    a = {name: np.asarray(v) for name, v in inputs.items()}
    d = {"x": a["x"][0]}
    w = a["ab_w_in"][0]
    half = [np.concatenate([np.arange(at + h * 64 + lo, at + h * 64 + lo + 32) for h in range(RH)])
            for lo in (0, 32) for at in (512, 768)]
    d["ab_in"] = columns(w[:, np.concatenate([np.arange(512), *half, np.arange(1024, 2048)])])
    d["ab_out"] = a["ab_w_out"][0].reshape(8, P, D)
    w = a["c_w_in"][0]
    order = np.concatenate([np.arange(D, 2 * D), np.arange(D), np.arange(2 * D, 4 * D)])
    d["c_in"] = columns(w[:, order])
    d["c_out"] = a["c_w_out"][0].reshape(8, P, D)
    for n, (wq, sub, u, v) in enumerate(((a["peer_w_q"][0], None, a["peer_u"][0], a["peer_v"][0]),
                                         (a["peer_w_q"][1], None, a["peer_u"][1], a["peer_v"][1]),
                                         (a["w_q_2"][0], None, a["expert_u_2"][0], a["expert_v_2"][0]))):
        d[f"wq{n}"] = columns(wq)
        d[f"u{n}"] = np.ascontiguousarray(u.reshape(KEYS, KEYS, DC, P).transpose(1, 3, 2, 0)).reshape(KEYS, P, D)
        d[f"v{n}"] = v.reshape(KEYS, KEYS, D)
    keys = np.concatenate([a["peer_sub_keys"], a["sub_keys_2"]])
    d["keys"] = np.ascontiguousarray(keys.reshape(3, HP, KEYS, P).transpose(0, 3, 1, 2))
    d["ln_g"] = a["ln_g"].reshape(4, D)
    d["ln_b"] = a["ln_b"].reshape(4, D)
    d["g_mix"], d["g_ffn"], d["g_final"] = a["g_mix_2"], a["g_ffn_2"], a["g_final_2"][None]
    d["pool_w"] = np.ascontiguousarray(a["pool_w"][0].transpose(1, 0, 2))
    d["pool_scale"] = np.ascontiguousarray(a["pool_scale"][0].reshape(POOLG, P).T)
    d["ret_g"] = a["ret_norm_g"]
    d["ident"] = np.eye(P, dtype=np.float32)
    d["iota"] = np.tile(np.arange(P, dtype=np.float32), (P, 1))
    inv = 1.0 / (np.float32(10000.0) ** np.linspace(0.0, 1.0, 32, dtype=np.float32))
    angle = np.arange(T, dtype=np.float32)[None, :] * inv.astype(np.float32)[:, None]
    d["cos"] = np.tile(np.cos(angle), (RH, 1)).astype(np.float32)
    d["sin"] = np.tile(np.sin(angle), (RH, 1)).astype(np.float32)
    count = np.arange(1, T + 1)
    d["pool_count"] = np.tile(np.stack([1.0 / np.minimum(count, n) for n in (2, 4, 8, 16)]), (P, 1, 1))\
        .astype(np.float32)
    log_gamma = np.log1p(-np.exp2(-5.0 - np.arange(RH)))
    diff = np.arange(T)[None, :] - np.arange(P)[:, None]
    decay = np.where(diff >= 0, np.exp(log_gamma[:, None, None] * np.maximum(diff, 0)), 0.0) * 64 ** -0.5
    d["ret_decay"] = np.ascontiguousarray(np.concatenate([decay, decay[:, :, :P]], 2).transpose(1, 0, 2))\
        .astype(np.float32)
    d["hgrn_lb"] = np.ascontiguousarray(a["hgrn_lb"].reshape(2, CH, P).transpose(2, 0, 1))
    d["hgrn_g"] = a["hgrn_norm_g"]
    d["restart"] = np.tile((np.arange(T) % CCH != 0).astype(np.float32), (P, 1))
    s, c = np.arange(P)[:, None], np.arange(P)[None, :]
    d["chunk_causal"] = ((s // CCH == c // CCH) & (c >= s)).astype(np.float32)
    w = a["w_in_2"][0]
    at_z, at_x, at_dt, at_sc = 0, SW, SW + MixS.CONVS * P, SW + MixS.CONVS * P + SH
    order = [np.arange(at_x, at_dt), np.arange(at_sc + 512, at_sc + 1536), np.arange(at_sc, at_sc + 512),
             np.arange(at_z, at_x)]
    d["s_in"] = columns(w[:, np.concatenate(order)])
    d["s_out"] = a["w_out_2"][0].reshape(16, P, D)
    d["dt_w"] = np.ascontiguousarray(w[:, at_dt:at_sc].reshape(DC, P, SH).transpose(1, 0, 2))
    d["meta"] = a["meta_tokens_2"]
    d["conv_w"] = np.ascontiguousarray(a["conv_ssd_w_2"][0].reshape(4, MixS.CONVS, P).transpose(2, 1, 0))
    d["conv_b"] = np.ascontiguousarray(a["conv_ssd_b_2"][0].reshape(MixS.CONVS, P).T)
    d["sc_w"] = np.ascontiguousarray(a["conv_sc_w_2"][0].reshape(3, 4, P).transpose(2, 1, 0))
    d["dt_bias"], d["a_log"], d["d_skip"] = a["dt_bias_2"], a["a_log_2"], a["d_skip_2"]
    d["ssd_norm"] = a["ssd_norm_w_2"]
    d["tri"] = (s <= c).astype(np.float32)
    d["after"] = (s > c).astype(np.float32)
    return d


def kernel(**inputs):
    import numpy as _np
    import concourse.bacc as _bacc
    from concourse import mybir as _mybir
    from concourse.bass_utils import run_bass_kernel_spmd as _run

    nc = _bacc.Bacc("TRN2", target_bir_lowering=False, num_devices=1)
    arrays = {f"in_{name}": _np.ascontiguousarray(v) for name, v in arrange(inputs).items()}
    dram = {name[3:]: nc.dram_tensor(name, v.shape, _mybir.dt.from_np(v.dtype), kind="ExternalInput").ap()
            for name, v in arrays.items()}
    out = nc.dram_tensor("out_h", (T, D), _mybir.dt.float32, kind="ExternalOutput").ap()
    build(nc, dram, out, STAGES)
    r = _run(nc, [arrays], core_ids=[0])
    return r.results[0]["out_h"].reshape(1, T, D)
```

```python
from contextlib import ExitStack

import numpy as np

import concourse.bass as bass
from concourse import mybir

F32 = mybir.dt.float32
F32R = mybir.dt.float32r
BF16 = mybir.dt.bfloat16
U32 = mybir.dt.uint32
ALU = mybir.AluOpType
ACT = mybir.ActivationFunctionType
AX = mybir.AxisListType.X

P = 128
D = 1024
DC = D // P
T = 256
NT = T // P
META = 16
TM = T + META
SLOTS = 3
NEG = -3.0e38

HEADS = 8
HP = 2 * HEADS
KEYS = 128
TOPK = 16
EARLY = KEYS // 2
ROUTED_AT = 60
EXP_AT = 54
SELS = HEADS * TOPK
UNROLL = 2 * SLOTS
PARTS = 3
GB = 4
BATCHES = T // GB
HEAD = BATCHES % UNROLL
TURNS = BATCHES // UNROLL
VREST = KEYS - BATCHES
assert BATCHES == KEYS - EARLY and HEAD > SLOTS and EXP_AT % UNROLL == 0 and VREST % SLOTS == 1

POOLG = 4
RH = 4
CH = 8
CCH = 32
SG, SR, SP_ = 4, 6, 64
SH = SG * SR
SW = SH * SP_
DN_ALPHA = 4.0 ** 0.25
LN_EPS = 1e-5
RMS_EPS = 1e-6

STREAM = [("ab_in", 8, "col"), ("ab_wide", 8, "wide"), ("ab_out", 8, "row"),
          ("wq0", HP, "col"), ("u0", KEYS, "col"), ("v0", KEYS, "row"),
          ("c_in", 16, "col"), ("c_wide", 16, "wide"), ("c_out", 8, "row"),
          ("wq1", HP, "col"), ("u1", KEYS, "col"), ("v1", KEYS, "row"),
          ("s_in", 32, "col"), ("s_wide", 12, "wide"), ("s_out", 16, "row"),
          ("wq2", HP, "col"), ("u2", KEYS, "col"), ("v2", KEYS, "row")]

STAGES = ("ab", "peer0", "c", "peer1", "s", "peer2")
STAGE_OF = {f"{x}_{part}": x for x in ("ab", "c", "s") for part in ("in", "wide", "out")} | {
    f"{x}{n}": f"peer{n}" for x in ("wq", "u", "v") for n in range(3)}


class Slab:

    def __init__(self, base, turn=None):
        self.base, self.turn = base, turn

    def __add__(self, n):
        return Slab(self.base + n, self.turn)

    def __sub__(self, n):
        return Slab(self.base - n, self.turn)

    @property
    def slot(self):
        return self.base % SLOTS

    def index(self, less=0):
        n = self.base - less
        return n if self.turn is None else self.turn * SLOTS + n

    def half(self):
        return self.base // 2 if self.turn is None else self.turn // 2 * SLOTS + self.base // 2

    def round(self, times=1, more=0):
        n = (self.base // SLOTS) * times + more
        return n if self.turn is None else self.turn * times + n


class Steps:

    def __init__(self, eng, sem):
        self.eng, self.sem, self.n = eng, sem, 0

    def do(self, ins):
        ins.then_inc(self.sem, 1)
        self.n += 1

    def join(self):
        self.eng.wait_ge(self.sem, self.n)


class Kernel:

    def __init__(self, nc, ctx, dram, out, stages):
        self.nc, self.d, self.out = nc, dram, out
        self.stages = stages
        self.first, self.kind, self.cols_before, self.rows_before = {}, [], [0], [0]
        self.count = {}
        for name, n, kind in STREAM:
            if STAGE_OF[name] not in stages:
                continue
            self.count[name] = n
            self.first[name] = len(self.kind)
            for _ in range(n):
                self.kind.append(kind)
                self.cols_before.append(self.cols_before[-1] + (kind == "col"))
                self.rows_before.append(self.rows_before[-1] + (kind == "row"))
        self.total = len(self.kind)

        def sb(name, shape, dt=F32):
            return ctx.enter_context(nc.sbuf_tensor(name, shape, dt))

        def ps(name, shape):
            return ctx.enter_context(nc.psum_tensor(name, shape, F32))

        def sem(name):
            return ctx.enter_context(nc.semaphore(name))

        self.ring = [sb(f"ring{i}", [P, D]) for i in range(SLOTS)]
        self.w_hi = [sb(f"w_hi{i}", [P, D], F32R) for i in range(SLOTS)]
        self.w_lo = [sb(f"w_lo{i}", [P, D], F32R) for i in range(SLOTS)]
        self.x_hi = sb("x_hi", [P, DC, TM], F32R)
        self.x_lo = sb("x_lo", [P, DC, TM], F32R)
        self.h = sb("h_tok", [P, NT, D])
        self.big = sb("work", [P, KEYS * T])
        self.c_hi = [sb(f"c_hi{i}", [P, T], F32R) for i in range(SLOTS)]
        self.c_lo = [sb(f"c_lo{i}", [P, T], F32R) for i in range(SLOTS)]
        self.oh1_room = sb("onehot_i1", [P, 2, GB, P])
        self.oh2_room = sb("gated_onehot_i2", [P, 2, GB, P])
        room = self.oh1_room[:, :, :, :].rearrange("p j t i -> p (j t i)")
        self.oh1 = room[:, 0:GB * P].bitcast(BF16).rearrange("p (j t i) -> p j t i", j=2, t=GB)
        self.gate = room[:, GB * P:GB * P + PARTS * T // 2].bitcast(BF16).rearrange("p (n t) -> p n t", n=PARTS)
        room = self.oh2_room[:, :, :, :].rearrange("p j t i -> p (j t i)")
        self.oh2 = room[:, 0:GB * PARTS * EARLY].bitcast(BF16)\
            .rearrange("p (j t n i) -> p j t n i", j=2, t=GB, n=PARTS)
        self.rest = room[:, 0:T]
        self.i1 = sb("i1", [P, T], BF16)
        self.neg_i1 = sb("neg_i1", [P, T])
        self.i2 = sb("i2", [P, T])
        self.ident = sb("ident", [P, P])
        self.iota = sb("iota", [P, P])
        self.iota_b = sb("iota_bf16", [P, P], BF16)
        self.small = sb("small", [P, 128])
        self.col = [ps(f"col{i}", [P, 512]) for i in range(SLOTS)]
        self.misc = ps("misc", [P, 512])
        self.acc = [ps(f"acc{i}", [P, 512]) for i in range(4)]

        self.load = [sem(f"slab_loaded{i}") for i in range(SLOTS)]
        self.hi = [sem(f"hi_ready{i}") for i in range(SLOTS)]
        self.lo = [sem(f"lo_ready{i}") for i in range(SLOTS)]
        self.used = sem("slab_used")
        self.evac = sem("column_evacuated")
        self.const = sem("const_loaded")
        self.xload = sem("x_loaded")
        self.param = [sem(f"norm_param{i}_loaded") for i in range(3)]
        self.dve_step = sem("dve_step")
        self.act_step = sem("act_step")
        self.h_half = sem("h_first_half_ready")
        self.h_ready = sem("h_ready")
        self.xt = sem("x_transposed")
        self.xhi = sem("x_hi_ready")
        self.x_ready = sem("x_ready")
        self.rms_in = sem("rms_input_ready")
        self.summed = sem("residual_added")
        self.norms = self.norms_before(None)
        self.var = sem("variance_ready")
        self.sq = sem("squares_ready")
        self.std = sem("std_ready")
        self.stored = sem("output_stored")
        self.keys = sem("keys_loaded")
        self.meta = sem("meta_loaded")
        self.s_full = sem("scores_full")
        self.s_evac = sem("scores_evacuated")
        self.m_ready = sem("gate_max_subtracted")
        self.e_ready = sem("gate_exp_ready")
        self.routed = sem("routed")
        self.rt = sem("routing_transposed")
        self.i1_ready = sem("neg_i1_ready")
        self.oh_ready = sem("vector_onehots_ready")
        self.oh1_abs = sem("onehot_distance")
        self.oh1_ready = sem("scalar_onehot_ready")
        self.g_full = sem("gate_matrix_full")
        self.g_used = sem("gate_matrix_used")
        self.coef = [sem(f"coef_ready{i}") for i in range(SLOTS)]
        self.coef_h = sem("coef_hi_ready")
        self.mload = [sem(f"mixer_const{i}_loaded") for i in range(3)]
        self.m = {name: sem(name) for name in (
            "pool_ready", "pool_mixed", "rope_ready", "ret_scores", "ret_probs", "ret_out", "ret_y", "ret_yT",
            "y_ready", "ab_wide", "c_wide", "s_wide", "pool_out",
            "c_lb", "c_lbe", "c_f", "c_logf", "c_b", "c_exps", "c_diff", "c_expdiff", "c_kout", "c_koutT", "c_ktok", "c_qk", "c_scores", "c_probs",
            "c_state_psum", "c_state", "c_out", "c_msq", "c_y", "c_yT",
            "s_dtw", "s_conv", "s_silu", "s_xsT", "s_xtok", "s_dt", "s_dtb", "s_exps", "s_w", "s_ln", "s_a", "s_cs", "s_diff", "s_exp2", "s_xdt", "s_btokT", "s_btok", "s_cb", "s_cbm",
            "s_st", "s_state", "s_yoff", "s_yoffd", "s_am", "s_seg", "s_E", "s_P", "s_ydiag", "s_ysum", "s_gated", "s_msq", "s_y", "s_yT", "s_y_ready")}

    def cols(self, s):
        n = self.cols_before[s.base]
        return n if s.turn is None else s.turn * SLOTS + n

    def after_s(self, name):
        return "s" in self.stages and self.stages.index("s") < self.stages.index(name)

    def rows_in_slot(self, s, more=0):
        n = sum(self.kind[m] == "row" for m in range(s.slot, s.base, SLOTS)) + more
        return n if s.turn is None else s.turn + n

    def rows(self, s, more=0):
        n = self.rows_before[s.base] + more
        return n if s.turn is None else s.turn * SLOTS + n

    def norms_before(self, stage):
        n = 0
        for name in self.stages:
            if name == stage:
                return n
            n += 2 if name == "s" else 1
        return n

    def gates_before(self, layer, late):
        peers = sum(name[:4] == "peer" for name in self.stages[:self.stages.index(f"peer{layer}")])
        return (2 * peers + late) * BATCHES

    def scalar_onehots(self, layer):
        return self.gates_before(layer, 0) // 4

    def gate_pass(self, layer, late):
        if late:
            return self.col, EARLY, self.gates_before(layer, 1)
        return self.acc, 0, self.gates_before(layer, 0)


class Waits:

    def __init__(self, eng):
        self.eng, self.seen = eng, {}

    def next(self, sem, n=1):
        self.skip(sem, n)
        self.eng.wait_ge(sem, self.seen[sem.name])

    def skip(self, sem, n):
        self.seen[sem.name] = self.seen.get(sem.name, 0) + n


G_AT = (0, 2 * D, 4 * D)
NORMED = 6 * D
JUNK = 9 * D
MIX = 10 * D
QT = EARLY * T
SCORES = QT + HP * T
KEYT = SCORES + NT * HP * KEYS
ROUTE = KEYT
CAND = QT
PICK = CAND + 2048
assert KEYT + HP * KEYS <= KEYS * T


def view(t, at, *shape, p=P):
    n = int(np.prod(shape))
    v = t[0:p, at:at + n]
    if len(shape) == 1:
        return v
    names = "abcd"[:len(shape)]
    sizes = dict(zip(names[1:], shape[1:], strict=True))
    return v.rearrange(f"p ({' '.join(names)}) -> p {' '.join(names)}", **sizes)


class Lay:

    def __init__(self, k, at, end=KEYS * T):
        self.k, self.at, self.end = k, at, end

    def __call__(self, *shape, p=P):
        v = view(self.k.big, self.at, *shape, p=p)
        self.at += int(np.prod(shape))
        assert self.at <= self.end, (self.at, self.end)
        return v


def slab_view(k, s):
    return (k.w_hi[s.slot][:, :].rearrange("p (c n) -> p c n", c=DC),
            k.w_lo[s.slot][:, :].rearrange("p (c n) -> p c n", c=DC))


def sync_program(k, sp):
    w = Waits(sp)

    def put(name, s, n):
        if s.turn is not None or s.base >= SLOTS:
            sp.wait_ge(k.lo[s.slot], s.round())
        src = k.d[name][:, n, :] if name[0] == "v" else k.d[name][n, :, :]
        sp.dma_start(k.ring[s.slot][:, :], src).then_inc(k.load[s.slot], 16)

    def stream(name, at=0, to=None):
        first = k.first[name]
        to = k.count[name] if to is None else to
        rounds = (to - at) // SLOTS
        if rounds > 1:
            with sp.Fori(0, rounds) as i:
                for p in range(SLOTS):
                    put(name, Slab(first + at + p, i), i * SLOTS + (at + p))
            at += rounds * SLOTS
        for n in range(at, to):
            put(name, Slab(first + n), n)

    def row(name, dst, i, sem):
        src = k.d[name][i:i + 1, :]
        sp.dma_start(dst, src.to_broadcast([P, src.shape[1]])).then_inc(sem, 16)

    def norm_param(slot, gain, bias=None):
        row(gain[0], view(k.big, G_AT[slot], D), gain[1], k.param[slot])
        if bias:
            row(bias[0], view(k.big, G_AT[slot] + D, D), bias[1], k.param[slot])

    def load(dst, name, i):
        sp.dma_start(dst, k.d[name]).then_inc(k.mload[i], 16)

    def params(stage):
        if stage == "ab":
            ab = MixAB(k)
            for dst, name in ((ab.cos, "cos"), (ab.sin, "sin"), (ab.count, "pool_count"), (ab.pool_w, "pool_w"),
                              (ab.pool_scale, "pool_scale"), (ab.decay, "ret_decay")):
                load(dst, name, 0)
            row("ret_g", ab.gain, 0, k.mload[0])
            norm_param(0, ("ln_g", 0), ("ln_b", 0))
        elif stage == "peer0":
            norm_param(1, ("ln_g", 1), ("ln_b", 1))
        elif stage == "c":
            norm_param(2, ("ln_g", 2), ("ln_b", 2))
            c = MixC(k)
            load(c.bound, "hgrn_lb", 1)
            load(c.restart, "restart", 1)
            load(c.causal.bitcast(F32), "chunk_causal", 1)
            row("hgrn_g", c.gain, 0, k.mload[1])
        elif stage == "peer1":
            norm_param(1, ("ln_g", 3), ("ln_b", 3))
        elif stage == "s":
            s = MixS(k)
            sp.dma_start(s.meta, k.d["meta"]).then_inc(k.meta, 16)
            norm_param(2, ("g_mix", 0))
            norm_param(0, ("g_ffn", 0))
            for dst, name in s.loads():
                load(dst, name, 2)
            for dst, name in s.rows():
                row(name, dst, 0, k.mload[2])
        else:
            norm_param(1, ("g_final", 0))

    def peer(n):
        layer = int(k.stages[n][4])
        stream(f"wq{layer}", SLOTS if n == 0 else 0)
        if k.norms_before(f"peer{layer}"):
            sp.wait_ge(k.h_ready, k.norms_before(f"peer{layer}"))
        sp.dma_start(view(k.big, KEYT, HP, KEYS), k.d["keys"][layer]).then_inc(k.keys, 16)
        stream(f"u{layer}")
        stream(f"v{layer}", 0, EARLY + 6)
        read = Slab(k.first[f"v{layer}"] + EARLY)
        sp.wait_ge(k.coef[read.slot], k.rows_in_slot(read, 1))
        for stage in k.stages[n:n + 2]:
            params(stage)
        stream(f"v{layer}", EARLY + 6)

    sp.dma_start(k.ident[:, :], k.d["ident"]).then_inc(k.const, 16)
    sp.dma_start(k.iota[:, :], k.d["iota"]).then_inc(k.const, 16)
    for t in range(NT):
        sp.dma_start(k.h[:, t, :], k.d["x"][t * P:(t + 1) * P, :]).then_inc(k.xload, 16)
    head = "wq" + k.stages[0][4] if k.stages[0][:4] == "peer" else f"{k.stages[0]}_in"
    for n in range(SLOTS):
        put(head, Slab(n), n)
    if k.stages[0][:4] != "peer":
        params(k.stages[0])
    for n, stage in enumerate(k.stages):
        if stage[:4] == "peer":
            peer(n)
        else:
            stream(f"{stage}_in", SLOTS if n == 0 else 0)
            stream(f"{stage}_wide")
            stream(f"{stage}_out")
    sp.wait_ge(k.h_ready, k.norms)
    for t in range(NT):
        src = view(k.big, NORMED + t * D, D) if k.stages[-1] in ("s", "peer2") else k.h[:, t, :]
        sp.dma_start(k.out[t * P:(t + 1) * P, :], src).then_inc(k.stored, 16)
    sp.wait_ge(k.stored, 16 * NT)


def split_rest(k, eng, s):
    eng.wait_ge(k.hi[s.slot], s.round(1, 1))
    eng.tensor_tensor(k.w_lo[s.slot][:, :], k.ring[s.slot][:, :], k.w_hi[s.slot][:, :].bitcast(F32),
                      ALU.subtract).then_inc(k.lo[s.slot], 1)


def gpsimd_program(k, pool):
    def run(name, at, rounds):
        with pool.Fori(0, rounds) as i:
            for p in range(SLOTS):
                split_rest(k, pool, Slab(k.first[name] + at + p, i))

    def run_third(name, at, rounds):
        with pool.Fori(0, rounds) as i:
            split_rest(k, pool, Slab(k.first[name] + at + 2, i))

    def some(name, at, to):
        for n in range(at, to):
            split_rest(k, pool, Slab(k.first[name] + n))

    def stage(name, count):
        run(name, 0, count // SLOTS)
        some(name, count - count % SLOTS, count)

    def peer(layer):
        stage(f"wq{layer}", HP)
        u, v = f"u{layer}", f"v{layer}"
        stage(u, KEYS)
        run(v, 0, BATCHES // SLOTS)
        some(v, BATCHES - BATCHES % SLOTS, BATCHES + 1)
        run_third(v, BATCHES + 1, VREST // SLOTS)

    for name in k.stages:
        if name[:4] == "peer":
            peer(int(name[4]))
        else:
            for part in ("in", "wide", "out"):
                stage(f"{name}_{part}", k.count[f"{name}_{part}"])


class Tensor:
    def __init__(self, k, pe):
        self.k, self.pe, self.w = k, pe, Waits(pe)

    def split_matmuls(self, out, a, b, start, stop, **kw):
        pe = self.pe
        pe.matmul(out, a[0], b[0], start=start, stop=False, **kw)
        pe.matmul(out, a[0], b[1], start=False, stop=False, **kw)
        return pe.matmul(out, a[1], b[0], start=False, stop=stop, **kw)

    def slab_ready(self, s):
        self.pe.wait_ge(self.k.lo[s.slot], s.round(1, 1))

    def bank_free(self, s):
        k = self.k
        if s.base >= SLOTS and k.cols_before[s.base - SLOTS + 1]:
            self.pe.wait_ge(k.evac, k.cols(s - (SLOTS - 1)))

    def features(self, s, n=T, fresh=False):
        k = self.k
        self.bank_free(s)
        self.slab_ready(s)
        hi, lo = slab_view(k, s)
        for c in range(DC):
            if fresh and c % 2 == 0:
                self.w.next(k.x_ready)
            ins = self.split_matmuls(k.col[s.slot][:, 0:n], (hi[:, c, :], lo[:, c, :]),
                                     (k.x_hi[:, c, 0:n], k.x_lo[:, c, 0:n]), c == 0, c == DC - 1)
        ins.then_inc(k.used, 1)

    def wide(self, s, c, banks, at=0):
        k = self.k
        self.slab_ready(s)
        for t in range(NT):
            cut = slice(at + t * P, at + (t + 1) * P)
            for half in range(2):
                n = slice(half * 512, (half + 1) * 512)
                ins = self.split_matmuls(banks[t * 2 + half][:, :], (k.x_hi[:, c, cut], k.x_lo[:, c, cut]),
                                         (k.w_hi[s.slot][:, n], k.w_lo[s.slot][:, n]), c == 0, c == DC - 1)
        ins.then_inc(k.used, 1)

    def narrow(self, s, c, banks, at=0):
        k = self.k
        self.slab_ready(s)
        for t in range(NT):
            cut = slice(at + t * P, at + (t + 1) * P)
            for j in range(2):
                n = slice(j * 512, (j + 1) * 512)
                ins = self.split_matmuls(banks[t][:, :], (k.x_hi[:, c + j, cut], k.x_lo[:, c + j, cut]),
                                         (k.w_hi[s.slot][:, n], k.w_lo[s.slot][:, n]), c + j == 0, c + j == DC - 1)
        ins.then_inc(k.used, 1)

    def rows(self, s, y_hi, y_lo, start, stop):
        k = self.k
        self.slab_ready(s)
        for t in range(NT):
            for half in range(2):
                cut, n = slice(t * P, (t + 1) * P), slice(half * 512, (half + 1) * 512)
                ins = self.split_matmuls(k.acc[t * 2 + half][:, :], (y_hi[:, cut], y_lo[:, cut]),
                                         (k.w_hi[s.slot][:, n], k.w_lo[s.slot][:, n]), start, stop,
                                         skip_group_check=True)
        ins.then_inc(k.used, 1)

    def transpose_x(self, src, meta, norms=None):
        k, pe = self.k, self.pe
        for b in range(4):
            if b == 2 and norms:
                pe.wait_ge(k.h_ready, norms)
            for c in range(2):
                for t in range(NT):
                    ins = pe.transpose(k.acc[b][:, c * T + t * P:c * T + (t + 1) * P],
                                       src[t][:, (2 * b + c) * P:(2 * b + c + 1) * P], k.ident[:, :])
            ins.then_inc(k.xt, 1)
        if meta is not None:
            for c in range(DC):
                ins = pe.transpose(k.misc[:, c * META:(c + 1) * META], meta[:, c * P:(c + 1) * P],
                                   k.ident[0:META, 0:META])
            ins.then_inc(k.xt, 1)

    def peer(self, layer):
        k, pe, w = self.k, self.pe, self.w
        first = k.first[f"wq{layer}"]
        for n in range(HP):
            self.features(Slab(first + n), fresh=n == 0)
        q = view(k.big, QT, HP, T)
        keys = view(k.big, KEYT, HP, KEYS)
        w.next(k.keys, 16)
        pe.wait_ge(k.evac, k.cols_before[first + HP])
        for t in range(NT):
            for quad in range(4):
                if t:
                    w.next(k.s_evac)
                for j in range(4):
                    hp = quad * 4 + j
                    ins = pe.matmul(k.acc[quad][:, j * KEYS:(j + 1) * KEYS], q[:, hp, t * P:(t + 1) * P],
                                    keys[:, hp, :], start=True, stop=True)
                ins.then_inc(k.s_full, 1)
        w.next(k.s_evac, 4)

        first = k.first[f"u{layer}"]
        with pe.Fori(0, ROUTED_AT // SLOTS) as i:
            for p in range(SLOTS):
                self.features(Slab(first + p, i))
        w.next(k.routed, NT)
        r = Route(k)
        for t in range(NT):
            pe.transpose(k.misc[:, t * P:(t + 1) * P], r.i1[t], k.ident[:, :])
            pe.transpose(k.acc[0][:, t * P:(t + 1) * P], r.gate[t], k.ident[:, :])
            ins = pe.transpose(k.acc[0][:, T + t * P:T + (t + 1) * P], r.i2[t], k.ident[:, :])
        ins.then_inc(k.rt, 1)
        for n in range(ROUTED_AT, EARLY):
            self.features(Slab(first + n))

        def gates(b, late, wait=True):
            banks, _, g0 = k.gate_pass(layer, late)
            pe.wait_ge(k.oh_ready, b.index() + (g0 + 1))
            if late and b.base % 2:
                pe.wait_ge(k.oh1_ready, b.half() + (k.scalar_onehots(layer) + 1))
            if wait:
                pe.wait_ge(k.g_used, b.index() + (g0 + 1 - SLOTS))
            for t in range(GB):
                for n in range(PARTS):
                    ins = pe.matmul(banks[b.slot][:, t * EARLY:(t + 1) * EARLY], k.oh1[:, b.base % 2, t, :],
                                    k.oh2[:, b.base % 2, t, n, :], start=n == 0, stop=n == PARTS - 1)
            ins.then_inc(k.g_full, 1)

        def gate_pass(late, slab):
            for n in range(HEAD):
                slab(n)
                gates(Slab(n), late, wait=n >= SLOTS)
            with pe.Fori(0, TURNS - 1) as i:
                for n in range(HEAD, HEAD + UNROLL):
                    slab(n, i * 2)
                    gates(Slab(n, i * 2), late)
            for n in range(BATCHES - UNROLL, BATCHES - 1):
                slab(n)
                gates(Slab(n), late)
            gates(Slab(BATCHES - 1), late)
            slab(BATCHES - 1)

        gate_pass(False, lambda n, i=None: self.features(Slab(first + EARLY + n, i)))

        values = k.first[f"v{layer}"]
        pe.wait_ge(k.g_used, k.gates_before(layer, 1))
        self.row_slab(Slab(values), start=True)
        pe.wait_ge(k.evac, k.cols_before[values])
        gate_pass(True, lambda n, i=None: None if n == 0 else self.row_slab(Slab(values + n, i)))
        first = values
        self.row_slab(Slab(first + BATCHES))
        with pe.Fori(0, VREST // SLOTS) as i:
            for p in range(SLOTS):
                self.row_slab(Slab(first + BATCHES + 1 + p, i))

    def row_slab(self, s, start=False, stop=False):
        k = self.k
        self.pe.wait_ge(k.coef[s.slot], k.rows_in_slot(s, 1))
        self.rows(s, k.c_hi[s.slot], k.c_lo[s.slot], start, stop)

    def row_stage(self, name, count, at=0, to=None):
        for n in range(at, count if to is None else to):
            self.row_slab(Slab(self.k.first[name] + n), n == 0, n == count - 1)


def tensor_program(k, pe):
    e = Tensor(k, pe)
    pe.wait_ge(k.const, 32)
    pe.wait_ge(k.xload, 16 * NT)
    for name in k.stages:
        if name == "s" or k.after_s(name):
            src = [view(k.big, NORMED + t * D, D) for t in range(NT)]
        else:
            src = [k.h[:, t, :] for t in range(NT)]
        meta = view(k.big, NORMED + 2 * D, D, p=META) if name == "s" else None
        norms = k.norms_before(name) + (name == "s")
        half = None if not norms or name == "s" or k.after_s(name) else norms
        if half:
            pe.wait_ge(k.h_half, half)
        elif norms:
            pe.wait_ge(k.h_ready, norms)
        e.transpose_x(src, meta, half)
        if name == "s":
            e.w.next(k.x_ready, 5)
        if name[:4] == "peer":
            e.peer(int(name[4]))
        else:
            MIXERS[name](k).tensor(e)


class Scalar:
    AHEAD = SLOTS

    def __init__(self, k, act):
        self.k, self.act, self.w = k, act, Waits(act)
        self.own = Steps(act, k.act_step)

    def split_lead(self, s):
        k, act = self.k, self.act
        if s.turn is None and s.base >= k.total:
            return
        if s.turn is not None or s.base >= SLOTS:
            act.wait_ge(k.used, s.index(SLOTS - 1))
        act.wait_ge(k.load[s.slot], s.round(16, 16))
        act.activation(k.w_hi[s.slot][:, :], k.ring[s.slot][:, :], ACT.Copy).then_inc(k.hi[s.slot], 1)

    def column(self, s, dst, func=ACT.Copy, n=T, src=None):
        k, act = self.k, self.act
        act.wait_ge(k.used, s.index(-1))
        src = k.col[s.slot][:, 0:n] if src is None else src(k.col[s.slot])
        act.activation(dst, src, func).then_inc(k.evac, 1)
        self.split_lead(s + self.AHEAD)

    def leads(self, first, count):
        for n in range(count):
            self.split_lead(Slab(first + n + self.AHEAD))

    def wide(self, last, parts, sem):
        k, act = self.k, self.act
        act.wait_ge(k.used, last + 1)
        for bank, dst, func in parts:
            act.activation(dst, bank[:, :], func).then_inc(sem, 1)

    def lead_x(self, meta=False):
        k, act, w = self.k, self.act, self.w
        at = META if meta else 0
        for b in range(4):
            w.next(k.xt)
            act.activation(k.x_hi[:, 2 * b:2 * b + 2, at:at + T],
                           k.acc[b][:, :].rearrange("p (c t) -> p c t", c=2), ACT.Copy).then_inc(k.xhi, 1)
        if meta:
            w.next(k.xt)
            act.activation(k.x_hi[:, :, 0:META], k.misc[:, 0:DC * META].rearrange("p (c t) -> p c t", c=DC),
                           ACT.Copy).then_inc(k.xhi, 1)

    def std(self, src=None, dst=None):
        k, act = self.k, self.act
        self.w.next(k.var)
        act.activation(k.small[:, 8:10] if dst is None else dst, k.small[:, 4:6] if src is None else src,
                       ACT.Sqrt).then_inc(k.std, 1)

    def squares(self, src, n):
        k, rows = self.k, src.shape[0]
        self.own.do(self.act.activation(view(k.big, JUNK, D, p=rows), src, ACT.Square,
                                        accum_out=k.small[0:rows, 40 + n:41 + n]))
        self.own.join()

    def rms(self, tiles, n=NT):
        k, act, w = self.k, self.act, self.w
        if n == NT:
            w.next(k.rms_in)
        self.squares(tiles[0], 0)
        act.activation(view(k.big, JUNK, D), tiles[1], ACT.Square, accum_out=k.small[:, 41:42]).then_inc(k.sq, 1)
        w.next(k.var)
        act.activation(k.small[:, 8:8 + n], k.small[:, 4:4 + n], ACT.Sqrt).then_inc(k.std, 1)

    def peer(self, layer):
        k, act, w = self.k, self.act, self.w
        first = k.first[f"wq{layer}"]
        q = view(k.big, QT, HP, T)
        for n in range(HP):
            self.column(Slab(first + n), q[:, n, :])
        scores = view(k.big, SCORES, NT, HP * KEYS)
        for t in range(NT):
            for quad in range(4):
                w.next(k.s_full)
                act.activation(scores[:, t, quad * 512:(quad + 1) * 512], k.acc[quad][:, :], ACT.Copy)\
                   .then_inc(k.s_evac, 1)

        first = k.first[f"u{layer}"]
        act_of = view(k.big, 0, KEYS, T)

        def expert(n, s):
            self.column(s, act_of[:, n, :], ACT.Gelu)

        with act.Fori(0, EXP_AT // UNROLL) as i:
            for p in range(UNROLL):
                expert(i * UNROLL + p, Slab(first + p, i * 2))
        r = Route(k)
        for t in range(NT):
            w.next(k.m_ready)
            act.activation(r.gate[t], r.gate[t], ACT.Exp).then_inc(k.e_ready, 1)
        for n in range(EXP_AT, ROUTED_AT + 1):
            expert(n, Slab(first + n))
        w.next(k.rt)
        act.activation(k.neg_i1[:, :], k.misc[:, 0:T], ACT.Copy, scale=-1.0).then_inc(k.i1_ready, 1)
        w.next(k.i1_ready)
        for n in range(ROUTED_AT + 1, EARLY + HEAD):
            expert(n, Slab(first + n))

        with act.Fori(0, (KEYS - EARLY - HEAD) // UNROLL) as i:
            for p in range(UNROLL):
                expert(i * UNROLL + (EARLY + HEAD + p), Slab(first + EARLY + HEAD + p, i * 2))

        def onehots(b):
            act.wait_ge(k.g_full, b.index() + (k.gates_before(layer, 1) - 1))
            for t in range(GB):
                at = bass.ds(b.index() * GB + t, 1)
                act.activation(k.oh1[:, 1, t, :], k.iota_b[:, :], ACT.Abs, bias=k.neg_i1[:, at])\
                   .then_inc(k.oh1_abs, 1)
            act.wait_ge(k.oh1_abs, b.half() * GB + (k.scalar_onehots(layer) + 1) * GB)
            act.activation(k.oh1[:, 1, :, :], k.oh1[:, 1, :, :], ACT.Relu, bias=1.0, scale=-1.0)\
               .then_inc(k.oh1_ready, 1)

        first = k.first[f"v{layer}"]

        def late(n, i=None):
            self.split_lead(Slab(first + n + self.AHEAD, i))
            if n % 2 and n + 2 < BATCHES:
                onehots(Slab(n + 2, i))

        onehots(Slab(1))
        for n in range(HEAD):
            late(n)
        with act.Fori(0, TURNS - 1) as i:
            for n in range(HEAD, HEAD + UNROLL):
                late(n, i * 2)
        for n in range(BATCHES - UNROLL, BATCHES):
            late(n)
        at = first + BATCHES + self.AHEAD
        self.split_lead(Slab(at))
        with act.Fori(0, VREST // SLOTS - 1) as i:
            for p in range(SLOTS):
                self.split_lead(Slab(at + 1 + p, i))
        for n in range(KEYS - SLOTS, KEYS):
            self.split_lead(Slab(first + n + self.AHEAD))


class Route:

    def __init__(self, k):
        lay = Lay(k, ROUTE)
        self.gate = [lay(SELS) for _ in range(NT)]
        self.i1 = [lay(SELS) for _ in range(NT)]
        self.i2 = [lay(SELS) for _ in range(NT)]
        self.top = lay(HP, TOPK)
        self.itop = lay(HP, TOPK).bitcast(U32)
        self.itop_f = lay(HP, TOPK)
        self.pos = lay(HEADS, TOPK).bitcast(U32)
        self.half = lay(HEADS, TOPK).bitcast(U32)
        self.half_f = lay(SELS)
        self.sums = [lay(HEADS) for _ in range(NT)]


class Vector:
    def __init__(self, k, dve):
        self.k, self.dve, self.w = k, dve, Waits(dve)
        self.own = Steps(dve, k.dve_step)

    def rest_x(self, meta=False):
        k, dve, w = self.k, self.dve, self.w
        at = META if meta else 0
        for b in range(4):
            w.next(k.xhi)
            cut = (slice(None), slice(2 * b, 2 * b + 2), slice(at, at + T))
            dve.tensor_tensor(k.x_lo[cut], k.acc[b][:, :].rearrange("p (c t) -> p c t", c=2),
                              k.x_hi[cut].bitcast(F32), ALU.subtract).then_inc(k.x_ready, 1)
        if meta:
            w.next(k.xhi)
            dve.tensor_tensor(k.x_lo[:, :, 0:META], k.misc[:, 0:DC * META].rearrange("p (c t) -> p c t", c=DC),
                              k.x_hi[:, :, 0:META].bitcast(F32), ALU.subtract).then_inc(k.x_ready, 1)

    def add_residual(self, last, alpha, ready=None):
        k, dve = self.k, self.dve
        ready = k.summed if ready is None else ready
        dve.wait_ge(k.used, last + 1)
        for t in range(NT):
            for half in range(2):
                part = k.h[:, t, half * 512:(half + 1) * 512]
                ins = dve.scalar_tensor_tensor(part, part, alpha, k.acc[t * 2 + half][:, :], ALU.mult, ALU.add)
        ins.then_inc(ready, 1)
        self.w.next(ready)

    def inverse_std(self, n):
        k, dve = self.k, self.dve
        self.w.next(k.std)
        self.own.do(dve.reciprocal(k.small[:, 12:12 + n], k.small[:, 8:8 + n]))
        self.own.join()

    def layer_norm(self, slot):
        k, dve, own = self.k, self.dve, self.own
        stats = k.small[:, 16:40].rearrange("p (t h s) -> p t h s", t=NT, h=2)
        mean_var = k.small[:, 0:4].rearrange("p (t s) -> p t s", t=NT)
        for t in range(NT):
            for half in range(2):
                own.do(dve.bn_stats(stats[:, t, half, :], k.h[:, t, half * 512:(half + 1) * 512]))
        own.join()
        for t in range(NT):
            own.do(dve.bn_aggr(mean_var[:, t, :], stats[:, t, :, :].rearrange("p h s -> p (h s)")))
        own.join()
        dve.tensor_scalar(k.small[:, 4:6], mean_var[:, :, 1], LN_EPS, None, ALU.add).then_inc(k.var, 1)
        self.inverse_std(NT)
        for t in range(NT):
            own.do(dve.tensor_scalar(k.h[:, t, :], k.h[:, t, :], mean_var[:, t, 0:1], k.small[:, 12 + t:13 + t],
                                     ALU.subtract, ALU.mult))
        own.join()
        self.w.next(k.param[slot], 32)
        gain, bias = view(k.big, G_AT[slot], D), view(k.big, G_AT[slot] + D, D)
        for half, ready in enumerate((k.h_half, k.h_ready)):
            cut = slice(half * 512, (half + 1) * 512)
            for t in range(NT):
                own.do(dve.tensor_tensor(k.h[:, t, cut], k.h[:, t, cut], gain[:, cut], ALU.mult))
            own.join()
            for t in range(NT):
                ins = dve.tensor_tensor(k.h[:, t, cut], k.h[:, t, cut], bias[:, cut], ALU.add)
            ins.then_inc(ready, 1)
        self.w.next(k.h_ready)

    def rms_norm(self, slot, meta=None):
        k, dve, own = self.k, self.dve, self.own
        n = 3 if meta is not None else 2
        self.w.next(k.sq)
        dve.tensor_scalar(k.small[:, 4:4 + n], k.small[:, 40:40 + n], 1.0 / D, RMS_EPS, ALU.mult, ALU.add)\
           .then_inc(k.var, 1)
        self.inverse_std(n)
        self.w.next(k.param[slot], 16)
        gain = view(k.big, G_AT[slot], D)
        for t in range(NT):
            ins = dve.scalar_tensor_tensor(view(k.big, NORMED + t * D, D), k.h[:, t, :], k.small[:, 12 + t:13 + t],
                                           gain, ALU.mult, ALU.mult)
        if meta is not None:
            ins = dve.scalar_tensor_tensor(view(k.big, NORMED + 2 * D, D, p=META), meta, k.small[0:META, 14:15],
                                           gain[0:META, :], ALU.mult, ALU.mult)
        ins.then_inc(k.h_ready, 1)
        self.w.next(k.h_ready)

    def coef(self, src, s):
        k, dve = self.k, self.dve
        dve.wait_ge(k.used, s.index(SLOTS - 1))
        dve.tensor_copy(k.c_hi[s.slot][:, :], src).then_inc(k.coef_h, 1)
        dve.wait_ge(k.coef_h, k.rows(s, 1))
        dve.tensor_tensor(k.c_lo[s.slot][:, :], src, k.c_hi[s.slot][:, :].bitcast(F32),
                          ALU.subtract).then_inc(k.coef[s.slot], 1)

    def top16(self, rows, top, index):
        dve, own = self.dve, self.own
        for n in range(len(rows)):
            own.do(dve.max(top(n)[:, 0:8], rows[n]))
        own.join()
        for n in range(len(rows)):
            own.do(dve.max_index(index(n)[:, 0:8], top(n)[:, 0:8], rows[n]))
        own.join()
        for n in range(len(rows)):
            own.do(dve.match_replace(rows[n], top(n)[:, 0:8], rows[n], NEG))
        own.join()
        for n in range(len(rows)):
            own.do(dve.max(top(n)[:, 8:16], rows[n]))
        own.join()
        for n in range(len(rows)):
            own.do(dve.max_index(index(n)[:, 8:16], top(n)[:, 8:16], rows[n]))
        own.join()

    def route(self, t):
        k, dve, own = self.k, self.dve, self.own
        r = Route(k)
        scores = view(k.big, SCORES, NT, HP, KEYS)
        cand = view(k.big, CAND, HEADS, TOPK * TOPK)
        self.top16([scores[:, t, n, :] for n in range(HP)], lambda n: r.top[:, n, :], lambda n: r.itop[:, n, :])
        own.do(dve.tensor_copy(r.itop_f, r.itop))
        halves = r.top.rearrange("p (h two) k -> p h two k", two=2)
        shape = [P, HEADS, TOPK, TOPK]
        own.do(dve.tensor_tensor(cand.rearrange("p h (a b) -> p h a b", a=TOPK),
                                 halves[:, :, 0, :].unsqueeze(3).to_broadcast(shape),
                                 halves[:, :, 1, :].unsqueeze(2).to_broadcast(shape), ALU.add))
        own.join()
        best = r.gate[t].rearrange("p (h k) -> p h k", h=HEADS)
        self.top16([cand[:, n, :] for n in range(HEADS)], lambda n: best[:, n, :], lambda n: r.pos[:, n, :])
        own.do(dve.tensor_copy(r.sums[t], best[:, :, 0]))
        own.join()
        dve.tensor_tensor(best, best, r.sums[t].unsqueeze(2).to_broadcast([P, HEADS, TOPK]), ALU.subtract)\
           .then_inc(k.m_ready, 1)
        pick = view(k.big, PICK, HEADS, TOPK, TOPK)
        places = r.itop_f.rearrange("p (h two) k -> p h two k", two=2)
        for half, dst in enumerate((r.i1[t], r.i2[t])):
            if half == 0:
                own.do(dve.tensor_scalar(r.half, r.pos, 4, None, ALU.logical_shift_right))
            else:
                own.do(dve.tensor_scalar(r.half, r.pos, TOPK - 1, None, ALU.bitwise_and))
            own.join()
            own.do(dve.tensor_copy(r.half_f, r.half.rearrange("p h k -> p (h k)")))
            own.join()
            own.do(dve.tensor_tensor(pick.rearrange("p h k a -> p (h k) a"),
                                     r.half_f.unsqueeze(2).to_broadcast([P, SELS, TOPK]),
                                     k.iota[:, 0:TOPK].unsqueeze(1).to_broadcast([P, SELS, TOPK]), ALU.is_equal))
            own.join()
            own.do(dve.tensor_tensor(pick, pick, places[:, :, half, :].unsqueeze(2).to_broadcast(shape), ALU.mult))
            own.join()
            own.do(dve.tensor_reduce(dst, pick.rearrange("p h k a -> p (h k) a"), AX, ALU.add))
            own.join()

    def peer(self, layer):
        k, dve, w, own = self.k, self.dve, self.w, self.own
        r = Route(k)
        w.next(k.s_evac, 8)
        for t in range(NT):
            self.route(t)
        for t in range(NT):
            w.next(k.e_ready)
            gate = r.gate[t].rearrange("p (h k) -> p h k", h=HEADS)
            own.do(dve.tensor_reduce(r.sums[t], gate, AX, ALU.add))
            own.join()
            own.do(dve.reciprocal(r.sums[t], r.sums[t]))
            own.join()
            dve.tensor_tensor(gate, gate, r.sums[t].unsqueeze(2).to_broadcast([P, HEADS, TOPK]), ALU.mult)\
               .then_inc(k.routed, 1)
        w.next(k.rt)
        w.next(k.i1_ready)
        own.do(dve.tensor_scalar(k.i1[:, :], k.neg_i1[:, :], -1.0, None, ALU.mult))
        own.do(dve.tensor_copy(k.i2[:, :], k.acc[0][:, T:2 * T]))
        rest = k.acc[0][:, 0:T]
        for n in range(PARTS):
            own.do(dve.tensor_copy(k.gate[:, n, :], rest))
            own.join()
            if n + 1 < PARTS:
                own.do(dve.tensor_tensor(k.rest, rest, k.gate[:, n, :], ALU.subtract))
                own.join()
                rest = k.rest

        experts = view(k.big, 0, KEYS, T)

        def onehots(b, late, wait=True):
            _, at, g0 = k.gate_pass(layer, late)
            if wait:
                dve.wait_ge(k.g_full, b.index() + (g0 - 1))
            slot, token = b.base % 2, b.index() * GB
            if slot == 0 or not late:
                shape = [P, GB, P]
                dve.tensor_tensor(k.oh1[:, slot, :, :], k.iota_b[:, :].unsqueeze(1).to_broadcast(shape),
                                  k.i1[:, bass.ds(token, GB)].unsqueeze(2).to_broadcast(shape), ALU.is_equal)
            shape = [P, PARTS, EARLY]
            for t in range(GB):
                sel = bass.ds(token + t, 1)
                ins = dve.scalar_tensor_tensor(k.oh2[:, slot, t, :, :],
                                               k.iota_b[:, at:at + EARLY].unsqueeze(1).to_broadcast(shape),
                                               k.i2[:, sel], k.gate[:, :, sel].to_broadcast(shape),
                                               ALU.is_equal, ALU.mult)
            ins.then_inc(k.oh_ready, 1)

        def weigh(b, late):
            banks, at, g0 = k.gate_pass(layer, late)
            dve.wait_ge(k.g_full, b.index() + (g0 + 1))
            part = experts[:, at:at + EARLY, bass.ds(b.index() * GB, GB)]
            dve.tensor_tensor(part, part, banks[b.slot][:, 0:GB * EARLY].rearrange("p (t i) -> p i t", t=GB),
                              ALU.mult).then_inc(k.g_used, 1)

        def gate_pass(step):
            for n in range(HEAD):
                step(n)
            with dve.Fori(0, TURNS - 1) as i:
                for n in range(HEAD, HEAD + UNROLL):
                    step(n, i * 2)
            for n in range(BATCHES - UNROLL, BATCHES):
                step(n)

        for n in range(2):
            onehots(Slab(n), 0, wait=k.gates_before(layer, 0) > 0)
        dve.wait_ge(k.evac, k.cols_before[k.first[f"u{layer}"] + EARLY])

        def early(n, i=None):
            weigh(Slab(n, i), 0)
            if n + 2 < BATCHES:
                onehots(Slab(n + 2, i), 0)
            elif n + 2 == BATCHES:
                onehots(Slab(0), 1)

        gate_pass(early)
        dve.wait_ge(k.g_used, k.gates_before(layer, 1))
        first = k.first[f"v{layer}"]
        for n in range(2):
            self.coef(experts[:, n, :], Slab(first + n))
        onehots(Slab(1), 1)
        dve.wait_ge(k.evac, k.cols_before[first])

        def late(n, i=None):
            weigh(Slab(n, i), 1)
            if n + 2 < BATCHES:
                s = Slab(first + n + 2, i)
                self.coef(experts[:, s.index(first), :], s)
                onehots(Slab(n + 2, i), 1)

        gate_pass(late)
        dve.wait_ge(k.g_used, k.gates_before(layer, 1) + BATCHES)
        self.coef(experts[:, BATCHES, :], Slab(first + BATCHES))
        with dve.Fori(0, VREST // SLOTS) as i:
            for p in range(SLOTS):
                s = Slab(first + BATCHES + 1 + p, i)
                if p < 2:
                    split_rest(k, dve, s)
                self.coef(experts[:, s.index(first), :], s)
        if layer < 2:
            self.add_residual(k.first[f"v{layer}"] + KEYS - 1, DN_ALPHA)
        else:
            self.add_residual(k.first[f"v{layer}"] + KEYS - 1, 1.0, k.rms_in)


def vector_program(k, dve):
    e = Vector(k, dve)
    e.own.do(dve.memset(k.small[:, :], 1.0))
    e.own.join()
    dve.wait_ge(k.const, 32)
    e.own.do(dve.tensor_copy(k.iota_b[:, :], k.iota[:, :]))
    dve.wait_ge(k.xload, 16 * NT)
    for name in k.stages:
        if name == "s":
            e.w.next(k.meta, 16)
            e.rms_norm(2, MixS(k).meta)
        e.rest_x(meta=name == "s")
        if name[:4] == "peer":
            e.peer(int(name[4]))
        else:
            MIXERS[name](k).vector(e)
            e.add_residual(k.first[f"{name}_out"] + k.count[f"{name}_out"] - 1, *((1.0, k.rms_in) if name == "s"
                                                                                  else (DN_ALPHA,)))
        if name in ("ab", "c", "peer0", "peer1"):
            e.layer_norm({"ab": 0, "c": 2}.get(name, 1))
        else:
            e.rms_norm({"s": 0}.get(name, 1))


def scalar_program(k, act):
    e = Scalar(k, act)
    tiles = [k.h[:, t, :] for t in range(NT)]
    for s in range(Scalar.AHEAD):
        e.split_lead(Slab(s))
    act.wait_ge(k.dve_step, 1)
    for name in k.stages:
        if name == "s":
            e.w.next(k.meta, 16)
            e.squares(MixS(k).meta, 2)
            act.wait_ge(k.xload, 16 * NT)
            if k.norms_before("s"):
                act.wait_ge(k.h_ready, k.norms_before("s"))
            e.rms(tiles, 3)
        e.lead_x(meta=name == "s")
        if name[:4] == "peer":
            e.peer(int(name[4]))
        else:
            MIXERS[name](k).scalar(e)
            e.leads(k.first[f"{name}_out"] + MIXERS[name].OUT_AHEAD,
                    k.count[f"{name}_out"] - MIXERS[name].OUT_AHEAD)
        if name in ("s", "peer2"):
            e.rms(tiles)
        else:
            e.std()


class MixAB:
    HALF = 32
    PAD = 16
    CONSTS = 7
    OUT_AHEAD = 3

    def __init__(self, k):
        self.k = k
        self.out = [k.col[0], k.col[2]]
        self.yT = [k.misc, k.col[1]]
        lay = Lay(k, MIX)
        self.cos, self.sin = lay(T), lay(T)
        self.count = lay(POOLG, T)
        self.pool_w = lay(POOLG, P)
        self.pool_scale = lay(POOLG)
        self.decay = lay(RH, 3 * P)
        self.gain = lay(RH * P)
        self.u = lay(POOLG, self.PAD + T)
        self.win = [lay(POOLG, self.PAD + T) for _ in range(2)]
        self.pooled = lay(POOLG, T)
        self.x = [lay(2, T) for _ in range(2)]
        self.prod = [lay(2, T) for _ in range(4)]
        self.rot = [lay(2, T) for _ in range(2)]
        self.v = lay(NT, RH * P)
        self.g = lay(NT, RH * P)
        self.probs = lay(RH, 3 * P)
        self.o = lay(NT, RH * P)
        self.stats = lay(NT, RH, 6)
        self.mean_var = lay(NT * RH, 2)
        self.var, self.std, self.inv = lay(NT * RH), lay(NT * RH), lay(NT * RH)
        self.y = lay(8, T)

    def tensor(self, e):
        k, pe, w = self.k, e.pe, e.w
        m = k.m
        first = k.first["ab_in"]
        for n in range(8):
            e.features(Slab(first + n), fresh=n == 0)
        pe.wait_ge(k.evac, k.cols_before[first + 8])
        wide = [*k.col, k.misc]
        for c in range(3):
            e.wide(Slab(first + 8 + c), c, wide)
        w.next(k.mload[0], 16 * self.CONSTS)
        w.next(m["pool_ready"])
        for g in range(POOLG):
            ins = pe.matmul(k.acc[g // 2][:, g % 2 * T:(g % 2 + 1) * T], self.pool_w[:, g, :],
                            self.pooled[:, g, :], start=True, stop=True)
        ins.then_inc(m["pool_mixed"], 1)
        for c in range(3, 5):
            e.wide(Slab(first + 8 + c), c, wide)
        w.next(m["pool_out"])
        w.next(m["rope_ready"])
        for h in range(RH):
            rows = slice(h * self.HALF, (h + 1) * self.HALF)
            for src, to, out in ((0, slice(0, T), slice(0, T)), (1, slice(P, T), slice(T, T + P))):
                for half in range(2):
                    r = self.rot[half]
                    ins = pe.matmul(k.acc[h][:, out], r[rows, 1, src * P:(src + 1) * P], r[rows, 0, to],
                                    start=half == 0, stop=half == 1)
            ins.then_inc(m["ret_scores"], 1)
        for c in range(5, DC):
            e.wide(Slab(first + 8 + c), c, wide)
        w.next(m["ab_wide"], 2)
        for h in range(RH):
            w.next(m["ret_probs"])
            cut = slice(h * P, (h + 1) * P)
            pe.matmul(self.out[0][:, cut], self.probs[:, h, 0:P], self.v[:, 0, cut], start=True, stop=True)
            pe.matmul(self.out[1][:, cut], self.probs[:, h, P:2 * P], self.v[:, 0, cut], start=True, stop=False)
            ins = pe.matmul(self.out[1][:, cut], self.probs[:, h, 2 * P:], self.v[:, 1, cut], start=False, stop=True)
        ins.then_inc(m["ret_out"], 1)
        e.row_stage("ab_out", 8, 0, self.OUT_AHEAD)
        w.next(m["ab_wide"], 2)
        w.next(m["ret_y"])
        for j in range(4):
            for t in range(NT):
                ins = pe.transpose(self.yT[j // 2][:, j % 2 * T + t * P:j % 2 * T + (t + 1) * P],
                                   self.o[:, t, j * P:(j + 1) * P], k.ident[:, :])
            if j % 2:
                ins.then_inc(m["ret_yT"], 1)
        e.row_stage("ab_out", 8, self.OUT_AHEAD)

    def scalar(self, e):
        k, act, w = self.k, e.act, e.w
        first = k.first["ab_in"]
        dst = [self.u[:, g, self.PAD:] for g in range(POOLG)]
        dst += [self.x[half][:, j, :] for half in range(2) for j in range(2)]
        for n in range(8):
            e.column(Slab(first + n), dst[n])
        e.leads(first + 8, DC)
        e.wide(first + 8 + DC - 1, [(k.col[0], self.v[:, 0, :], ACT.Copy), (k.col[2], self.v[:, 1, :], ACT.Copy),
                                    (k.col[1], self.g[:, 0, :], ACT.Silu), (k.misc, self.g[:, 1, :], ACT.Silu)],
               k.m["ab_wide"])
        e.leads(k.first["ab_out"], 1)
        e.std(self.var, self.std)
        e.leads(k.first["ab_out"] + 1, self.OUT_AHEAD - 1)
        for b in range(2):
            w.next(k.m["ret_yT"])
            act.activation(self.y[:, 4 + 2 * b:6 + 2 * b, :],
                           self.yT[b][:, :].rearrange("p (c t) -> p c t", c=2), ACT.Copy)\
               .then_inc(k.m["y_ready"], 1)

    def vector(self, e):
        k, dve, w, own = self.k, e.dve, e.w, e.own
        m = k.m
        first = k.first["ab_in"]
        w.next(k.mload[0], 16 * self.CONSTS)
        own.do(dve.memset(self.u[:, :, 0:self.PAD], 0.0))
        own.join()
        dve.wait_ge(k.evac, first + POOLG)
        end = self.PAD + T
        for j in range(POOLG):
            for g in range(j, POOLG):
                at = self.PAD - (2 ** (g + 1) - 2 ** (j + 1))
                src = self.u if j == 0 else self.win[(j - 1) % 2]
                own.do(dve.tensor_tensor(self.win[j % 2][:, g, at:end], src[:, g, at:end],
                                         src[:, g, at - 2 ** j:end - 2 ** j], ALU.add))
            own.join()
            own.do(dve.tensor_tensor(self.pooled[:, j, :], self.win[j % 2][:, j, self.PAD:], self.count[:, j, :],
                                     ALU.mult))
        own.join()
        dve.tensor_tensor(self.pooled, self.pooled, self.u[:, :, self.PAD:], ALU.subtract)\
           .then_inc(m["pool_ready"], 1)
        dve.wait_ge(k.evac, first + 8)
        for n, (half, table) in enumerate(((0, self.cos), (1, self.sin), (1, self.cos), (0, self.sin))):
            own.do(dve.tensor_tensor(self.prod[n], self.x[half], table.unsqueeze(1).to_broadcast([P, 2, T]),
                                     ALU.mult))
        own.join()
        own.do(dve.tensor_tensor(self.rot[0], self.prod[0], self.prod[1], ALU.subtract))
        dve.tensor_tensor(self.rot[1], self.prod[2], self.prod[3], ALU.add).then_inc(m["rope_ready"], 1)
        w.next(m["pool_mixed"])
        for g in range(POOLG):
            ins = dve.tensor_scalar(self.y[:, g, :], k.acc[g // 2][:, g % 2 * T:(g % 2 + 1) * T],
                                    self.pool_scale[:, g:g + 1], None, ALU.mult)
        ins.then_inc(m["pool_out"], 1)
        w.next(m["pool_out"])
        for h in range(RH):
            w.next(m["ret_scores"])
            dve.tensor_tensor(self.probs[:, h, :], k.acc[h][:, 0:3 * P], self.decay[:, h, :], ALU.mult)\
               .then_inc(m["ret_probs"], 1)
        w.next(m["ab_wide"], 4)
        own.do(dve.tensor_tensor(self.g, self.g, self.gain.unsqueeze(1).to_broadcast([P, NT, RH * P]), ALU.mult))
        out = k.first["ab_out"]
        for n in range(self.OUT_AHEAD):
            e.coef(self.y[:, n, :], Slab(out + n))
        w.next(m["ret_out"])
        for t in range(NT):
            for h in range(RH):
                own.do(dve.bn_stats(self.stats[:, t, h, :], self.out[t][:, h * P:(h + 1) * P]))
        own.join()
        for t in range(NT):
            for h in range(RH):
                own.do(dve.bn_aggr(self.mean_var[:, t * RH + h, :], self.stats[:, t, h, :]))
        own.join()
        dve.tensor_scalar(self.var, self.mean_var[:, :, 1], LN_EPS, None, ALU.add).then_inc(k.var, 1)
        w.next(k.std)
        own.do(dve.reciprocal(self.inv, self.std))
        own.join()
        for t in range(NT):
            for h in range(RH):
                n = t * RH + h
                own.do(dve.tensor_scalar(self.o[:, t, h * P:(h + 1) * P], self.out[t][:, h * P:(h + 1) * P],
                                         self.mean_var[:, n, 0:1], self.inv[:, n:n + 1], ALU.subtract, ALU.mult))
        own.join()
        dve.tensor_tensor(self.o, self.o, self.g, ALU.mult).then_inc(m["ret_y"], 1)
        for n in range(self.OUT_AHEAD, 8):
            if n >= 4 and n % 2 == 0:
                w.next(m["y_ready"])
            e.coef(self.y[:, n, :], Slab(out + n))


class MixC:
    CONSTS = 4
    OUT_AHEAD = 0

    def __init__(self, k):
        self.k = k
        self.banks = [*k.col, k.misc]
        lay = Lay(k, MIX)
        self.bound = lay(2, CH)
        self.restart = lay(T)
        self.causal = lay(P).bitcast(U32)
        self.gain = lay(D)
        self.f = lay(CH, T)
        self.q = lay(CH, T)
        self.key = lay(CH, T)
        self.log = lay(CH, T)
        self.b = lay(CH, T)
        self.v = lay(NT, D)
        self.g = lay(NT, D)
        self.probs = lay(NT, CH, P)
        self.ktok = lay(NT, CH, P)
        self.state = [lay(CH, P) for _ in range(2)]
        self.max = lay(CH)
        self.exps = lay(2, CH)
        self.low, self.span = lay(CH), lay(CH)
        self.b_last = lay(CH, T // CCH)
        self.msq, self.var, self.std, self.inv = (lay(NT * CH) for _ in range(4))
        self.yT = self.f
        self.y = self.key.rearrange("p h t -> p (h t)").rearrange("p (t c) -> p t c", t=NT)

    def block(self, banks, t, h):
        n = t * CH + h
        return banks[n // 4][:, n % 4 * P:(n % 4 + 1) * P]

    def tensor(self, e):
        k, pe, w = self.k, e.pe, e.w
        m = k.m
        first = k.first["c_in"]
        for n in range(16):
            e.features(Slab(first + n), fresh=n == 0)
        for c in range(DC):
            e.wide(Slab(first + 16 + c), c, k.acc)
        pe.wait_ge(k.evac, k.cols_before[first + 16])

        def gate_slabs(*cs):
            for c in cs:
                e.wide(Slab(first + 24 + c), c, self.banks)

        gate_slabs(0, 1)
        w.next(m["c_wide"], 4)
        w.next(m["c_qk"])
        for t in range(NT):
            for h in range(CH):
                cut = slice(t * P, (t + 1) * P)
                ins = pe.matmul(self.block(k.acc, t, h), self.f[:, h, cut], self.q[:, h, cut],
                                start=True, stop=True)
                if h % 4 == 3:
                    ins.then_inc(m["c_scores"], 1)
        gate_slabs(2, 3, 4)
        w.next(m["c_probs"], 4)
        w.next(m["c_kout"])
        for t in range(NT):
            for h in range(CH):
                ins = pe.transpose(self.block(k.acc, t, h), self.b[:, h, t * P:(t + 1) * P], k.ident[:, :])
                if h % 4 == 3:
                    ins.then_inc(m["c_koutT"], 1)
        gate_slabs(5, 6, 7)
        w.next(m["c_ktok"], 4)
        for t in range(NT):
            for h in range(CH):
                pe.matmul(self.block(k.acc, t, h), self.probs[:, t, h, :], self.v[:, t, h * P:(h + 1) * P],
                          start=h % 4 == 0, stop=False, skip_group_check=True)
        w.next(m["c_wide"], 4)
        chunks = T // CCH
        for n in range(chunks):
            t, j = divmod(n, P // CCH)
            rows = slice(j * CCH, (j + 1) * CCH)
            if n:
                w.next(m["c_state"])
                for h in range(CH):
                    ins = pe.matmul(self.block(k.acc, t, h)[rows, :], self.q[:, h, n * CCH:(n + 1) * CCH],
                                    self.state[n % 2][:, h, :], start=False, stop=n % 4 == 3, skip_group_check=True)
                if n % 4 == 3:
                    ins.then_inc(m["c_out"], 1)
            if n < chunks - 1:
                for h in range(CH):
                    ins = pe.matmul(self.banks[n % 2 * 2 + h // 4][:, h % 4 * P:(h % 4 + 1) * P],
                                    self.ktok[rows, t, h, :], self.v[rows, t, h * P:(h + 1) * P],
                                    start=True, stop=True)
                ins.then_inc(m["c_state_psum"], 1)
        w.next(m["c_y"], 2)
        for b in range(4):
            for c in range(2):
                for t in range(NT):
                    ins = pe.transpose(self.banks[b][:, c * T + t * P:c * T + (t + 1) * P],
                                       self.y[:, t, (2 * b + c) * P:(2 * b + c + 1) * P], k.ident[:, :])
            ins.then_inc(m["c_yT"], 1)
        e.row_stage("c_out", 8)

    def scalar(self, e):
        k, act, w = self.k, e.act, e.w
        m = k.m
        first = k.first["c_in"]
        w.next(m["c_lb"])
        act.activation(self.exps, self.exps, ACT.Exp).then_inc(m["c_lbe"], 1)
        for n in range(8):
            e.column(Slab(first + n), self.f[:, n, :], ACT.Sigmoid)
        halves = (slice(0, CH // 2), slice(CH // 2, CH))

        def log(half):
            if half == 0:
                w.next(m["c_f"])
            act.activation(self.log[:, halves[half], :], self.f[:, halves[half], :], ACT.Ln)\
               .then_inc(m["c_logf"], 1)

        def exp(dst, half, ready, scale=1.0):
            act.activation(dst[:, halves[half], :], self.b[:, halves[half], :], ACT.Exp, scale=scale)\
               .then_inc(m[ready], 1)

        for n in range(8):
            e.column(Slab(first + 8 + n), self.q[:, n, :])
            if n in (3, 4):
                log(n - 3)
        for n in range(DC):
            e.leads(first + 16 + n, 1)
            if n == 0:
                w.next(m["c_b"])
            if n in (0, 1):
                exp(self.f, n, "c_exps", -1.0)
            if n in (2, 3):
                exp(self.log, n - 2, "c_exps")
            if n == 5:
                w.next(m["c_diff"])
            if n in (5, 6):
                exp(self.b, n - 5, "c_expdiff")
        e.wide(first + 16 + DC - 1, [(k.acc[t * 2 + half], self.v[:, t, half * 512:(half + 1) * 512], ACT.Copy)
                                     for t in range(NT) for half in range(2)], m["c_wide"])
        e.leads(first + 24, 5)
        for b in range(4):
            w.next(m["c_koutT"])
            t, h = divmod(4 * b, CH)
            act.activation(self.ktok[:, t, h:h + 4, :], k.acc[b][:, :].rearrange("p (h d) -> p h d", h=4), ACT.Copy)\
               .then_inc(m["c_ktok"], 1)
        e.leads(first + 24 + 5, DC - 5)
        e.wide(first + 24 + DC - 1, [(self.banks[t * 2 + half], self.g[:, t, half * 512:(half + 1) * 512], ACT.Silu)
                                     for t in range(NT) for half in range(2)], m["c_wide"])
        for t in range(NT):
            w.next(m["c_out"])
            for h in range(CH):
                n = t * CH + h
                ins = act.activation(self.y[:, t, h * P:(h + 1) * P], self.block(k.acc, t, h), ACT.Square,
                                     accum_out=self.msq[:, n:n + 1])
            ins.then_inc(m["c_msq"], 1)
            cut = slice(t * CH, (t + 1) * CH)
            e.std(self.var[:, cut], self.std[:, cut])
        for b in range(4):
            w.next(m["c_yT"])
            act.activation(self.yT[:, 2 * b:2 * b + 2, :], self.banks[b][:, :].rearrange("p (c t) -> p c t", c=2),
                           ACT.Copy).then_inc(m["y_ready"], 1)

    def vector(self, e):
        k, dve, w, own = self.k, e.dve, e.w, e.own
        m = k.m
        before = k.cols_before[k.first["c_in"]]
        w.next(k.mload[1], 16 * self.CONSTS)
        own.do(dve.tensor_tensor(self.max, self.bound[:, 0, :], self.bound[:, 1, :], ALU.max))
        own.do(dve.memset(self.probs, 0.0))
        own.join()
        dve.tensor_tensor(self.exps, self.bound, self.max.unsqueeze(1).to_broadcast([P, 2, CH]), ALU.subtract)\
           .then_inc(m["c_lb"], 1)
        w.next(m["c_lbe"])
        own.do(dve.tensor_tensor(self.max, self.exps[:, 0, :], self.exps[:, 1, :], ALU.add))
        own.join()
        own.do(dve.reciprocal(self.max, self.max))
        own.join()
        own.do(dve.tensor_tensor(self.low, self.exps[:, 1, :], self.max, ALU.mult))
        own.join()
        own.do(dve.tensor_scalar(self.span, self.low, -1.0, 1.0, ALU.mult, ALU.add))
        own.join()
        dve.wait_ge(k.evac, before + 8)
        for h in range(CH):
            ins = dve.tensor_scalar(self.f[:, h, :], self.f[:, h, :], self.span[:, h:h + 1], self.low[:, h:h + 1],
                                    ALU.mult, ALU.add)
        ins.then_inc(m["c_f"], 1)
        w.next(m["c_f"])
        own.do(dve.tensor_scalar(self.key, self.f, -1.0, 1.0, ALU.mult, ALU.add))
        w.next(m["c_logf"], 2)
        for h in range(CH):
            ins = dve.tensor_tensor_scan(self.b[:, h, :], self.restart, self.log[:, h, :], 0.0, ALU.mult, ALU.add)
        ins.then_inc(m["c_b"], 1)
        w.next(m["c_b"])
        by_chunk = self.b.rearrange("p h t -> p (h t)").rearrange("p (n c) -> p n c", c=CCH)
        last = self.b_last.rearrange("p h n -> p (h n)")
        own.do(dve.tensor_copy(last, by_chunk[:, :, CCH - 1]))
        w.next(m["c_exps"], 4)
        own.join()
        dve.tensor_tensor(by_chunk, last.unsqueeze(2).to_broadcast([P, CH * T // CCH, CCH]), by_chunk, ALU.subtract)\
           .then_inc(m["c_diff"], 1)
        dve.wait_ge(k.evac, before + 16)
        own.do(dve.tensor_tensor(self.f, self.f, self.key, ALU.mult))
        dve.tensor_tensor(self.q, self.q, self.log, ALU.mult).then_inc(m["c_qk"], 1)
        w.next(m["c_expdiff"], 2)
        dve.tensor_tensor(self.b, self.b, self.key, ALU.mult).then_inc(m["c_kout"], 1)
        for b in range(4):
            w.next(m["c_scores"])
            t, h = divmod(4 * b, CH)
            dve.copy_predicated(self.probs[:, t, h:h + 4, :], self.causal.unsqueeze(1).to_broadcast([P, 4, P]),
                                k.acc[b][:, :].rearrange("p (h c) -> p h c", h=4)).then_inc(m["c_probs"], 1)
        w.next(m["c_wide"], 8)
        own.do(dve.tensor_tensor(self.g, self.g, self.gain.unsqueeze(1).to_broadcast([P, NT, D]), ALU.mult))

        def finish(t):
            cut = slice(t * CH, (t + 1) * CH)
            w.next(m["c_msq"])
            dve.tensor_scalar(self.var[:, cut], self.msq[:, cut], 1.0 / P, LN_EPS, ALU.mult, ALU.add)\
               .then_inc(k.var, 1)
            w.next(k.std)
            own.do(dve.reciprocal(self.inv[:, cut], self.std[:, cut]))
            own.join()
            for h in range(CH):
                n = t * CH + h
                cols = slice(h * P, (h + 1) * P)
                ins = dve.scalar_tensor_tensor(self.y[:, t, cols], self.block(k.acc, t, h), self.inv[:, n:n + 1],
                                               self.g[:, t, cols], ALU.mult, ALU.mult)
            ins.then_inc(m["c_y"], 1)

        decay = self.log.rearrange("p h (n c) -> p h n c", c=CCH)[:, :, :, CCH - 1]
        for n in range(T // CCH - 1):
            w.next(m["c_state_psum"])
            for h in range(CH):
                new = self.banks[n % 2 * 2 + h // 4][:, h % 4 * P:(h % 4 + 1) * P]
                if n:
                    ins = dve.scalar_tensor_tensor(self.state[(n + 1) % 2][:, h, :], self.state[n % 2][:, h, :],
                                                   decay[:, h, n:n + 1], new, ALU.mult, ALU.add)
                else:
                    ins = dve.tensor_copy(self.state[1][:, h, :], new)
            ins.then_inc(m["c_state"], 1)
            w.next(m["c_state"])
            if n == 5:
                finish(0)
        finish(1)
        first = k.first["c_out"]
        for n in range(8):
            if n % 2 == 0:
                w.next(m["y_ready"])
            e.coef(self.yT[:, n, :], Slab(first + n))


class MixS:
    XS = SW // P
    CONVS = XS + 2 * SG
    TAPS, SC_TAPS = 4, 3
    SC = 4
    UNIT = 3
    GW = SR * SP_
    LOADS = 10
    OUT_AHEAD = 3
    M = 2

    def __init__(self, k):
        self.k = k
        self.banks = [*k.col, k.misc]
        self.seg = [k.col[2], k.misc]
        lay = Lay(k, MIX)
        self.meta = lay(D, p=META)
        self.conv_w, self.conv_b = lay(self.CONVS, self.TAPS), lay(self.CONVS)
        self.sc_w = lay(self.SC, self.SC_TAPS)
        self.dt_w = lay(DC, SH)
        self.tri = lay(P)
        self.after = lay(P)
        self.dt_bias, self.a_log, self.d_skip = lay(SH), lay(SH), lay(SH)
        self.gain = lay(SW)
        self.x = lay(NT + 1, SW)
        self.xdecay = lay(2, SW)
        self.y = lay(NT, SW)
        self.z = lay(NT, SW)
        self.state = lay(SW)
        self.bc = lay(2 * SG, TM)
        self.btok = lay(2, SG * P)
        self.dt = lay(NT + 1, SH)
        self.a = lay(NT + 1, SH)
        self.sums = lay(3, NT + 1, SH)
        self.t = [lay(NT + 1, SH) for _ in range(5)]
        self.msq, self.var, self.std, self.inv = (lay(NT * SG) for _ in range(4))
        low = Lay(k, 2 * D, MIX)
        self.raw = [low(self.TAPS - 1 + TM) for _ in range(SLOTS)]
        at = low.at
        self.conv = [low(TM) for _ in range(SLOTS)]
        self.silu = [low(TM) for _ in range(SLOTS)]
        self.tmp = view(k.big, at, SW)
        self.weighted = [view(k.big, 2 * D + j * self.UNIT * P, self.UNIT, P) for j in range(2)]
        self.m = low(self.SC, self.SC_TAPS - 1 + TM)
        self.sc_x = low(self.SC, TM)
        self.sc_b = low(self.SC, TM)
        self.sc_y = low(self.SC, T)
        self.cb = low(NT, SG, P)
        self.dt_hi, self.dt_lo = (part[0][:, 0:DC * SH].rearrange("p (c h) -> p c h", c=DC)
                                  for part in (k.c_hi, k.c_lo))
        self.am = [k.oh1_room[:, j, 0:self.UNIT, :] for j in range(2)]
        self.e = [k.oh2_room[:, j, 0:self.UNIT, :] for j in range(2)]
        self.ones = k.oh1_room[:, 0, 3, :]
        self.yT = self.xdecay.rearrange("p t c -> p (t c)").rearrange("p (n t) -> p n t", t=T)

    def loads(self):
        return ((self.conv_w, "conv_w"), (self.conv_b, "conv_b"), (self.sc_w, "sc_w"),
                (self.dt_w, "dt_w"), (self.tri, "tri"), (self.after, "after"))

    def rows(self):
        return ((self.dt_bias, "dt_bias"), (self.a_log, "a_log"), (self.d_skip, "d_skip"), (self.gain, "ssd_norm"))

    def tile(self, t):
        return (slice(0, META), META) if t == self.M else (slice(META + t * P, META + (t + 1) * P), P)

    def tensor(self, e):
        k, pe, w = self.k, e.pe, e.w
        m = k.m
        first = k.first["s_in"]
        def time_steps():
            w.next(k.mload[2], 16 * self.LOADS)
            w.next(m["s_dtw"], 2)
            for t in (0, 1, self.M):
                cut, n = self.tile(t)
                for c in range(DC):
                    ins = e.split_matmuls(k.misc[0:n, t * SH:(t + 1) * SH], (k.x_hi[:, c, cut], k.x_lo[:, c, cut]),
                                          (self.dt_hi[:, c, :], self.dt_lo[:, c, :]), c == 0, c == DC - 1)
            ins.then_inc(m["s_dt"], 1)

        def x_tokens(n):
            w.next(m["s_silu"])
            if n >= 2:
                w.next(m["s_xtok"])
            for t in (0, 1, self.M):
                cut, rows = self.tile(t)
                ins = pe.transpose(k.acc[n % 2][0:rows, t * P:(t + 1) * P], self.silu[n % SLOTS][:, cut],
                                   k.ident[:, :])
            ins.then_inc(m["s_xsT"], 1)

        for n in range(self.CONVS):
            e.features(Slab(first + n), TM)
            if n == 1:
                time_steps()
            if 2 <= n < self.XS + 2:
                x_tokens(n - 2)
            if n == 5:
                w.next(m["s_a"])
                for t in (0, 1, self.M):
                    _, rows = self.tile(t)
                    at = t * SH
                    pe.matmul(k.acc[3][0:rows, at:at + SH], self.tri[0:rows, 0:rows], self.a[0:rows, t, :],
                              start=True, stop=True)
                    at += 96
                    ins = pe.matmul(k.acc[3][:, at:at + SH], self.ones[0:rows, :], self.a[0:rows, t, :],
                                    start=True, stop=True)
                ins.then_inc(m["s_cs"], 1)
        for n in range(self.CONVS, self.CONVS + 3 * self.SC):
            e.features(Slab(first + n), TM)
        wide = k.first["s_wide"]
        w.next(m["s_silu"], self.CONVS - self.XS)
        w.next(m["s_xtok"], 2)

        def gate_slabs(*cs):
            for c in cs:
                e.wide(Slab(wide + c), c, self.banks, META)

        for b, t in enumerate((0, self.M)):
            cut, rows = self.tile(t)
            for g in range(SG):
                ins = pe.transpose(k.acc[b][0:rows, g * P:(g + 1) * P], self.bc[:, g, cut], k.ident[:, :])
            ins.then_inc(m["s_btokT"], 1)
        for t in range(NT):
            cut, _ = self.tile(t)
            for g in range(SG):
                ins = pe.matmul(k.acc[2 + t][:, g * P:(g + 1) * P], self.bc[:, g, cut], self.bc[:, SG + g, cut],
                                start=True, stop=True)
            ins.then_inc(m["s_cb"], 1)
        pe.wait_ge(k.evac, k.cols_before[wide])
        gate_slabs(0, 1, 2)
        w.next(m["s_btok"], 2)
        w.next(m["s_cbm"], 2)
        for t, source in ((0, self.M), (1, 0)):
            _, rows = self.tile(source)
            b = 1 if source == self.M else 0
            w.next(m["s_xdt"])
            if t:
                w.next(m["s_yoffd"])
            for g in range(SG):
                ins = pe.matmul(k.acc[g][:, 0:self.GW], self.btok[0:rows, b, g * P:(g + 1) * P],
                                self.xdecay[0:rows, b, g * self.GW:(g + 1) * self.GW], start=True, stop=True)
            ins.then_inc(m["s_st"], 1)
            gate_slabs(3 + 2 * t)
            w.next(m["s_state"])
            cut, _ = self.tile(t)
            for g in range(SG):
                ins = pe.matmul(k.acc[g][:, 0:self.GW], self.bc[:, SG + g, cut],
                                self.state[:, g * self.GW:(g + 1) * self.GW], start=True, stop=True)
            ins.then_inc(m["s_yoff"], 1)
            gate_slabs(4 + 2 * t)
        gate_slabs(7)
        w.next(m["s_yoffd"])
        w.next(m["s_wide"], 4)

        units = SH // self.UNIT

        def decays(n):
            w.next(m["s_am"])
            if n >= 2:
                w.next(m["s_E"])
            for r in range(self.UNIT):
                ins = pe.matmul(self.seg[n % 2][:, r * P:(r + 1) * P], self.am[n % 2][:, r, :], self.tri,
                                start=True, stop=True)
            ins.then_inc(m["s_seg"], 1)

        def products(n):
            t, u = divmod(n, units)
            w.next(m["s_P"])
            if u == 0 and t:
                w.next(m["s_ysum"])
            for r in range(self.UNIT):
                h = u * self.UNIT + r
                g, at = h // SR, h % SR * SP_
                ins = pe.matmul(k.acc[g][:, at:at + SP_], self.weighted[n % 2][:, r, :],
                                self.x[:, t, h * SP_:(h + 1) * SP_], start=True, stop=True)
            ins.then_inc(m["s_ydiag"], 1)

        decays(0)
        for n in range(NT * units):
            if n % 2 == 0 and n < DC:
                e.narrow(Slab(wide + DC + n // 2), n, k.col[0:2], META)
            if n + 1 < NT * units:
                decays(n + 1)
            products(n)
        w.next(m["s_ysum"])
        e.row_stage("s_out", 16, 0, self.OUT_AHEAD)
        w.next(m["s_y"])
        w.next(m["s_E"], 2)
        w.next(m["s_wide"], 2)
        for b in range(6):
            if b >= 4:
                w.next(m["s_y_ready"])
            for c in range(2):
                for t in range(NT):
                    ins = pe.transpose(self.banks[b % 4][:, c * T + t * P:c * T + (t + 1) * P],
                                       self.y[:, t, (2 * b + c) * P:(2 * b + c + 1) * P], k.ident[:, :])
            ins.then_inc(m["s_yT"], 1)
        e.row_stage("s_out", 16, self.OUT_AHEAD)

    def scalar(self, e):
        k, act, w = self.k, e.act, e.w
        m = k.m
        first = k.first["s_in"]

        def silu(n):
            w.next(m["s_conv"])
            if n < self.XS:
                if n >= SLOTS:
                    w.next(m["s_xsT"])
                dst = self.silu[n % SLOTS]
            else:
                dst = self.bc[:, n - self.XS, :]
            act.activation(dst, self.conv[n % SLOTS], ACT.Silu, bias=self.conv_b[:, n:n + 1])\
               .then_inc(m["s_silu"], 1)

        for n in range(self.CONVS):
            if n >= SLOTS:
                act.wait_ge(m["s_conv"], n - 2)
            e.column(Slab(first + n), self.raw[n % SLOTS][:, self.TAPS - 1:], n=TM)
            if n:
                silu(n - 1)
            if n == 2:
                w.next(m["s_dtb"])
                act.activation(self.a_log, self.a_log, ACT.Exp).then_inc(m["s_exps"], 1)
                act.activation(self.t[1], self.t[0], ACT.Exp, scale=-1.0).then_inc(m["s_exps"], 1)
            if n == 3:
                w.next(m["s_w"])
                act.activation(self.t[3], self.t[2], ACT.Ln).then_inc(m["s_ln"], 1)
            if n == 7:
                w.next(m["s_diff"])
                act.activation(self.sums, self.sums, ACT.Exp).then_inc(m["s_exp2"], 1)
        silu(self.CONVS - 1)
        dst = [self.m[:, g, self.SC_TAPS - 1:] for g in range(self.SC)]
        dst += [self.sc_x[:, g, :] for g in range(self.SC)] + [self.sc_b[:, g, :] for g in range(self.SC)]
        for n in range(3 * self.SC):
            e.column(Slab(first + self.CONVS + n), dst[n], n=TM)
        for b, t in enumerate((0, self.M)):
            w.next(m["s_btokT"])
            _, rows = self.tile(t)
            act.activation(self.btok[0:rows, b, :], k.acc[b][0:rows, :], ACT.Copy).then_inc(m["s_btok"], 1)
        wide = k.first["s_wide"]
        e.leads(wide, DC)
        e.wide(wide + DC - 1, [(self.banks[t * 2 + half], self.z[:, t, half * 512:(half + 1) * 512], ACT.Silu)
                               for t in range(NT) for half in range(2)], m["s_wide"])

        def squares(t):
            w.next(m["s_gated"])
            for g in range(SG):
                cut = slice(g * self.GW, (g + 1) * self.GW)
                ins = act.activation(self.x[:, t, cut], self.y[:, t, cut], ACT.Square,
                                     accum_out=self.msq[:, t * SG + g:t * SG + g + 1])
            ins.then_inc(m["s_msq"], 1)

        units = SH // self.UNIT
        for n in range(NT * units):
            if n == DC:
                e.wide(wide + DC + DC // 2 - 1, [(k.col[t], self.z[:, t, D:], ACT.Silu) for t in range(NT)],
                       m["s_wide"])
            if n == units + 6:
                squares(0)
            w.next(m["s_seg"])
            if n >= 2:
                w.next(m["s_P"])
            act.activation(self.e[n % 2], self.seg[n % 2][:, 0:self.UNIT * P].rearrange("p (r l) -> p r l", l=P),
                           ACT.Exp).then_inc(m["s_E"], 1)
            if n % 2 == 0 and n < DC:
                e.leads(wide + DC + n // 2, 1)
        squares(1)
        e.std(self.var, self.std)
        e.leads(k.first["s_out"], self.OUT_AHEAD)
        for b in range(6):
            w.next(m["s_yT"])
            act.activation(self.yT[:, 2 * b:2 * b + 2, :], self.banks[b % 4][:, :].rearrange("p (c t) -> p c t", c=2),
                           ACT.Copy).then_inc(m["s_y_ready"], 1)

    def heads(self, x):
        return x.rearrange("p (h c) -> p h c", c=SP_)

    def per_head(self, s, rows=P):
        return s.unsqueeze(2).to_broadcast([rows, s.shape[1], SP_])

    def vector(self, e):
        k, dve, w, own = self.k, e.dve, e.w, e.own
        m = k.m
        out = k.first["s_out"]
        before = k.cols_before[k.first["s_in"]]
        w.next(k.mload[2], 16 * self.LOADS)
        dve.tensor_copy(self.dt_hi, self.dt_w).then_inc(m["s_dtw"], 1)
        w.next(m["s_dtw"])
        dve.tensor_tensor(self.dt_lo, self.dt_w, self.dt_hi.bitcast(F32), ALU.subtract).then_inc(m["s_dtw"], 1)
        own.do(dve.memset(self.ones, 1.0))
        own.do(dve.memset(self.m[:, :, 0:self.SC_TAPS - 1], 0.0))
        own.do(dve.memset(self.sums, 0.0))
        own.do(dve.memset(self.t[4], 0.0))
        for r in self.raw:
            own.do(dve.memset(r[:, 0:self.TAPS - 1], 0.0))
        own.join()

        def part(out, t):
            return out[0:self.tile(t)[1], t, :]

        def conv(n):
            dve.wait_ge(k.evac, before + n + 1)
            if n >= SLOTS:
                w.next(m["s_silu"])
            out, raw = self.conv[n % SLOTS], self.raw[n % SLOTS]
            last = self.TAPS - 1
            own.do(dve.tensor_scalar(out, raw[:, last:last + TM], self.conv_w[:, n, last:last + 1], None, ALU.mult))
            for tap in range(last - 1, -1, -1):
                own.join()
                ins = dve.scalar_tensor_tensor(out, raw[:, tap:tap + TM], self.conv_w[:, n, tap:tap + 1], out,
                                               ALU.mult, ALU.add)
                if tap:
                    own.do(ins)
            ins.then_inc(m["s_conv"], 1)

        def x_tokens(n):
            w.next(m["s_xsT"])
            cut = slice(n * P, (n + 1) * P)
            own.do(dve.tensor_copy(self.x[:, 0:NT, cut], k.acc[n % 2][:, 0:NT * P].rearrange("p (t c) -> p t c", t=NT)))
            dve.tensor_copy(self.x[0:META, self.M, cut], k.acc[n % 2][0:META, NT * P:(NT + 1) * P])\
               .then_inc(m["s_xtok"], 1)

        for n in range(self.CONVS):
            conv(n)
            if n == 1:
                w.next(m["s_dt"])
                x = self.t[4]
                for t in (0, 1, self.M):
                    rows = self.tile(t)[1]
                    own.do(dve.tensor_tensor(part(x, t), k.misc[0:rows, t * SH:(t + 1) * SH], self.dt_bias[0:rows, :], ALU.add))
                own.join()
                own.do(dve.tensor_scalar(self.t[2], x, -1.0, None, ALU.mult))
                own.join()
                dve.tensor_tensor(self.t[0], x, self.t[2], ALU.max).then_inc(m["s_dtb"], 1)
            if 2 <= n < self.XS + 2:
                x_tokens(n - 2)
            if n == 2:
                w.next(m["s_exps"], 2)
                z = self.t[1]
                own.do(dve.tensor_scalar(self.a_log, self.a_log, -1.0, None, ALU.mult))
                dve.tensor_scalar(self.t[2], z, 1.0, None, ALU.add).then_inc(m["s_w"], 1)
                w.next(m["s_w"])
                own.do(dve.tensor_scalar(self.t[0], self.t[2], 1.0, None, ALU.subtract))
                own.join()
                own.do(dve.tensor_scalar(self.dt, self.t[0], 0.0, None, ALU.is_equal))
                own.join()
                own.do(dve.tensor_tensor(self.t[0], self.t[0], self.dt, ALU.add))
                own.join()
                own.do(dve.reciprocal(self.t[0], self.t[0]))
                own.do(dve.tensor_tensor(self.dt, self.dt, z, ALU.mult))
                own.join()
                own.do(dve.tensor_tensor(self.t[0], self.t[0], z, ALU.mult))
                own.do(dve.scalar_tensor_tensor(self.dt, self.t[4], 0.0, self.dt, ALU.max, ALU.add))
            if n == 4:
                w.next(m["s_ln"])
                own.join()
                own.do(dve.tensor_tensor(self.t[0], self.t[0], self.t[3], ALU.mult))
                own.join()
                own.do(dve.tensor_tensor(self.dt, self.dt, self.t[0], ALU.add))
                own.join()
                dve.tensor_tensor(self.a, self.dt, self.a_log.unsqueeze(1).to_broadcast([P, NT + 1, SH]), ALU.mult)\
                   .then_inc(m["s_a"], 1)
            if n == 6:
                w.next(m["s_cs"])
                for t in (0, 1, self.M):
                    rows = self.tile(t)[1]
                    own.do(dve.tensor_copy(self.sums[0:rows, 0, t, :], k.acc[3][0:rows, t * SH:(t + 1) * SH]))
                    own.do(dve.tensor_copy(self.sums[:, 1, t, :], k.acc[3][:, 96 + t * SH:96 + (t + 1) * SH]))
                own.join()
                dve.tensor_tensor(self.sums[:, 2, :, :], self.sums[:, 1, :, :], self.sums[:, 0, :, :], ALU.subtract)\
                   .then_inc(m["s_diff"], 1)
        own.join()
        w.next(m["s_xtok"], self.XS)
        w.next(m["s_exp2"])
        w.next(m["s_silu"], SLOTS)
        for t in range(NT):
            own.do(dve.tensor_tensor(self.heads(self.y[:, t, :]), self.heads(self.x[:, t, :]),
                                     self.per_head(self.d_skip), ALU.mult))
        own.join()
        for t in (0, 1, self.M):
            rows = self.tile(t)[1]
            xt = self.heads(self.x[0:rows, t, :])
            own.do(dve.tensor_tensor(xt, xt, self.per_head(self.dt[0:rows, t, :], rows), ALU.mult))
        own.join()
        for b, t in ((1, self.M), (0, 0)):
            rows = self.tile(t)[1]
            dve.tensor_tensor(self.heads(self.xdecay[0:rows, b, :]), self.heads(self.x[0:rows, t, :]),
                              self.per_head(self.sums[0:rows, 2, t, :], rows), ALU.mult).then_inc(m["s_xdt"], 1)
        for t in range(NT):
            w.next(m["s_cb"])
            dve.tensor_tensor(self.cb[:, t, :, :], k.acc[2 + t][:, :].rearrange("p (g l) -> p g l", g=SG),
                              self.tri.unsqueeze(1).to_broadcast([P, SG, P]), ALU.mult).then_inc(m["s_cbm"], 1)
        dve.wait_ge(k.evac, before + self.CONVS + 3 * self.SC)
        taps = self.SC_TAPS
        for g in range(self.SC):
            own.do(dve.tensor_tensor(self.m[:, g, taps - 1:], self.m[:, g, taps - 1:], self.sc_x[:, g, :], ALU.mult))
        own.join()
        for g in range(self.SC):
            own.do(dve.tensor_scalar(self.sc_y[:, g, :], self.m[:, g, META:META + T], self.sc_w[:, g, 0:1], None,
                                     ALU.mult))
        for tap in range(1, taps):
            own.join()
            for g in range(self.SC):
                own.do(dve.scalar_tensor_tensor(self.sc_y[:, g, :], self.m[:, g, META + tap:META + tap + T],
                                                self.sc_w[:, g, tap:tap + 1], self.sc_y[:, g, :], ALU.mult, ALU.add))
        own.join()
        own.do(dve.tensor_tensor(self.sc_y, self.sc_y, self.sc_b[:, :, META:], ALU.mult))
        for t in range(NT):
            w.next(m["s_st"])
            if t:
                own.do(dve.tensor_tensor(self.heads(self.state), self.heads(self.state),
                                         self.per_head(self.sums[:, 1, 0, :]), ALU.mult))
                own.join()
            for g in range(SG):
                cut = slice(g * self.GW, (g + 1) * self.GW)
                src = k.acc[g][:, 0:self.GW]
                if t:
                    ins = dve.tensor_tensor(self.state[:, cut], self.state[:, cut], src, ALU.add)
                else:
                    ins = dve.tensor_copy(self.state[:, cut], src)
            ins.then_inc(m["s_state"], 1)
            w.next(m["s_state"])
            w.next(m["s_yoff"])
            for g in range(SG):
                cut = slice(g * self.GW, (g + 1) * self.GW)
                ins = dve.tensor_tensor(self.heads(self.tmp[:, cut]), self.heads(k.acc[g][:, 0:self.GW]),
                                        self.per_head(self.sums[:, 0, t, g * SR:(g + 1) * SR]), ALU.mult)
            ins.then_inc(m["s_yoffd"], 1)
            w.next(m["s_yoffd"])
            own.do(dve.tensor_tensor(self.y[:, t, :], self.y[:, t, :], self.tmp, ALU.add))
            own.join()
        units = SH // self.UNIT

        def decays(n):
            t, u = divmod(n, units)
            if n >= 2:
                w.next(m["s_seg"])
            for r in range(self.UNIT):
                h = u * self.UNIT + r
                ins = dve.tensor_scalar(self.am[n % 2][:, r, :], self.after, self.a[:, t, h:h + 1], None, ALU.mult)
            ins.then_inc(m["s_am"], 1)

        decays(0)
        for n in range(NT * units):
            t, u = divmod(n, units)
            if n + 1 < NT * units:
                decays(n + 1)
            w.next(m["s_E"])
            if n >= 2:
                w.next(m["s_ydiag"])
            g = u * self.UNIT // SR
            dve.tensor_tensor(self.weighted[n % 2], self.e[n % 2],
                              self.cb[:, t, g, :].unsqueeze(1).to_broadcast([P, self.UNIT, P]), ALU.mult)\
               .then_inc(m["s_P"], 1)
            if u == units - 1:
                dve.wait_ge(m["s_ydiag"], n + 1)
                for g in range(SG):
                    cut = slice(g * self.GW, (g + 1) * self.GW)
                    ins = dve.tensor_tensor(self.y[:, t, cut], self.y[:, t, cut], k.acc[g][:, 0:self.GW], ALU.add)
                ins.then_inc(m["s_ysum"], 1)
                w.next(m["s_ysum"])
            if n in (units + 4, NT * units - 1):
                t = n // (NT * units - 1)
                if t:
                    e.coef(self.sc_y[:, 0, :], Slab(out))
                if t == 0:
                    w.next(m["s_wide"], 6)
                dve.tensor_tensor(self.y[:, t, :], self.y[:, t, :], self.z[:, t, :], ALU.mult)\
                   .then_inc(m["s_gated"], 1)
        for n in range(1, self.OUT_AHEAD):
            e.coef(self.sc_y[:, n, :], Slab(out + n))
        w.next(m["s_msq"], 2)
        dve.tensor_scalar(self.var, self.msq, 1.0 / self.GW, RMS_EPS, ALU.mult, ALU.add).then_inc(k.var, 1)
        w.next(k.std)
        own.do(dve.reciprocal(self.inv, self.std))
        own.join()
        for t in range(NT):
            for g in range(SG):
                cut = slice(g * self.GW, (g + 1) * self.GW)
                n = t * SG + g
                ins = dve.scalar_tensor_tensor(self.y[:, t, cut], self.y[:, t, cut], self.inv[:, n:n + 1],
                                               self.gain[:, cut], ALU.mult, ALU.mult)
        ins.then_inc(m["s_y"], 1)
        for n in range(self.OUT_AHEAD, k.count["s_out"]):
            if n >= self.SC and n % 2 == 0:
                w.next(m["s_y_ready"])
            e.coef(self.sc_y[:, n, :] if n < self.SC else self.yT[:, n - self.SC, :], Slab(out + n))


MIXERS = {"ab": MixAB, "c": MixC, "s": MixS}


def build(nc, dram, out, stages):
    with ExitStack() as ctx:
        k = Kernel(nc, ctx, dram, out, stages)
        block = ctx.enter_context(nc.Block())

        @block.sync
        def _(sp):
            sync_program(k, sp)

        @block.gpsimd
        def _(pool):
            gpsimd_program(k, pool)

        @block.scalar
        def _(act):
            scalar_program(k, act)

        @block.tensor
        def _(pe):
            tensor_program(k, pe)

        @block.vector
        def _(dve):
            vector_program(k, dve)


def columns(w):
    n = w.shape[1] // P
    return np.ascontiguousarray(w.reshape(DC, P, n, P).transpose(2, 1, 0, 3)).reshape(n, P, D)


def arrange(inputs):
    a = {name: np.asarray(v) for name, v in inputs.items()}
    d = {"x": a["x"][0]}
    w = a["ab_w_in"][0]
    half = [np.concatenate([np.arange(at + h * 64 + lo, at + h * 64 + lo + 32) for h in range(RH)])
            for lo in (0, 32) for at in (512, 768)]
    d["ab_in"] = columns(w[:, np.concatenate([np.arange(512), *half])])
    d["ab_wide"] = w[:, 1024:2048].reshape(DC, P, D)
    d["ab_out"] = a["ab_w_out"][0].reshape(8, P, D)
    w = a["c_w_in"][0]
    d["c_in"] = columns(w[:, np.concatenate([np.arange(D, 2 * D), np.arange(D)])])
    d["c_wide"] = np.concatenate([w[:, at:at + D].reshape(DC, P, D) for at in (2 * D, 3 * D)])
    d["c_out"] = a["c_w_out"][0].reshape(8, P, D)
    for n, (wq, u, v) in enumerate(((a["peer_w_q"][0], a["peer_u"][0], a["peer_v"][0]),
                                    (a["peer_w_q"][1], a["peer_u"][1], a["peer_v"][1]),
                                    (a["w_q_2"][0], a["expert_u_2"][0], a["expert_v_2"][0]))):
        d[f"wq{n}"] = columns(wq)
        d[f"u{n}"] = np.ascontiguousarray(u.reshape(KEYS, KEYS, DC, P).transpose(1, 3, 2, 0)).reshape(KEYS, P, D)
        d[f"v{n}"] = v.reshape(KEYS, KEYS, D)
    keys = np.concatenate([a["peer_sub_keys"], a["sub_keys_2"]])
    d["keys"] = np.ascontiguousarray(keys.reshape(3, HP, KEYS, P).transpose(0, 3, 1, 2))
    d["ln_g"] = a["ln_g"].reshape(4, D)
    d["ln_b"] = a["ln_b"].reshape(4, D)
    d["g_mix"], d["g_ffn"], d["g_final"] = a["g_mix_2"], a["g_ffn_2"], a["g_final_2"][None]
    d["pool_w"] = np.ascontiguousarray(a["pool_w"][0].transpose(1, 0, 2))
    d["pool_scale"] = np.ascontiguousarray(a["pool_scale"][0].reshape(POOLG, P).T)
    d["ret_g"] = a["ret_norm_g"]
    d["ident"] = np.eye(P, dtype=np.float32)
    d["iota"] = np.tile(np.arange(P, dtype=np.float32), (P, 1))
    inv = 1.0 / (np.float32(10000.0) ** np.linspace(0.0, 1.0, 32, dtype=np.float32))
    angle = np.arange(T, dtype=np.float32)[None, :] * inv.astype(np.float32)[:, None]
    d["cos"] = np.tile(np.cos(angle), (RH, 1)).astype(np.float32)
    d["sin"] = np.tile(np.sin(angle), (RH, 1)).astype(np.float32)
    count = np.arange(1, T + 1)
    d["pool_count"] = np.tile(np.stack([1.0 / np.minimum(count, n) for n in (2, 4, 8, 16)]), (P, 1, 1))\
        .astype(np.float32)
    log_gamma = np.log1p(-np.exp2(-5.0 - np.arange(RH)))
    diff = np.arange(T)[None, :] - np.arange(P)[:, None]
    decay = np.where(diff >= 0, np.exp(log_gamma[:, None, None] * np.maximum(diff, 0)), 0.0) * 64 ** -0.5
    d["ret_decay"] = np.ascontiguousarray(np.concatenate([decay, decay[:, :, :P]], 2).transpose(1, 0, 2))\
        .astype(np.float32)
    d["hgrn_lb"] = np.ascontiguousarray(a["hgrn_lb"].reshape(2, CH, P).transpose(2, 0, 1))
    d["hgrn_g"] = a["hgrn_norm_g"]
    d["restart"] = np.tile((np.arange(T) % CCH != 0).astype(np.float32), (P, 1))
    s, c = np.arange(P)[:, None], np.arange(P)[None, :]
    d["chunk_causal"] = ((s // CCH == c // CCH) & (c >= s)).astype(np.float32)
    w = a["w_in_2"][0]
    at_z, at_x, at_dt, at_sc = 0, SW, SW + MixS.CONVS * P, SW + MixS.CONVS * P + SH
    order = [np.arange(at_x, at_dt), np.arange(at_sc + 512, at_sc + 1536), np.arange(at_sc, at_sc + 512)]
    d["s_in"] = columns(w[:, np.concatenate(order)])
    z = w[:, at_z:at_x]
    d["s_wide"] = np.concatenate([z[:, :D].reshape(DC, P, D),
                                  z[:, D:].reshape(DC // 2, 2, P, 512).transpose(0, 2, 1, 3).reshape(DC // 2, P, D)])
    d["s_out"] = np.concatenate([a["w_out_2"][0][SW:], a["w_out_2"][0][:SW]]).reshape(16, P, D)
    d["dt_w"] = np.ascontiguousarray(w[:, at_dt:at_sc].reshape(DC, P, SH).transpose(1, 0, 2))
    d["meta"] = a["meta_tokens_2"]
    d["conv_w"] = np.ascontiguousarray(a["conv_ssd_w_2"][0].reshape(4, MixS.CONVS, P).transpose(2, 1, 0))
    d["conv_b"] = np.ascontiguousarray(a["conv_ssd_b_2"][0].reshape(MixS.CONVS, P).T)
    d["sc_w"] = np.ascontiguousarray(a["conv_sc_w_2"][0].reshape(3, 4, P).transpose(2, 1, 0))
    d["dt_bias"], d["a_log"], d["d_skip"] = a["dt_bias_2"], a["a_log_2"], a["d_skip_2"]
    d["ssd_norm"] = a["ssd_norm_w_2"]
    d["tri"] = (s <= c).astype(np.float32)
    d["after"] = (s > c).astype(np.float32)
    return d


def kernel(**inputs):
    import numpy as _np
    import concourse.bacc as _bacc
    from concourse import mybir as _mybir
    from concourse.bass_utils import run_bass_kernel_spmd as _run

    nc = _bacc.Bacc("TRN2", target_bir_lowering=False, num_devices=1)
    arrays = {f"in_{name}": _np.ascontiguousarray(v) for name, v in arrange(inputs).items()}
    dram = {name[3:]: nc.dram_tensor(name, v.shape, _mybir.dt.from_np(v.dtype), kind="ExternalInput").ap()
            for name, v in arrays.items()}
    out = nc.dram_tensor("out_h", (T, D), _mybir.dt.float32, kind="ExternalOutput").ap()
    build(nc, dram, out, STAGES)
    r = _run(nc, [arrays], core_ids=[0])
    return r.results[0]["out_h"].reshape(1, T, D)
```
